# Optimizing a Trainium2 kernel written in Bass

```python
import jax, jax.numpy as jnp
from jax import lax
import numpy as np

D_MODEL = 1024
BATCH = 1
SEQ = 256
DEPTH = 1

GRID_W = 64
CTX_LEN = 256
N_FOURIER_GROUPS = 4
FOURIER_GROUP_DIM = 128
FOURIER_WIDTH = N_FOURIER_GROUPS * FOURIER_GROUP_DIM
NA_HEADS = 8
HEAD_DIM = 64
NA_WIDTH = NA_HEADS * HEAD_DIM
IN_WIDTH = FOURIER_WIDTH + 3 * NA_WIDTH
WIN_ROWS = 8
WIN_COLS = 16
N_BRANCHES = 2
D_FF = 4 * D_MODEL
ROPE_THETA = 10000.0
NORM_EPS = 1e-6
N_MOD = 6


def rms_norm(x, g):
    xf = x.astype(jnp.float32)
    y = xf * lax.rsqrt(jnp.mean(xf * xf, axis=-1, keepdims=True) + NORM_EPS)
    return (y * g.astype(jnp.float32)).astype(x.dtype)

def modulate(h, shift, scale):
    return h * (1 + scale) + shift

def ada_mod(cond, w, b):
    m = jax.nn.silu(cond) @ w + b
    return jnp.split(m, N_MOD, axis=-1)

def split_heads(a):
    return a.reshape(a.shape[0], a.shape[1], NA_HEADS, HEAD_DIM)

def split_projection(p):
    f = p[..., :FOURIER_WIDTH]
    q = p[..., FOURIER_WIDTH:FOURIER_WIDTH + NA_WIDTH]
    k = p[..., FOURIER_WIDTH + NA_WIDTH:FOURIER_WIDTH + 2 * NA_WIDTH]
    v = p[..., FOURIER_WIDTH + 2 * NA_WIDTH:]
    return f, split_heads(q), split_heads(k), split_heads(v)

def rope_1d(x, cos, sin):
    m = x.shape[-1] // 2
    x1, x2 = x[..., :m], x[..., m:]
    cos = cos[None, :, None, :]
    sin = sin[None, :, None, :]
    return jnp.concatenate([x1 * cos - x2 * sin, x1 * sin + x2 * cos], axis=-1)

def axial_rope(x):
    n_tok = x.shape[1]
    t = jnp.arange(n_tok)
    row = (t // GRID_W).astype(jnp.float32)
    col = (t % GRID_W).astype(jnp.float32)
    axis_dim = HEAD_DIM // 2
    inv_freq = ROPE_THETA ** (-jnp.arange(0, axis_dim, 2, dtype=jnp.float32) / axis_dim)
    ang_r = row[:, None] * inv_freq
    ang_c = col[:, None] * inv_freq
    xf = x.astype(jnp.float32)
    xr = rope_1d(xf[..., :axis_dim], jnp.cos(ang_r), jnp.sin(ang_r))
    xc = rope_1d(xf[..., axis_dim:], jnp.cos(ang_c), jnp.sin(ang_c))
    return jnp.concatenate([xr, xc], axis=-1).astype(x.dtype)

def fourier_mix(u):
    b, n, _ = u.shape
    ug = u.astype(jnp.float32).reshape(b, n, N_FOURIER_GROUPS, FOURIER_GROUP_DIM)
    y = jnp.fft.fft2(ug, axes=(1, 3), norm="ortho").real
    return y.reshape(b, n, FOURIER_WIDTH).astype(u.dtype)

def neighbourhood_attention(q, k, v, k_ctx, v_ctx, rpb):
    b, s, h, dh = q.shape
    rows = s // GRID_W
    kr = min(WIN_ROWS, rows)
    kc = WIN_COLS
    n_loc = kr * kc
    scale = dh ** -0.5
    qg = q.reshape(b, rows, GRID_W, h, dh)
    kg = k.reshape(b, rows, GRID_W, h, dh)
    vg = v.reshape(b, rows, GRID_W, h, dh)
    r = jnp.arange(rows)
    cc = jnp.arange(GRID_W)
    row_start = jnp.clip(r - kr // 2, 0, rows - kr)
    col_start = jnp.clip(cc - kc // 2, 0, GRID_W - kc)
    col_idx = col_start[:, None] + jnp.arange(kc)
    dc_idx = col_idx - cc[:, None] + (WIN_COLS - 1)
    dr_idx = row_start[:, None] + jnp.arange(kr) - r[:, None] + (WIN_ROWS - 1)

    def one_row(args):
        q_row, rs, dr = args
        k_rows = lax.dynamic_slice_in_dim(kg, rs, kr, axis=1)
        v_rows = lax.dynamic_slice_in_dim(vg, rs, kr, axis=1)
        k_win = k_rows[:, :, col_idx]
        v_win = v_rows[:, :, col_idx]
        bias = rpb[:, dr][:, :, dc_idx].transpose(0, 2, 1, 3)
        s_loc = (jnp.einsum('bqhd,brqchd->bhqrc', q_row, k_win).astype(jnp.float32) * scale
                 + bias[None].astype(jnp.float32))
        s_ctx = jnp.einsum('bqhd,bkhd->bhqk', q_row, k_ctx).astype(jnp.float32) * scale
        sc = jnp.concatenate([s_loc.reshape(b, h, GRID_W, n_loc), s_ctx], axis=-1)
        p = jax.nn.softmax(sc, axis=-1).astype(v.dtype)
        p_loc = p[..., :n_loc].reshape(b, h, GRID_W, kr, kc)
        p_ctx = p[..., n_loc:]
        return (jnp.einsum('bhqrc,brqchd->bqhd', p_loc, v_win)
                + jnp.einsum('bhqk,bkhd->bqhd', p_ctx, v_ctx))

    out = lax.map(one_row, (qg.transpose(1, 0, 2, 3, 4), row_start, dr_idx))
    return out.transpose(1, 0, 2, 3, 4).reshape(b, s, h * dh)

def context_attention(q, k, v):
    b, n, h, dh = q.shape
    s = jnp.einsum('bqhd,bkhd->bhqk', q, k).astype(jnp.float32) * dh ** -0.5
    p = jax.nn.softmax(s, axis=-1).astype(v.dtype)
    return jnp.einsum('bhqk,bkhd->bqhd', p, v).reshape(b, n, h * dh)

def gated_merge(h, y_four, y_attn, w_gate, w_fo, w_ao, w_o):
    gates = jax.nn.sigmoid(h @ w_gate)
    g_f, g_a = jnp.split(gates, N_BRANCHES, axis=-1)
    merged = g_f * (y_four @ w_fo) + g_a * (y_attn @ w_ao)
    return merged @ w_o

def sqrelu_mlp(h, w1, w2):
    a = jax.nn.relu(h @ w1)
    return (a * a) @ w2

def first_inputs(seed: int = 0) -> dict:
    key = jax.random.key(seed)
    ks = jax.random.split(key, 20)
    nrm = lambda k, shape, s: jax.random.normal(k, shape, jnp.float32) * s
    return {
        "x": nrm(ks[0], (BATCH, SEQ, D_MODEL), 1.0),
        "c": nrm(ks[1], (BATCH, D_MODEL), 1.0),
        "ctx": nrm(ks[2], (BATCH, CTX_LEN, D_MODEL), 1.0),
        "c_ctx": nrm(ks[3], (D_MODEL,), 1.0),
        "w_ada": nrm(ks[4], (DEPTH, D_MODEL, N_MOD * D_MODEL), D_MODEL ** -0.5),
        "b_ada": nrm(ks[5], (DEPTH, N_MOD * D_MODEL), 0.02),
        "norm1_g": 1.0 + nrm(ks[6], (DEPTH, D_MODEL), 0.02),
        "norm2_g": 1.0 + nrm(ks[7], (DEPTH, D_MODEL), 0.02),
        "w_in": nrm(ks[8], (DEPTH, D_MODEL, IN_WIDTH), D_MODEL ** -0.5),
        "q_norm_g": 1.0 + nrm(ks[9], (DEPTH, HEAD_DIM), 0.02),
        "k_norm_g": 1.0 + nrm(ks[10], (DEPTH, HEAD_DIM), 0.02),
        "rpb": nrm(ks[11], (DEPTH, NA_HEADS, 2 * WIN_ROWS - 1, 2 * WIN_COLS - 1), 0.1),
        "w_branch_gate": nrm(ks[12], (DEPTH, D_MODEL, N_BRANCHES * D_MODEL), D_MODEL ** -0.5),
        "w_fourier_out": nrm(ks[13], (DEPTH, FOURIER_WIDTH, D_MODEL), FOURIER_WIDTH ** -0.5),
        "w_attn_out": nrm(ks[14], (DEPTH, NA_WIDTH, D_MODEL), NA_WIDTH ** -0.5),
        "w_out": nrm(ks[15], (DEPTH, D_MODEL, D_MODEL), D_MODEL ** -0.5),
        "w_mlp1": nrm(ks[16], (DEPTH, D_MODEL, D_FF), D_MODEL ** -0.5),
        "w_mlp2": nrm(ks[17], (DEPTH, D_FF, D_MODEL), D_FF ** -0.5),
    }

def first_block(x, c, ctx, c_ctx, w_ada, b_ada, norm1_g, norm2_g, w_in, q_norm_g, k_norm_g,
              rpb, w_branch_gate, w_fourier_out, w_attn_out, w_out, w_mlp1, w_mlp2):
    h_ctx = ctx
    for l in range(DEPTH):
        last = l == DEPTH - 1
        sh1, sc1, g1, sh2, sc2, g2 = [m[:, None, :] for m in ada_mod(c, w_ada[l], b_ada[l])]
        csh1, csc1, cg1, csh2, csc2, cg2 = ada_mod(c_ctx, w_ada[l], b_ada[l])

        hc = modulate(rms_norm(h_ctx, norm1_g[l]), csh1, csc1)
        fc, qc, kc, vc = split_projection(hc @ w_in[l])
        kc = rms_norm(kc, k_norm_g[l])

        hx = modulate(rms_norm(x, norm1_g[l]), sh1, sc1)
        fx, qx, kx, vx = split_projection(hx @ w_in[l])
        qx = axial_rope(rms_norm(qx, q_norm_g[l]))
        kx = axial_rope(rms_norm(kx, k_norm_g[l]))
        y_four = fourier_mix(fx)
        y_attn = neighbourhood_attention(qx, kx, vx, kc, vc, rpb[l])
        mixed = gated_merge(hx, y_four, y_attn, w_branch_gate[l], w_fourier_out[l],
                            w_attn_out[l], w_out[l])
        x = x + g1 * mixed
        hx2 = modulate(rms_norm(x, norm2_g[l]), sh2, sc2)
        x = x + g2 * sqrelu_mlp(hx2, w_mlp1[l], w_mlp2[l])

        if not last:
            qc = rms_norm(qc, q_norm_g[l])
            yc_four = fourier_mix(fc)
            yc_attn = context_attention(qc, kc, vc)
            mixed_c = gated_merge(hc, yc_four, yc_attn, w_branch_gate[l], w_fourier_out[l],
                                  w_attn_out[l], w_out[l])
            h_ctx = h_ctx + cg1 * mixed_c
            hc2 = modulate(rms_norm(h_ctx, norm2_g[l]), csh2, csc2)
            h_ctx = h_ctx + cg2 * sqrelu_mlp(hc2, w_mlp1[l], w_mlp2[l])
    return x


N_MEM = 256
ATT_HEADS = 4
ATT_WIDTH = ATT_HEADS * HEAD_DIM
CONV_WIDTH = 384
CONV_KERNEL = 31
CONV_PAD = CONV_KERNEL // 2
RWKV_HEADS = 6
RWKV_WIDTH = RWKV_HEADS * HEAD_DIM
MIX_WIDTH = ATT_WIDTH + CONV_WIDTH + RWKV_WIDTH
DECAY_RANK = 64
ICLR_RANK = 64
GATE_RANK = 128
RWKV_PROJ = 3 * RWKV_WIDTH + 2 * DECAY_RANK + 2 * ICLR_RANK + GATE_RANK
IN_PROJ = ATT_WIDTH + 2 * CONV_WIDTH + RWKV_PROJ
N_EXPERTS = 16
EXPERT_FF = 1024
CAPACITY_FACTOR = 2
LN_EPS = 1e-5
GN_EPS = 64e-5
L2_EPS = 1e-12
DECAY_SCALE = 0.606531


def rms_norm_2(x, g):
    xf = x.astype(jnp.float32)
    y = xf * lax.rsqrt(jnp.mean(xf * xf, axis=-1, keepdims=True) + NORM_EPS)
    return (y * g.astype(jnp.float32)).astype(x.dtype)

def memory_cross_attention(q, mem_n, w_mk, w_mv):
    B, S, _ = q.shape
    qh = q.reshape(B, S, ATT_HEADS, HEAD_DIM)
    kh = (mem_n @ w_mk).reshape(B, -1, ATT_HEADS, HEAD_DIM)
    vh = (mem_n @ w_mv).reshape(B, -1, ATT_HEADS, HEAD_DIM)
    s = jnp.einsum('bqhd,bmhd->bhqm', qh, kh).astype(jnp.float32) * (HEAD_DIM ** -0.5)
    pr = jax.nn.softmax(s, axis=-1).astype(vh.dtype)
    o = jnp.einsum('bhqm,bmhd->bqhd', pr, vh)
    return o.reshape(B, S, ATT_WIDTH)

def conformer_conv(pc, conv_w, conv_b, ln_g, ln_b):
    val, gate = jnp.split(pc, 2, axis=-1)
    u = val * jax.nn.sigmoid(gate)
    u = lax.conv_general_dilated(
        u, conv_w[:, None, :].astype(u.dtype), window_strides=(1,),
        padding=[(CONV_PAD, CONV_PAD)], dimension_numbers=('NWC', 'WIO', 'NWC'),
        feature_group_count=CONV_WIDTH) + conv_b.astype(u.dtype)
    uf = u.astype(jnp.float32)
    mu = jnp.mean(uf, axis=-1, keepdims=True)
    var = jnp.mean(jnp.square(uf - mu), axis=-1, keepdims=True)
    uf = (uf - mu) * lax.rsqrt(var + LN_EPS) * ln_g.astype(jnp.float32) + ln_b.astype(jnp.float32)
    return jax.nn.silu(uf).astype(pc.dtype)

def token_shift_centred(p, mu):
    prev = jnp.pad(p, ((0, 0), (1, 0), (0, 0)))[:, :-1]
    nxt = jnp.pad(p, ((0, 0), (0, 1), (0, 0)))[:, 1:]
    return p + mu[0] * (prev - p) + mu[1] * (nxt - p)

def wkv7_scan(r, w, k, v, kk, a, reverse):
    def step(state, inp):
        r_t, w_t, k_t, v_t, kk_t, a_t = inp
        sa = jnp.einsum('bhij,bhj->bhi', state, -kk_t)
        state = (state * w_t[..., None, :]
                 + sa[..., :, None] * (kk_t * a_t)[..., None, :]
                 + v_t[..., :, None] * k_t[..., None, :])
        y_t = jnp.einsum('bhij,bhj->bhi', state, r_t)
        return state, y_t
    S, B, H, N = r.shape
    state0 = jnp.zeros((B, H, N, N), jnp.float32)
    _, ys = lax.scan(step, state0, (r, w, k, v, kk, a), reverse=reverse)
    return ys

def rwkv7_bidirectional(pr, shift_mu, decay_w0, decay_up, iclr_a0, iclr_up, gate_up,
                        k_k, k_a, r_k, lnx_g, lnx_b):
    f32 = jnp.float32
    B, S, _ = pr.shape
    pf = token_shift_centred(pr.astype(f32), shift_mu.astype(f32))
    c0 = 3 * RWKV_WIDTH
    cuts = [RWKV_WIDTH, 2 * RWKV_WIDTH, c0, c0 + DECAY_RANK, c0 + 2 * DECAY_RANK,
            c0 + 2 * DECAY_RANK + ICLR_RANK, c0 + 2 * DECAY_RANK + 2 * ICLR_RANK]
    r, k, v, wdf, wdb, adf, adb, gd = jnp.split(pf, cuts, axis=-1)

    def heads(t):
        return t.reshape(t.shape[:-1] + (RWKV_HEADS, HEAD_DIM))

    def tm(t):
        return jnp.moveaxis(t, 1, 0)

    g = jax.nn.sigmoid(gd) @ gate_up.astype(f32)
    kk = heads(k * k_k.astype(f32))
    kk = kk * lax.rsqrt(jnp.sum(kk * kk, axis=-1, keepdims=True) + L2_EPS)
    r_h, v_h = heads(r), heads(v)
    r_tm, v_tm, kk_tm = tm(r_h), tm(v_h), tm(kk)
    r_k32 = r_k.astype(f32)

    outs, bonuses = [], []
    for d, (wd, ad) in enumerate(((wdf, adf), (wdb, adb))):
        w = jnp.exp(-DECAY_SCALE * jax.nn.sigmoid(
            decay_w0[d].astype(f32) + jnp.tanh(wd) @ decay_up[d].astype(f32)))
        a = jax.nn.sigmoid(iclr_a0[d].astype(f32) + ad @ iclr_up[d].astype(f32))
        k_d = heads(k * (1.0 + (a - 1.0) * k_a.astype(f32)))
        ys = wkv7_scan(r_tm, tm(heads(w)), tm(k_d), v_tm, kk_tm, tm(heads(a)), reverse=(d == 1))
        outs.append(jnp.moveaxis(ys, 0, 1))
        bonuses.append(jnp.sum(r_h * k_d * r_k32, axis=-1, keepdims=True) * v_h)
    y = outs[0] + outs[1]
    mu = jnp.mean(y, axis=-1, keepdims=True)
    var = jnp.mean(jnp.square(y - mu), axis=-1, keepdims=True)
    y = ((y - mu) * lax.rsqrt(var + GN_EPS) * lnx_g.astype(f32).reshape(RWKV_HEADS, HEAD_DIM)
         + lnx_b.astype(f32).reshape(RWKV_HEADS, HEAD_DIM))
    y = (y + bonuses[0] + bonuses[1]).reshape(B, S, RWKV_WIDTH) * g
    return y.astype(pr.dtype)

def expert_choice_ffn(h, w_router, w_gate, w_up, w_down):
    B, S, D = h.shape
    cap = CAPACITY_FACTOR * S // N_EXPERTS
    aff = jax.nn.softmax((h @ w_router).astype(jnp.float32), axis=-1)
    gates, idx = lax.top_k(jnp.swapaxes(aff, 1, 2), cap)
    xe = jax.vmap(lambda hb, ib: hb[ib])(h, idx)
    hid = jax.nn.silu(jnp.einsum('becd,edf->becf', xe, w_gate)) * jnp.einsum('becd,edf->becf', xe, w_up)
    ye = jnp.einsum('becf,efd->becd', hid, w_down) * gates[..., None].astype(h.dtype)
    bidx = jnp.arange(B)[:, None, None]
    return jnp.zeros_like(h).at[bidx, idx].add(ye)

def second_inputs(seed: int = 0) -> dict:
    key = jax.random.key(seed)
    ks = iter(jax.random.split(key, 40))
    L, D = DEPTH, D_MODEL

    def nrm(shape, scale):
        return scale * jax.random.normal(next(ks), shape, jnp.float32)

    return {
        "x": nrm((BATCH, SEQ, D), 1.0),
        "mem": nrm((BATCH, N_MEM, D), 1.0),
        "norm_mix_g": 1.0 + nrm((L, D), 0.05),
        "norm_mem_g": 1.0 + nrm((L, D), 0.05),
        "w_in": nrm((L, D, IN_PROJ), D ** -0.5),
        "w_mk": nrm((L, D, ATT_WIDTH), D ** -0.5),
        "w_mv": nrm((L, D, ATT_WIDTH), D ** -0.5),
        "conv_w": nrm((L, CONV_KERNEL, CONV_WIDTH), CONV_KERNEL ** -0.5),
        "conv_b": nrm((L, CONV_WIDTH), 0.01),
        "conv_ln_g": 1.0 + nrm((L, CONV_WIDTH), 0.05),
        "conv_ln_b": nrm((L, CONV_WIDTH), 0.01),
        "shift_mu": jax.random.uniform(next(ks), (L, 2, RWKV_PROJ), jnp.float32, 0.0, 0.5),
        "decay_w0": nrm((L, 2, RWKV_WIDTH), 0.5),
        "decay_up": nrm((L, 2, DECAY_RANK, RWKV_WIDTH), 0.1),
        "iclr_a0": nrm((L, 2, RWKV_WIDTH), 0.5),
        "iclr_up": nrm((L, 2, ICLR_RANK, RWKV_WIDTH), 0.1),
        "gate_up": nrm((L, GATE_RANK, RWKV_WIDTH), GATE_RANK ** -0.5),
        "k_k": 0.85 + nrm((L, RWKV_WIDTH), 0.05),
        "k_a": 1.0 + nrm((L, RWKV_WIDTH), 0.05),
        "r_k": nrm((L, RWKV_HEADS, HEAD_DIM), 0.1),
        "lnx_g": 1.0 + nrm((L, RWKV_WIDTH), 0.05),
        "lnx_b": nrm((L, RWKV_WIDTH), 0.01),
        "w_out": nrm((L, MIX_WIDTH, D), MIX_WIDTH ** -0.5),
        "norm_ffn_g": 1.0 + nrm((L, D), 0.05),
        "w_router": nrm((L, D, N_EXPERTS), D ** -0.5),
        "w_e_gate": nrm((L, N_EXPERTS, D, EXPERT_FF), D ** -0.5),
        "w_e_up": nrm((L, N_EXPERTS, D, EXPERT_FF), D ** -0.5),
        "w_e_down": nrm((L, N_EXPERTS, EXPERT_FF, D), EXPERT_FF ** -0.5),
        "final_norm_g": 1.0 + nrm((D,), 0.05),
    }

def second_block(x, mem, norm_mix_g, norm_mem_g, w_in, w_mk, w_mv, conv_w, conv_b, conv_ln_g,
              conv_ln_b, shift_mu, decay_w0, decay_up, iclr_a0, iclr_up, gate_up, k_k, k_a,
              r_k, lnx_g, lnx_b, w_out, norm_ffn_g, w_router, w_e_gate, w_e_up, w_e_down,
              final_norm_g):
    for l in range(DEPTH):
        h = rms_norm_2(x, norm_mix_g[l])
        p = h @ w_in[l]
        q, pc, pr = jnp.split(p, [ATT_WIDTH, ATT_WIDTH + 2 * CONV_WIDTH], axis=-1)
        mem_n = rms_norm_2(mem, norm_mem_g[l])
        o_att = memory_cross_attention(q, mem_n, w_mk[l], w_mv[l])
        o_conv = conformer_conv(pc, conv_w[l], conv_b[l], conv_ln_g[l], conv_ln_b[l])
        o_rwkv = rwkv7_bidirectional(pr, shift_mu[l], decay_w0[l], decay_up[l], iclr_a0[l],
                                     iclr_up[l], gate_up[l], k_k[l], k_a[l], r_k[l],
                                     lnx_g[l], lnx_b[l])
        x = x + jnp.concatenate([o_att, o_conv, o_rwkv], axis=-1) @ w_out[l]
        x = x + expert_choice_ffn(rms_norm_2(x, norm_ffn_g[l]), w_router[l], w_e_gate[l],
                                  w_e_up[l], w_e_down[l])
    return rms_norm_2(x, final_norm_g)


def setup_inputs(seed=0):
    out = dict(first_inputs(seed))
    for name, value in second_inputs(seed + 1).items():
        if name != "x":
            out[name + "_2"] = value
    return out


def reference(
    x, c, ctx, c_ctx, w_ada, b_ada, norm1_g, norm2_g, w_in, q_norm_g, k_norm_g, rpb,
    w_branch_gate, w_fourier_out, w_attn_out, w_out, w_mlp1, w_mlp2, mem_2, norm_mix_g_2,
    norm_mem_g_2, w_in_2, w_mk_2, w_mv_2, conv_w_2, conv_b_2, conv_ln_g_2, conv_ln_b_2,
    shift_mu_2, decay_w0_2, decay_up_2, iclr_a0_2, iclr_up_2, gate_up_2, k_k_2, k_a_2, r_k_2,
    lnx_g_2, lnx_b_2, w_out_2, norm_ffn_g_2, w_router_2, w_e_gate_2, w_e_up_2, w_e_down_2,
    final_norm_g_2,
):
    x = first_block(
        x, c, ctx, c_ctx, w_ada, b_ada, norm1_g, norm2_g, w_in, q_norm_g, k_norm_g, rpb,
        w_branch_gate, w_fourier_out, w_attn_out, w_out, w_mlp1, w_mlp2,
    )
    return second_block(
        x, mem_2, norm_mix_g_2, norm_mem_g_2, w_in_2, w_mk_2, w_mv_2, conv_w_2, conv_b_2,
        conv_ln_g_2, conv_ln_b_2, shift_mu_2, decay_w0_2, decay_up_2, iclr_a0_2, iclr_up_2,
        gate_up_2, k_k_2, k_a_2, r_k_2, lnx_g_2, lnx_b_2, w_out_2, norm_ffn_g_2, w_router_2,
        w_e_gate_2, w_e_up_2, w_e_down_2, final_norm_g_2,
    )


_drawn_inputs = setup_inputs


def setup_inputs(seed=0):
    import zlib

    import numpy as np

    out = dict(_drawn_inputs(seed))
    spreads = {}
    factors = {'norm1_g': 6.484,
     'norm2_g': 3.012,
     'q_norm_g': 8.0,
     'k_norm_g': 8.0,
     'rpb': 8.0,
     'norm_mem_g_2': 8.0,
     'conv_b_2': 8.0,
     'conv_ln_g_2': 15.42,
     'conv_ln_b_2': 64.0,
     'k_k_2': 26.538,
     'k_a_2': 2.788,
     'lnx_g_2': 19.476,
     'lnx_b_2': 64.0,
     'norm_ffn_g_2': 3.643,
     'r_k_2': 4.62}
    for name, (base, spread) in spreads.items():
        noise = np.random.default_rng([zlib.crc32(name.encode()), seed]).standard_normal(out[name].shape)
        drawn = base * np.exp(spread * noise) if base else spread * noise
        out[name] = __import__('jax').numpy.asarray(drawn.astype(out[name].dtype))
    for name, factor in factors.items():
        out[name] = (out[name] * factor).astype(out[name].dtype)
    return out
```

```python
from collections import deque
from contextlib import ExitStack

import numpy as np

import concourse.bass as bass
from concourse import mybir

F32 = mybir.dt.float32
U8 = mybir.dt.uint8
ALU = mybir.AluOpType
ACT = mybir.ActivationFunctionType
AX = mybir.AxisListType

DECAY = 0.606531
SLAB = 2048

PACK = [
    ("c2", 16), ("bada", 48), ("n1", 8), ("n2", 8), ("qg", 64), ("kg", 64), ("nmix", 8), ("nmem", 8),
    ("convw", 93), ("convb", 3), ("lng", 3), ("lnb", 3), ("smu", 24), ("dw0", 6), ("ia0", 6), ("kk", 3),
    ("ka", 3), ("rk", 3), ("nffn", 8), ("fing", 8), ("lnxg", 384), ("lnxb", 384), ("wr", 128),
    ("dup", 384), ("iup", 384), ("gup", 384),
]
CONST = [
    ("ident", 128), ("ones", 128), ("blk", 128), ("dftc", 256), ("dftn", 1024), ("cos", 128), ("sin", 128),
    ("amask", 64), ("iota", 32), ("ind2", 2),
]
LEVELS = 7


def offsets(table):
    at, out = 0, {}
    for name, n in table:
        out[name] = (at, n)
        at += n
    return out, at


SLABS = [("ada", 24), ("win", 8), ("gate", 8), ("fo", 2), ("ao", 2), ("wo", 4), ("m1", 16), ("m2", 16),
         ("win2", 10), ("mk", 1), ("mv", 1), ("wo2", 4), ("eg", 64), ("eu", 64), ("ed", 64)]


def slab_order():
    order = [("ada", s) for s in range(8)]
    order += [("win", s) for s in (4, 5, 2, 3, 6, 7, 0, 1)]
    mid = [("gate", s) for s in range(8)]
    late = [("ada", s) for s in range(8, 24)]
    while mid or late:
        if mid:
            order.append(mid.pop(0))
        order += late[:2]
        late = late[2:]
    order += [("fo", 0), ("fo", 1), ("ao", 0), ("ao", 1)]
    order += [("wo", s) for s in range(4)]
    order += [("mk", 0), ("mv", 0)]
    order += [("m1", s) for s in range(16)] + [("m2", s) for s in range(16)]
    order += [("win2", s) for s in (1, 2, 3, 5, 6, 4, 7, 8, 9, 0)]
    order += [("wo2", s) for s in range(4)]
    for e in range(17):
        if e < 16:
            order += [("eg", 4 * e + s) for s in range(4)] + [("eu", 4 * e + s) for s in range(4)]
        if e:
            order += [("ed", 4 * e - 4 + s) for s in range(4)]
    return order


class Engine:

    def __init__(self, sem):
        self.queue, self.sem, self.tick, self.passed = [], sem, 0, {}

    def wait(self, producers):
        need, left = {}, [producers]
        while left:
            p = left.pop()
            if isinstance(p, tuple) and len(p) == 2 and isinstance(p[1], int):
                need[p[0]] = max(need.get(p[0], 0), p[1])
            elif p is not None:
                left.extend(p)
        for sem, value in need.items():
            if self.passed.get(sem, 0) < value:
                self.passed[sem] = value
                self.queue.append(lambda e, s=sem, v=value: e.wait_ge(s, v))

    def run(self, fn, *producers):
        self.wait(producers)
        self.tick += 1
        self.queue.append(lambda e, f=fn, s=self.sem: f(e).then_inc(s, 1))
        return (self.sem, self.tick)

    def quiet(self, fn, *producers):
        self.wait(producers)
        self.queue.append(fn)

    def load(self, out, src, sem, value, *producers):
        self.wait(producers)
        self.queue.append(lambda e: e.dma_start(out, src).then_inc(sem, 16))
        return (sem, value)


def build(nc, xT, cT, memT, pack, bias, const, masks, w, out):
    PO, PN = offsets(PACK)
    CO, CN = offsets(CONST)
    ctx = ExitStack()
    with ctx:
        def sb(name, shape, dt=F32):
            return ctx.enter_context(nc.sbuf_tensor(name, shape, dt))

        def sem(name):
            return ctx.enter_context(nc.semaphore(name))

        NRING = 6
        AR = 136 * 256
        packt = sb("packt", [128, PN])
        constt = sb("constt", [128, CN])
        maskt = sb("maskt", [128, LEVELS * 384 + 512], U8)
        small = sb("small", [128, 640])
        ring = sb("ring", [128, NRING * SLAB])
        arena = sb("arena", [128, AR])
        banks = [ctx.enter_context(nc.psum_tensor(f"bank{i}", [128, 512], F32)) for i in range(8)]

        PE, AC, DV, PL, SP = (Engine(sem(n)) for n in ("s_pe", "s_act", "s_dve", "s_pool", "s_sp"))

        def pk(name):
            a, n = PO[name]
            return packt[:, a:a + n]

        def cn(name):
            a, n = CO[name]
            return constt[:, a:a + n]

        small_at = [0]

        def tiny(n):
            a = small_at[0]
            small_at[0] += n
            assert small_at[0] <= 640
            return small[:, a:a + n]

        def region(kb, *dims):
            n = int(np.prod(dims))
            a = int(kb * 256)
            assert a + n <= AR, (kb, dims)
            v = arena[:, a:a + n]
            names = "abcd"[:len(dims)]
            if len(dims) > 1:
                v = v.rearrange(f"p ({' '.join(names)}) -> p {' '.join(names)}",
                                **{names[i]: dims[i] for i in range(len(dims))})
            return v

        ident = cn("ident")
        ones = cn("ones")

        pool = deque((i, []) for i in range(8))

        def bank():
            i, readers = pool.popleft()
            return i, banks[i], readers

        def free(i, *readers):
            pool.append((i, list(readers)))

        slots = deque()
        for i in range(NRING):
            slots.append((ring[:, i * SLAB:(i + 1) * SLAB], sem(f"s_w{i}"), 0, []))
        pending = deque(slab_order())
        landed = {}

        def refill():
            while slots and pending:
                place, s, used, readers = slots.popleft()
                name, n = pending.popleft()
                t = SP.load(place, w[name][n], s, 16 * (used + 1), readers)
                landed[(name, n)] = (place, t, s, used + 1)

        def add_slot(view, *readers):
            slots.append((view, sem(f"s_x{len(landed)}_{len(slots)}"), 0, list(readers)))

        def slab(name, n, k):
            refill()
            place, t, s, used = landed[(name, n)]
            return place.rearrange("p (k n) -> p k n", k=k), t

        def done(name, n, reader):
            place, t, s, used = landed.pop((name, n))
            slots.append((place, s, used, [reader]))
            refill()

        def mm(dst, pairs, *producers):
            PE.wait(producers)
            last = len(pairs) - 1
            for j, (l, r) in enumerate(pairs):
                f = lambda e, l=l, r=r, j=j: e.matmul(dst, l, r, start=(j == 0), stop=(j == last))
                if j < last:
                    PE.quiet(f)
                else:
                    t = PE.run(f)
            return t

        def turn(dst, src, *producers):
            return PE.run(lambda e: e.transpose(dst, src, ident), *producers)

        def act(dst, src, func, *producers, bias=0.0, scale=1.0, accum=None):
            if accum is None:
                return AC.run(lambda e: e.activation(dst, src, func, bias=bias, scale=scale), *producers)
            return AC.run(lambda e: e.activation(dst, src, func, bias=bias, scale=scale, accum_out=accum),
                          *producers)

        def copy(eng, dst, src, *producers):
            if eng is AC:
                return act(dst, src, ACT.Copy, *producers)
            return eng.run(lambda e: e.tensor_copy(dst, src), *producers)

        def tt(eng, dst, a, b, op, *producers):
            return eng.run(lambda e: e.tensor_tensor(dst, a, b, op), *producers)

        def ts(eng, dst, a, s1, s2, op0, op1, *producers):
            if op1 is None:
                return eng.run(lambda e: e.tensor_scalar(dst, a, s1, None, op0), *producers)
            return eng.run(lambda e: e.tensor_scalar(dst, a, s1, s2, op0, op1), *producers)

        def stt(dst, a, s, b, op0, op1, *producers):
            return DV.run(lambda e: e.scalar_tensor_tensor(dst, a, s, b, op0, op1), *producers)

        def rsq(dst, src, scale, eps, *producers):
            a = ts(DV, dst, src, scale, eps, ALU.mult, ALU.add, *producers)
            b = act(dst, dst, ACT.Sqrt, a)
            c = DV.run(lambda e: e.reciprocal(dst, dst), b)
            return a, c

        MUL, ADD, SUB = ALU.mult, ALU.add, ALU.subtract

        X = region(0, 8, 256)
        C = region(8, 8, 256)
        HX = region(16, 8, 512)
        TH = region(32, 16, 256)
        BI = region(48, 64, 64)
        V = region(64, 4, 512)
        QT = region(72, 4, 256)
        KT = region(76, 4, 512)
        QN = region(84, 4, 512)
        FT = region(92, 4, 256)
        O = region(92, 2, 512)
        YF = region(96, 4, 256)
        YA = region(100, 4, 256)
        P = region(104, 3, 512)
        PT = region(110, 3, 512)
        UC = region(104, 2, 4, 256)
        CQ = region(116, 2, 64)
        SQ = region(116.5, 2, 64)
        CK = region(117, 2, 64)
        SK = region(117.5, 2, 64)
        RS = region(118, 512)
        SQR = region(32, 8, 512)

        t_pack = AC.load(packt[:, :], pack, sem("s_pack"), 16)
        t_x = AC.load(X, xT, sem("s_x"), 16)
        t_c = AC.load(C, cT, sem("s_c"), 16)
        t_const = AC.load(constt[:, :], const, sem("s_const"), 16)
        MF = region(120, LEVELS * 384 + 512)
        t_mask = AC.load(MF, masks, sem("s_mask"), 16)
        refill()

        c2 = tiny(16)
        a = act(c2, pk("c2"), ACT.Tanh, t_pack, scale=0.5)
        a = ts(DV, c2, c2, 0.5, 0.5, MUL, ADD, a)
        t_c2 = tt(DV, c2, c2, pk("c2"), MUL, a)
        c2v = c2.rearrange("p (k b) -> p k b", k=8)

        mod = tiny(96).rearrange("p (m b) -> p m b", m=48)

        def ada(s, b, readers):
            wv, t = slab("ada", s, 8)
            for j in range(2):
                m = 2 * s + j
                last = mm(b[:, 2 * m:2 * m + 2], [(wv[:, k, j * 128:(j + 1) * 128], c2v[:, k, :]) for k in range(8)],
                          t, t_c2, readers)
            done("ada", s, last)
            return last

        sa = act(SQR[:, :, 0:256], X, ACT.Square, t_x)
        sc = act(SQR[:, :, 256:512], C, ACT.Square, t_c)
        bi, b, rd = bank()
        t = mm(b[:, :], [(ones, SQR[:, k, :]) for k in range(8)], sa, sc, t_const, rd)
        fr, t_rs = rsq(RS, b[:, :], 1.0 / 1024, 1e-6, t)
        free(bi, fr)
        t_bias = AC.load(region(48, 4096), bias, sem("s_bias"), 16)
        xn0 = tt(DV, HX[:, :, 0:256], X, RS[:, 0:256].unsqueeze(1).to_broadcast([128, 8, 256]), MUL, t_rs, t_x)
        xn1 = tt(PL, HX[:, :, 256:512], C, RS[:, 256:512].unsqueeze(1).to_broadcast([128, 8, 256]), MUL, t_rs, t_c)

        ai, ab, ard = bank()
        for s in range(8):
            last = ada(s, ab, ard)
        bada = pk("bada")
        t_mod0 = t = tt(DV, mod[:, 0:16, :], ab[:, 0:32].rearrange("p (m b) -> p m b", b=2),
               bada[:, 0:16].unsqueeze(2).to_broadcast([128, 16, 2]), ADD, last)
        free(ai, t_mod0)
        gs1 = tiny(16).rearrange("p (m b) -> p m b", m=8)
        t = stt(gs1, mod[:, 8:16, :], 1.0, pk("n1").unsqueeze(2).to_broadcast([128, 8, 2]), ADD, MUL, t)
        t_h = [None] * 8
        for k in range(8):
            u = ts(DV, HX[:, k, 0:256], HX[:, k, 0:256], gs1[:, k, 0:1], mod[:, k, 0:1], MUL, ADD, t, xn0)
            v = act(HX[:, k, 256:512], HX[:, k, 256:512], ACT.Identity, t, xn1,
                    scale=gs1[:, k, 1:2], bias=mod[:, k, 1:2])
            t_h[k] = [u, v]

        qg, kg = pk("qg"), pk("kg")

        def tables(g, dc, ds, scale):
            gg = tiny(64)
            a = ts(PL, gg, g, scale, 0.0, MUL, ADD, t_pack)
            o = []
            for i in range(2):
                cs = cn("cos").rearrange("p (i d) -> p i d", i=2)[:, i, :]
                sn = cn("sin").rearrange("p (i d) -> p i d", i=2)[:, i, :]
                o.append(tt(PL, dc[:, i, :], cs, gg, MUL, a, t_const))
                for x in range(2):
                    for half in range(2):
                        d, f = 32 * x + 16 * half, 32 * x + 16 * (1 - half)
                        o.append(tt(PL, ds[:, i, d:d + 16], sn[:, d:d + 16], gg[:, f:f + 16], MUL, a, t_const))
            return o

        t_tq = tables(qg, CQ, SQ, 0.125)
        t_tk = tables(kg, CK, SK, 1.0)
        t_mask = PL.run(lambda e: e.tensor_copy(maskt[:, :], MF), t_mask)
        t_bm = tt(PL, BI, BI, cn("amask").unsqueeze(1).to_broadcast([128, 64, 64]), ADD, t_bias, t_const)

        QNR = region(32, 6, 512)
        m_free = [None] * 4

        def rows(names, tiles):
            got = [bank() for _ in tiles]
            for h, n in enumerate(names):
                wv, t = slab("win", n, 8)
                for ti, tl in enumerate(tiles):
                    i, b, rd = got[ti]
                    last = mm(b[:, h * 256:(h + 1) * 256],
                              [(HX[:, k, tl * 128:(tl + 1) * 128], wv[:, k, :]) for k in range(8)],
                              t, t_h, rd)
                    got[ti] = (i, b, last)
                done("win", n, last)
            return got

        rstd = tiny(8 * 6).rearrange("p (i h) -> p i h", i=6)
        t_turned = {}
        normed = []

        def norm_rope(kind, tl, i, b, t):
            z = len(normed)
            n = QNR[:, z, :]
            m = QN[:, z % 4, :]
            bv = b[:, :].rearrange("p (h d) -> p h d", h=8)
            nv = n.rearrange("p (h d) -> p h d", h=8)
            mv = m.rearrange("p (h d) -> p h d", h=8)
            r = rstd[:, z, :]
            a = act(n, b[:, :], ACT.Square, t)
            a = DV.run(lambda e: e.tensor_reduce(r, nv, AX.X, ADD), a)
            _, a = rsq(r, r, 1.0 / 64, 1e-6, a)
            a = tt(DV, nv, bv, r.unsqueeze(2).to_broadcast([128, 8, 64]), MUL, a)
            free(i, a)
            if kind == "c":
                a = tt(PL, nv, nv, kg.unsqueeze(1).to_broadcast([128, 8, 64]), MUL, a)
            else:
                cs, sn, tabs = (CQ, SQ, t_tq) if kind == "q" else (CK, SK, t_tk)
                o = []
                for x in range(2):
                    for half in range(2):
                        d, f = 32 * x + 16 * half, 32 * x + 16 * (1 - half)
                        o.append(tt(DV, mv[:, :, d:d + 16], nv[:, :, f:f + 16],
                                    sn[:, tl, d:d + 16].unsqueeze(1).to_broadcast([128, 8, 16]), MUL, a, tabs,
                                    m_free[z % 4]))
                c = tt(PL, nv, nv, cs[:, tl, :].unsqueeze(1).to_broadcast([128, 8, 64]), MUL, o, a, tabs)
                a = tt(PL, n, n, m, ADD, c, o)
                m_free[z % 4] = a
            normed.append((kind, tl, n, a))

        def turn_rows(kind, tl, n, a):
            j, p, rd = bank()
            for c in range(4):
                t = turn(p[:, c * 128:(c + 1) * 128], n[:, c * 128:(c + 1) * 128], a, rd)
            at = tl + (2 if kind == "c" else 0)
            dst = (QT if kind == "q" else KT)[:, :, at * 128:(at + 1) * 128]
            e = copy(AC, dst, p[:, :].rearrange("p (c t) -> p c t", c=4), t)
            free(j, e)
            t_turned[(kind, tl)] = e

        got = rows((4, 5), (0, 1, 2, 3))
        gq = rows((2, 3), (0, 1))
        for tl in range(4):
            norm_rope("k" if tl < 2 else "c", tl % 2, *got[tl])
        for tl in range(2):
            norm_rope("q", tl, *gq[tl])
        got = rows((6, 7), (0, 1, 2, 3))
        t_v = []
        for tl in range(4):
            i, b, t = got[tl]
            e = copy(AC, V[:, tl, :], b[:, :], t)
            free(i, e)
            t_v.append(e)

        t_f = []
        for n in range(2):
            wv, t = slab("win", n, 8)
            i, b, rd = bank()
            for j in range(2):
                last = mm(b[:, j * 256:(j + 1) * 256],
                          [(wv[:, k, j * 128:(j + 1) * 128], HX[:, k, 0:256]) for k in range(8)], t, t_h, rd)
            done("win", n, last)
            e = copy(AC, FT[:, 2 * n:2 * n + 2, :], b[:, :].rearrange("p (j t) -> p j t", j=2), last)
            free(i, e)
            t_f.append(e)
        for z in normed:
            turn_rows(*z)

        dc = cn("dftc")
        dn = cn("dftn").rearrange("p (s m t) -> p s m t", s=2, m=2)
        t_u = []
        for m in range(2):
            for g2 in range(2):
                i, b, rd = bank()
                for j in range(2):
                    t = mm(b[:, j * 256:(j + 1) * 256], [(FT[:, 2 * g2 + j, m * 128:(m + 1) * 128], dc)],
                           t_f[g2], t_const, rd)
                e = copy(DV, UC[:, m, 2 * g2:2 * g2 + 2, :], b[:, :].rearrange("p (j t) -> p j t", j=2), t)
                free(i, e)
                t_u.append(e)
        t_yf = []
        for g2 in range(2):
            i, b, rd = bank()
            for j in range(2):
                g = 2 * g2 + j
                t = mm(b[:, j * 256:(j + 1) * 256],
                       [(UC[:, m, g, s * 128:(s + 1) * 128], dn[:, s, m, :]) for m in range(2) for s in range(2)],
                       t_u, rd)
            e = copy(DV, YF[:, 2 * g2:2 * g2 + 2, :], b[:, :].rearrange("p (j t) -> p j t", j=2), t)
            free(i, e)
            t_yf.append(e)
        t_uc_read = t

        t_th = [None] * 8
        ada_last = [None]

        def gate_step(s):
            wv, t = slab("gate", s, 8)
            i, b, rd = bank()
            for j in range(2):
                last = mm(b[:, j * 256:(j + 1) * 256],
                          [(wv[:, k, j * 128:(j + 1) * 128], HX[:, k, 0:256]) for k in range(8)], t, t_h, rd)
            done("gate", s, last)
            e = act(TH[:, 2 * s:2 * s + 2, :], b[:, :].rearrange("p (j t) -> p j t", j=2), ACT.Tanh, last, scale=0.5)
            free(i, e)
            t_th[s] = ts(PL, TH[:, 2 * s:2 * s + 2, :], TH[:, 2 * s:2 * s + 2, :], 0.5, 0.5, MUL, ADD, e)
            ada_last[0] = last

        def ada_step(s):
            ada_last[0] = ada(s, ab, ard)

        ai, ab, ard = bank()
        filler = deque()
        ns = 8
        for s in range(8):
            filler.append(lambda s=s: gate_step(s))
            for _ in range(2):
                filler.append(lambda s=ns: ada_step(s))
                ns += 1

        stat = tiny(3 * 16 * 2).rearrange("p (a u) -> p a u", a=3)
        units = [(h, qt) for h in range(8) for qt in range(2)]
        t_o = [[], []]
        o_last = {}
        BIv = region(48, 16, 256)
        p_free = [t_uc_read] * 3
        pt_free = [t_uc_read] * 3
        held = {}

        def att_scores(u):
            h, qt = units[u]
            c, r0 = h // 2, 64 * (h % 2)
            i, b, rd = bank()
            q = QT[r0:r0 + 64, c, qt * 128:(qt + 1) * 128]
            t = mm(b[:, :], [(q, KT[r0:r0 + 64, c, :])], list(t_turned.values()), rd)
            t = tt(DV, b[:, 0:256], b[:, 0:256], BIv[:, 2 * h + qt, :], ADD, t, t_bm)
            t = DV.run(lambda e: e.tensor_reduce(stat[:, 0, u:u + 1], b[:, :], AX.X, ALU.max, negate=True), t)
            t = act(P[:, u % 3, :], b[:, :], ACT.Exp, t, p_free[u % 3], bias=stat[:, 0, u:u + 1],
                    accum=stat[:, 1, u:u + 1])
            free(i, t)
            t2 = DV.run(lambda e: e.reciprocal(stat[:, 2, u:u + 1], stat[:, 1, u:u + 1]), t)
            held[u] = (t, t2)

        def att_turn(u):
            t, t2 = held[u]
            i, b, rd = bank()
            for j in range(4):
                x = turn(b[:, j * 128:(j + 1) * 128], P[:, u % 3, j * 128:(j + 1) * 128], t, rd)
            p_free[u % 3] = x
            e = copy(AC if u % 2 else DV, PT[:, u % 3, :], b[:, :], x, pt_free[u % 3])
            free(i, e)
            held[u] = (e, t2)

        def att_out(u):
            h, qt = units[u]
            e, t2 = held.pop(u)
            i, b, rd = bank()
            x = mm(b[:, 0:64],
                   [(PT[:, u % 3, j * 128:(j + 1) * 128], V[:, j, h * 64:(h + 1) * 64]) for j in range(4)],
                   e, t_v, rd)
            pt_free[u % 3] = x
            t_o[qt].append(ts(DV, O[:, qt, h * 64:(h + 1) * 64], b[:, 0:64],
                              stat[:, 2, u:u + 1], None, MUL, None, x, t2, t_u))
            free(i, t_o[qt][-1])

        for u in range(18):
            if u < 16:
                att_scores(u)
            for _ in range(2 if u % 2 else 1):
                if filler:
                    filler.popleft()()
            if 0 <= u - 1 < 16:
                att_turn(u - 1)
            if 0 <= u - 2 < 16:
                att_out(u - 2)
        while filler:
            filler.popleft()()
        t_mod = tt(DV, mod[:, 16:48, :], ab[:, 32:96].rearrange("p (m b) -> p m b", b=2),
                   bada[:, 16:48].unsqueeze(2).to_broadcast([128, 32, 2]), ADD, ada_last[0])
        free(ai, t_mod)
        gs2 = tiny(8)
        t_mod = [t_mod, stt(gs2, mod[:, 32:40, 0], 1.0, pk("n2"), ADD, MUL, t_mod)]
        t_ya = []
        for qt in range(2):
            i, b, rd = bank()
            for c in range(4):
                t = turn(b[:, c * 128:(c + 1) * 128], O[:, qt, c * 128:(c + 1) * 128], t_o[qt], rd)
            e = copy(AC, YA[:, :, qt * 128:(qt + 1) * 128], b[:, :].rearrange("p (c t) -> p c t", c=4), t)
            free(i, e)
            t_ya.append(e)

        MG = C
        M2 = region(84, 4, 512)
        t_mg = [None] * 4
        part = {}
        for name, Y, ty, g0 in (("fo", YF, t_yf, 0), ("ao", YA, t_ya, 8)):
            for s in range(2):
                wv, t = slab(name, s, 4)
                for c2_ in range(2):
                    n = 2 * s + c2_
                    i, b, rd = bank()
                    for j in range(2):
                        col = (2 * c2_ + j) * 128
                        last = mm(b[:, j * 256:(j + 1) * 256], [(wv[:, k, col:col + 128], Y[:, k, :]) for k in range(4)],
                                  t, ty, rd)
                    bv = b[:, :].rearrange("p (j t) -> p j t", j=2)
                    if name == "fo":
                        part[n] = tt(DV, MG[:, 2 * n:2 * n + 2, :], bv, TH[:, 2 * n:2 * n + 2, :], MUL,
                                     last, t_th[n], xn1)
                        free(i, part[n])
                    else:
                        m = M2[:, n, :].rearrange("p (j t) -> p j t", j=2)
                        e = tt(DV, m, bv, TH[:, 8 + 2 * n:10 + 2 * n, :], MUL, last, t_th[4 + n], m_free)
                        free(i, e)
                        t_mg[n] = tt(PL, MG[:, 2 * n:2 * n + 2, :], MG[:, 2 * n:2 * n + 2, :], m, ADD, e, part[n])
                done(name, s, last)

        MEM = region(24, 8, 256)
        t_mem = SP.load(MEM, memT, sem("s_mem"), 16, last)
        t_x1 = [None] * 8
        for s in range(4):
            wv, t = slab("wo", s, 8)
            i, b, rd = bank()
            for j in range(2):
                last = mm(b[:, j * 256:(j + 1) * 256],
                          [(wv[:, k, j * 128:(j + 1) * 128], MG[:, k, :]) for k in range(8)], t, t_mg, rd)
            done("wo", s, last)
            o = []
            for j in range(2):
                c = 2 * s + j
                t_x1[c] = stt(X[:, c, :], b[:, j * 256:(j + 1) * 256], mod[:, 16 + c, 0:1], X[:, c, :], MUL, ADD,
                              last, t_mod)
                o.append(t_x1[c])
            free(i, *o)

        def norm(src, producers, sq, rs, *sq_free):
            t = [act(sq[:, k, :], src[:, k, :], ACT.Square, producers[k], *sq_free) for k in range(8)]
            i, b, rd = bank()
            t = mm(b[:, 0:256], [(ones, sq[:, k, :]) for k in range(8)], t, rd)
            fr, t = rsq(rs, b[:, 0:256], 1.0 / 1024, 1e-6, t)
            free(i, fr)
            return t

        SQ2 = region(8, 8, 256)
        RS2 = region(118, 256)
        RS3 = region(119, 256)
        H = region(16, 8, 256)
        t_rm = norm(MEM, [t_mem] * 8, SQ2, RS3, last)
        t_m = []
        for k in range(8):
            t_m.append(stt(MEM[:, k, :], MEM[:, k, :], pk("nmem")[:, k:k + 1], RS3, MUL, MUL, t_rm))
        t_r2 = norm(X, t_x1, SQ2, RS2, t_rm)
        KH = region(64, 2, 256)
        VH = region(66, 2, 256)
        wv, t = slab("mk", 0, 8)
        i, b, rd = bank()
        for j in range(2):
            last = mm(b[:, j * 256:(j + 1) * 256], [(wv[:, k, j * 128:(j + 1) * 128], MEM[:, k, :]) for k in range(8)],
                      t, t_m, rd)
        done("mk", 0, last)
        t_kh = copy(AC, KH, b[:, :].rearrange("p (j t) -> p j t", j=2), last)
        free(i, t_kh)
        wv, t = slab("mv", 0, 8)
        i, b, rd = bank()
        for j in range(2):
            last = mm(b[:, j * 256:(j + 1) * 256], [(MEM[:, k, j * 128:(j + 1) * 128], wv[:, k, :]) for k in range(8)],
                      t, t_m, rd)
        done("mv", 0, last)
        t_vh = copy(AC, VH, b[:, :].rearrange("p (j t) -> p j t", j=2), last)
        free(i, t_vh)

        t_h2 = []
        for k in range(8):
            a = tt(DV, H[:, k, :], X[:, k, :], RS2, MUL, t_r2, t_x1[k])
            t_h2.append(ts(DV, H[:, k, :], H[:, k, :], gs2[:, k:k + 1], mod[:, 24 + k, 0:1], MUL, ADD, a, t_mod))

        A = region(32, 32, 256)
        t_a = [None] * 16
        for s in range(16):
            wv, t = slab("m1", s, 8)
            i, b, rd = bank()
            for j in range(2):
                last = mm(b[:, j * 256:(j + 1) * 256],
                          [(wv[:, k, j * 128:(j + 1) * 128], H[:, k, :]) for k in range(8)], t, t_h2, rd)
            done("m1", s, last)
            av = A[:, 2 * s:2 * s + 2, :]
            bv = b[:, :].rearrange("p (j t) -> p j t", j=2)
            e = act(av, bv, ACT.Relu, last)
            t_a[s] = tt(DV, av, av, bv, MUL, e)
            free(i, t_a[s])
        for s in range(16):
            wv, t = slab("m2", s, 16)
            if s % 2 == 0:
                i, b, rd = bank()
            c = s // 2
            PE.wait([t, rd] + t_a)
            for k in range(16):
                f = lambda e, k=k, b=b, wv=wv, s=s: e.matmul(b[:, 0:256], wv[:, k, :], A[:, 16 * (s % 2) + k, :],
                                                             start=(s % 2 == 0 and k == 0), stop=(s % 2 == 1 and k == 15))
                if k < 15:
                    PE.quiet(f)
                else:
                    last = PE.run(f)
            done("m2", s, last)
            if s % 2:
                t_x1[c] = stt(X[:, c, :], b[:, 0:256], mod[:, 40 + c, 0:1], X[:, c, :], MUL, ADD, last, t_mod)
                free(i, t_x1[c])
        t_x2 = t_x1
        t_mlp = last

        t_r = norm(X, t_x2, SQ2, RS2)
        t_h = [stt(H[:, k, :], X[:, k, :], pk("nmix")[:, k:k + 1], RS2, MUL, MUL, t_r) for k in range(8)]

        MIX = region(8, 8, 256)
        PF = region(24, 12, 256)
        VAL = region(68, 3, 256)
        GA = region(71, 3, 256)
        U = region(74, 3, 288)
        CA = region(77.5, 3, 256)
        CSQ = region(80.5, 3, 256)
        RAW = region(83.5, 4, 258)
        QH = region(88, 2, 256)
        P2 = region(90, 2, 512)
        PT2 = region(94, 2, 512)
        CM = region(98, 256)
        CR = region(99, 256)

        zz = [PL.run(lambda e: e.memset(U[:, :, 0:15], 0.0), t_mlp),
              PL.run(lambda e: e.memset(U[:, :, 271:288], 0.0), t_mlp),
              PL.run(lambda e: e.memset(RAW[:, :, 0:1], 0.0), t_mlp),
              PL.run(lambda e: e.memset(RAW[:, :, 257:258], 0.0), t_mlp)]
        smu = pk("smu").rearrange("p (a c) -> p a c", a=2)
        c0 = tiny(12)
        a = tt(PL, c0, smu[:, 0, :], smu[:, 1, :], ADD, t_pack)
        t_c0 = ts(PL, c0, c0, -1.0, 1.0, MUL, ADD, a)
        raw_free = [None] * 4
        t_pf = [None] * 12
        t_val = [None] * 3
        t_ga = [None] * 3
        t_q2 = [None] * 2

        def in_step(s):
            wv, t = slab("win2", s, 8)
            i, b, rd = bank()
            o = []
            for j in range(2):
                last = mm(b[:, j * 256:(j + 1) * 256],
                          [(wv[:, k, j * 128:(j + 1) * 128], H[:, k, :]) for k in range(8)], t, t_h, rd)
            done("win2", s, last)
            for j in range(2):
                c = 2 * s + j
                bv = b[:, j * 256:(j + 1) * 256]
                if c < 2:
                    t_q2[c] = copy(AC, QH[:, c, :], bv, last)
                    o.append(t_q2[c])
                elif c < 5:
                    t_val[c - 2] = copy(AC, VAL[:, c - 2, :], bv, last, t_mlp)
                    o.append(t_val[c - 2])
                elif c < 8:
                    t_ga[c - 5] = act(GA[:, c - 5, :], bv, ACT.Tanh, last, t_mlp, scale=0.5)
                    o.append(t_ga[c - 5])
                else:
                    c -= 8
                    r = RAW[:, c % 4, :]
                    e = copy(AC, r[:, 1:257], bv, last, raw_free[c % 4])
                    x = act(PF[:, c, :], bv, ACT.Copy, last, t_c0, t_mlp, scale=c0[:, c:c + 1])
                    o += [e, x]
                    x = stt(PF[:, c, :], r[:, 0:256], smu[:, 0, c:c + 1], PF[:, c, :], MUL, ADD, e, x, zz)
                    t_pf[c] = stt(PF[:, c, :], r[:, 2:258], smu[:, 1, c:c + 1], PF[:, c, :], MUL, ADD, x)
                    raw_free[c % 4] = t_pf[c]
            free(i, *o)

        for s in (1, 2, 3):
            in_step(s)
        cw = pk("convw").rearrange("p (c k) -> p c k", c=3)
        t_cv = [None] * 3
        for c in range(3):
            a = ts(DV, GA[:, c, :], GA[:, c, :], 0.5, 0.5, MUL, ADD, t_ga[c])
            a = tt(DV, U[:, c, 15:271], VAL[:, c, :], GA[:, c, :], MUL, a, t_val[c])
            t_cv[c] = ts(DV, CA[:, c, :], U[:, c, 0:256], cw[:, c, 0:1], pk("convb")[:, c:c + 1], MUL, ADD, a, zz)
        for s in (5, 6, 4, 7, 8, 9, 0):
            in_step(s)
            taps = {5: range(1, 6), 6: range(6, 11), 4: range(11, 16), 7: range(16, 21), 8: range(21, 26),
                    9: range(26, 31), 0: ()}[s]
            for k in taps:
                for c in range(3):
                    t_cv[c] = stt(CA[:, c, :], U[:, c, k:k + 256], cw[:, c, k:k + 1], CA[:, c, :], MUL, ADD, t_cv[c])

        O2S = region(106, 2, 256)
        s2 = tiny(32).rearrange("p (a h q) -> p a h q", a=4, h=4)
        t_o2 = []
        pf2, ptf2 = [None, None], [None, None]

        def mem_head(h):
            c, r0 = h // 2, 64 * (h % 2)
            i, b, rd = bank()
            bv = b[:, :].rearrange("p (q m) -> p q m", q=2)
            for q in range(2):
                t = mm(bv[:, q, :], [(QH[r0:r0 + 64, c, q * 128:(q + 1) * 128], KH[r0:r0 + 64, c, :])],
                       t_q2, t_kh, rd)
            m = s2[:, 0, h, :]
            a = DV.run(lambda e: e.tensor_reduce(m, bv, AX.X, ALU.max), t)
            a = ts(DV, s2[:, 1, h, :], m, -0.125, None, MUL, None, a)
            pv = P2[:, h % 2, :].rearrange("p (q m) -> p q m", q=2)
            x = [act(pv[:, q, :], bv[:, q, :], ACT.Exp, a, pf2[h % 2], scale=0.125, bias=s2[:, 1, h, q:q + 1],
                     accum=s2[:, 2, h, q:q + 1]) for q in range(2)]
            free(i, *x)
            r = DV.run(lambda e: e.reciprocal(s2[:, 3, h, :], s2[:, 2, h, :]), x)
            i, b, rd = bank()
            for j in range(4):
                t = turn(b[:, j * 128:(j + 1) * 128], P2[:, h % 2, j * 128:(j + 1) * 128], x, rd)
            pf2[h % 2] = t
            e = copy(AC, PT2[:, h % 2, :], b[:, :], t, ptf2[h % 2])
            free(i, e)
            i, b, rd = bank()
            for q in range(2):
                t = mm(b[:, q * 64:(q + 1) * 64],
                       [(PT2[:, h % 2, (2 * q + m) * 128:(2 * q + m + 1) * 128], VH[:, m, h * 64:(h + 1) * 64])
                        for m in range(2)], e, t_vh, rd)
            t_o2.append(tt(DV, O2S[:, :, h * 64:(h + 1) * 64], b[:, 0:128].rearrange("p (q d) -> p q d", q=2),
                           s2[:, 3, h, :].unsqueeze(2).to_broadcast([128, 2, 64]), MUL, t, r))
            free(i, t_o2[-1])
            ptf2[h % 2] = t

        def mem_end():
            i, b, rd = bank()
            for q in range(2):
                for c in range(2):
                    t = turn(b[:, (c * 2 + q) * 128:(c * 2 + q + 1) * 128], O2S[:, q, c * 128:(c + 1) * 128], t_o2, rd)
            e = copy(AC, MIX[:, 0:2, :], b[:, :].rearrange("p (c t) -> p c t", c=2), t)
            free(i, e)
            return e

        KK = region(36, 3, 256)
        RRK = region(39, 3, 256)
        AA = region(42, 3, 256)
        LW = region(45, 3, 256)
        X1 = region(48, 3, 256)
        RHS = [region(51 + 1.5 * d, 384) for d in range(2)]
        KD = [region(54 + 3 * d, 3, 256) for d in range(2)]
        SA = [region(60 + 1.5 * d, 384) for d in range(2)]
        VV = [region(100 + 3 * d, 6, 128) for d in range(2)]
        Y = region(106, 2, 384)
        KR = [region(109 + 12 * d, 6, 2, 128) for d in range(2)]
        BG = [region(115 + 12 * d, 6, 2, 128) for d in range(2)]
        VN = region(133, 2, 384)
        BGN = [region(16 + 3 * d, 2, 384) for d in range(2)]
        ST = [region(22 + d, 3, 64) for d in range(2)]
        G = region(36, 2, 384)
        XX = [region(64 + 18 * d, 6, 2, 128) for d in range(2)]
        LN = [region(70 + 18 * d, 6, 2, 128) for d in range(2)]
        MQ = [region(76 + 18 * d, 6, 2, 128) for d in range(2)]

        def tiles(v):
            return v.rearrange("p c (i t) -> p (c i) t", i=2)

        hw = tiny(12)
        t_hw = [ts(PL, hw[:, 0:6], pk("dw0"), 0.5, 0.0, MUL, ADD, t_pack),
                ts(PL, hw[:, 6:12], pk("ia0"), 0.5, 0.0, MUL, ADD, t_pack)]
        omka = tiny(3)
        t_ka = ts(PL, omka, pk("ka"), -1.0, 1.0, MUL, ADD, t_pack)

        t_kk = []
        RSK = [X1[:, c, :] for c in range(3)]
        for c in range(3):
            a = ts(DV, KK[:, c, :], PF[:, 3 + c, :], pk("kk")[:, c:c + 1], None, MUL, None, t_pf[3 + c], t_mlp)
            s = act(LW[:, c, :], KK[:, c, :], ACT.Square, a)
            i, b, rd = bank()
            t = mm(b[:, 0:256], [(cn("blk"), LW[:, c, :])], s, rd)
            fr, r = rsq(RSK[c], b[:, 0:256], 1.0, 1e-12, t)
            free(i, fr)
            t_kk.append(tt(DV, KK[:, c, :], KK[:, c, :], RSK[c], MUL, r))
        t_rrk = [ts(DV, RRK[:, c, :], PF[:, c, :], pk("rk")[:, c:c + 1], None, MUL, None, t_pf[c]) for c in range(3)]
        t_wd = act(PF[:, 9, :], PF[:, 9, :], ACT.Tanh, t_pf[9])
        a = act(PF[:, 11, :], PF[:, 11, :], ACT.Tanh, t_pf[11], scale=0.5)
        t_sg = ts(PL, PF[:, 11, :], PF[:, 11, :], 0.5, 0.5, MUL, ADD, a)

        t_vn = []
        for m in range(2):
            i, b, rd = bank()
            for c in range(3):
                t = turn(b[:, c * 128:(c + 1) * 128], PF[:, 6 + c, m * 128:(m + 1) * 128], t_pf[6 + c], rd)
            e = copy(AC, VN[:, m, :], b[:, 0:384], t)
            free(i, e)
            t_vn.append(e)

        es = tiny(6).rearrange("p (d c) -> p d c", d=2)
        ht = tiny(12).rearrange("p (d c i) -> p d c i", d=2, c=3)
        t_es, t_kr, t_bg, t_kd, t_bgn = [None] * 2, [None] * 2, [None] * 2, [None] * 2, [None] * 2
        lw_free, aa_free, x1_free = [None], [None], [t_kk]

        def up(name, src, d, dst, bias, *producers):
            o = []
            for c in range(3):
                i, b, rd = bank()
                t = mm(b[:, 0:256], [(pk(name)[64 * d:64 * d + 64, c * 128:(c + 1) * 128], src[64 * d:64 * d + 64, :])],
                       rd, *producers[:1])
                e = act(dst[:, c, :], b[:, 0:256], ACT.Tanh, t, t_hw, *producers[1:], scale=0.5,
                        bias=bias[:, 3 * d + c:3 * d + c + 1])
                free(i, e)
                o.append(e)
            return o

        aa_free[0] = [t_mask]
        for d in range(2):
            t = up("dup", PF[:, 9, :], d, LW, hw[:, 0:6], t_wd, lw_free[0], t_kk)
            u = up("iup", PF[:, 10, :], d, AA, hw[:, 6:12], t_pf[10], aa_free[0])
            t = ts(DV, LW, LW, -0.5 * DECAY, -0.5 * DECAY, MUL, ADD, t)
            sc = [DV.run(lambda e, c=c, m=m: e.tensor_tensor_scan(
                X1[:, c, m * 128:(m + 1) * 128], ones, LW[:, c, m * 128:(m + 1) * 128], 0.0, MUL, ADD),
                t, x1_free[0], t_const) for c in range(3) for m in range(2)]
            hd = ht[:, d, :, :].rearrange("p c i -> p (c i)")
            h = ts(DV, hd, tiles(X1)[:, :, 127], 0.5, None, MUL, None, sc)
            x1 = tt(DV, tiles(X1), tiles(X1), hd.unsqueeze(2).to_broadcast([128, 6, 128]), SUB, h)
            x2 = tt(DV, LW, X1, LW, SUB, x1)
            a = tt(DV, es[:, d, :], ht[:, d, :, 0], ht[:, d, :, 1], ADD, h)
            x1v, x2v = tiles(X1), tiles(LW)
            if d == 0:
                e0 = act(KR[d][:, :, 0, :], x2v, ACT.Exp, x2, t_h)
                e1 = act(KR[d][:, :, 1, :], x1v, ACT.Exp, x1)
                e2 = act(BG[d][:, :, 1, :], x1v, ACT.Exp, x1, scale=-1.0)
            else:
                e0 = act(KR[d][:, :, 0, :], x1v, ACT.Exp, x1, scale=-1.0)
                e1 = act(KR[d][:, :, 1, :], x2v, ACT.Exp, x2, scale=-1.0)
                e2 = act(BG[d][:, :, 1, :], x2v, ACT.Exp, x2)
            lw_free[0], x1_free[0] = [e0, e1, e2], [e0, e1, e2]
            t_es[d] = act(es[:, d, :], es[:, d, :], ACT.Exp, a)
            u = ts(DV, AA, AA, 0.5, 0.5, MUL, ADD, u)
            k0 = [ts(DV, KD[d][:, c, :], AA[:, c, :], pk("ka")[:, c:c + 1], omka[:, c:c + 1], MUL, ADD, u, t_ka)
                  for c in range(3)]
            t_kd[d] = tt(PL, KD[d], KD[d], PF[:, 3:6, :], MUL, k0, t_pf[3:6])
            n = stt(AA, AA, -1.0, KK, MUL, MUL, k0, t_kk)
            a = tt(PL, KR[d][:, :, 0, :], KR[d][:, :, 0, :], tiles(KK), MUL, e0, t_kk)
            b_ = tt(PL, KR[d][:, :, 1, :], KR[d][:, :, 1, :], tiles(PF[:, 0:3, :]), MUL, e1, t_pf[0:3])
            t_kr[d] = [a, b_]
            a = tt(DV, BG[d][:, :, 0, :], tiles(AA), BG[d][:, :, 1, :], MUL, n, e2)
            aa_free[0] = a
            b_ = tt(DV, BG[d][:, :, 1, :], BG[d][:, :, 1, :], tiles(KD[d]), MUL, e2, t_kd[d], a)
            t_bg[d] = [a, b_]

        i, b, rd = bank()
        t = mm(b[:, 0:256], [(ones, CA[:, c, :]) for c in range(3)], t_cv, rd)
        a = ts(DV, CM, b[:, 0:256], 1.0 / 384, None, MUL, None, t)
        free(i, a)
        a = tt(DV, CA, CA, CM.unsqueeze(1).to_broadcast([128, 3, 256]), SUB, a)
        s = act(CSQ, CA, ACT.Square, a)
        i, b, rd = bank()
        t = mm(b[:, 0:256], [(ones, CSQ[:, c, :]) for c in range(3)], s, rd)
        fr, r = rsq(CR, b[:, 0:256], 1.0 / 384, 1e-5, t)
        free(i, fr)
        a = tt(PL, CA, CA, CR.unsqueeze(1).to_broadcast([128, 3, 256]), MUL, r)
        z = [ts(PL, CA[:, c, :], CA[:, c, :], pk("lng")[:, c:c + 1], pk("lnb")[:, c:c + 1], MUL, ADD, a)
             for c in range(3)]
        a = act(CSQ, CA, ACT.Tanh, z, scale=0.5)
        a = ts(PL, CSQ, CSQ, 0.5, 0.5, MUL, ADD, a)
        t_conv = tt(PL, MIX[:, 2:5, :], CA, CSQ, MUL, a)
        for h in range(4):
            mem_head(h)
        t_mem2 = mem_end()

        for d in range(2):
            for y in range(2):
                i, b, rd = bank()
                for c in range(3):
                    t = turn(b[:, c * 128:(c + 1) * 128], BG[d][:, 2 * c + d, y, :], t_bg[d], rd)
                e = copy(AC, BGN[d][:, y, :], b[:, 0:384], t)
                free(i, e)
                t_bgn[d] = [e, t_bgn[d]] if y == 0 else [t_bgn[d][0], e]

        lm = maskt[:, 0:LEVELS * 384].rearrange("p (l m) -> p l m", l=LEVELS)
        si = maskt[:, LEVELS * 384:LEVELS * 384 + 512].rearrange("p (d m) -> p d m", d=2)
        t_zero = [None] * 2
        for d in range(2):
            t_zero[d] = [PL.run(lambda e, d=d: e.memset(LN[d], 0.0), t_conv, t_mem2),
                         PL.run(lambda e, d=d: e.memset(MQ[d], 0.0), t_conv, t_mem2)]
        set_free = [None, None]
        t_st = [None, None]
        y_done = [None, None]

        def flat(v):
            return v.rearrange("p a t -> p (a t)")

        def batch(d, m, second):
            x_, l_, q_ = XX[d], LN[d], MQ[d]
            init = PL.run(lambda e: e.tensor_copy(x_.rearrange("p u a t -> p (u a) t"),
                                                  ident.unsqueeze(1).to_broadcast([128, 12, 128])),
                          set_free[d], t_conv, t_mem2, t_const)
            ready = [None] * 6
            for p in range(3):
                j, bq, rdq = bank()
                o = []
                tq = None
                for u in (2 * p, 2 * p + 1):
                    r0, idx = 64 * (u % 2), 2 * (u // 2) + m
                    kr = KR[d][r0:r0 + 64, idx, :, :]
                    be = BG[d][r0:r0 + 64, idx, 0, :]
                    ga = BG[d][r0:r0 + 64, idx, 1, :]
                    i, b, rd = bank()
                    mm(b[:, 0:128], [(kr[:, 0, :], be)], t_kr[d], t_bg[d], rd)
                    t = mm(b[:, 128:384], [(be, flat(kr))])
                    tq = mm(bq[:, (u % 2) * 256:(u % 2) * 256 + 256], [(ga, flat(kr))], rdq, tq)
                    a = DV.run(lambda e, u=u, b=b: e.copy_predicated(flat(x_[:, u, :, :]), lm[:, 0, 128 * d:128 * d + 256],
                                                                     b[:, 0:256]), t, init, t_mask)
                    c = DV.run(lambda e, u=u, b=b: e.copy_predicated(flat(l_[:, u, :, :]), si[:, d, :], b[:, 128:384]),
                               t, t_zero[d], set_free[d])
                    free(i, a, c)
                    o += [a, c]
                c = DV.run(lambda e, p=p, bq=bq: e.copy_predicated(
                    q_[:, 2 * p:2 * p + 2, :, :].rearrange("p u a t -> p u (a t)"),
                    si[:, d, :].unsqueeze(1).to_broadcast([128, 2, 256]),
                    bq[:, :].rearrange("p (u t) -> p u t", u=2)), tq, t_zero[d], set_free[d])
                free(j, c)
                ready[2 * p] = ready[2 * p + 1] = [*o, c]
            yield
            vfree = [None] * 3
            for lv in range(1, LEVELS):
                tv = []
                for p in range(3):
                    i, b, rd = bank()
                    for u in (2 * p, 2 * p + 1):
                        t = mm(b[:, (u % 2) * 128:(u % 2) * 128 + 128], [(l_[:, u, 0, :], x_[:, u, 0, :])], ready[u], rd)
                    e = copy(AC, VV[d][:, 2 * p:2 * p + 2, :], b[:, 0:256].rearrange("p (u t) -> p u t", u=2), t,
                             vfree[p], set_free[d])
                    free(i, e)
                    tv.append(e)
                yield
                for p in range(3):
                    i, b, rd = bank()
                    for u in (2 * p, 2 * p + 1):
                        o = (u % 2) * 256
                        mm(b[:, o:o + 128], [(x_[:, u, 1, :], VV[d][:, u, :])], tv[p], rd)
                        t = mm(b[:, o + 128:o + 256], [(VV[d][:, u, :], x_[:, u, 1, :])])
                    vfree[p] = t
                    c = DV.run(lambda e, p=p, b=b, lv=lv: e.copy_predicated(
                        x_[:, 2 * p:2 * p + 2, :, :].rearrange("p u a t -> p u (a t)"),
                        lm[:, lv, 128 * d:128 * d + 256].unsqueeze(1).to_broadcast([128, 2, 256]),
                        b[:, :].rearrange("p (u t) -> p u t", u=2)), t)
                    free(i, c)
                    ready[2 * p] = ready[2 * p + 1] = c
                yield

            def st(h):
                return ST[d][64 * (h % 2):64 * (h % 2) + 64, h // 2, :]

            def kr_(h, a):
                return KR[d][64 * (h % 2):64 * (h % 2) + 64, 2 * (h // 2) + m, a, :]

            def vn(h):
                return VN[:, m, h * 64:(h + 1) * 64]

            i, b, rd = bank()
            for h in range(6):
                pr = [(q_[:, h, 0, :], vn(h))]
                if second:
                    pr.append((kr_(h, 0), st(h)))
                t = mm(b[:, h * 64:(h + 1) * 64], pr, t if h and second else None, t_vn, ready, t_st[d] if second else None, rd)
            e = copy(DV, RHS[d], b[:, 0:384], t)
            free(i, e)
            yield
            i, b, rd = bank()
            for h in range(6):
                t = mm(b[:, h * 64:(h + 1) * 64], [(x_[:, h, 1, :], RHS[d][:, h * 64:(h + 1) * 64])], e, rd)
            e = copy(DV, SA[d], b[:, 0:384], t)
            free(i, e)
            yield
            if not second:
                i, b, rd = bank()
                for h in range(6):
                    r0 = 64 * (h % 2)
                    t = mm(b[r0:r0 + 64, (h // 2) * 64:(h // 2) * 64 + 64],
                           [(BGN[d][:, 0, h * 64:(h + 1) * 64], SA[d][:, h * 64:(h + 1) * 64]),
                            (BGN[d][:, 1, h * 64:(h + 1) * 64], vn(h))], e, t_bgn[d], rd)
                t_st[d] = tt(DV, ST[d], b[:, 0:192].rearrange("p (c j) -> p c j", c=3),
                             es[:, d, :].unsqueeze(2).to_broadcast([128, 3, 64]), MUL, t, t_es[d])
                free(i, t_st[d])
            i, b, rd = bank()
            for h in range(6):
                pr = [(l_[:, h, 1, :], SA[d][:, h * 64:(h + 1) * 64]), (q_[:, h, 1, :], vn(h))]
                if second:
                    pr.append((kr_(h, 1), st(h)))
                t = mm(b[:, h * 64:(h + 1) * 64], pr, t if h and second else None, e, rd)
            set_free[d] = t
            if second:
                y_done[m] = tt(DV, Y[:, m, :], b[:, 0:384], Y[:, m, :], ADD, t, y_done[m])
            else:
                y_done[m] = copy(DV, Y[:, m, :], b[:, 0:384], t, t_mem2)
            free(i, y_done[m])
            yield

        def together(*gens):
            live = list(gens)
            while live:
                for g in list(live):
                    try:
                        next(g)
                    except StopIteration:
                        live.remove(g)

        together(batch(0, 0, False), batch(1, 1, False))
        a = tt(PL, KD[0], KD[0], KD[1], ADD, t_kd, t_bg[0], t_bg[1])
        t_bp = tt(PL, KD[0], KD[0], RRK, MUL, a, t_rrk)
        i, b, rd = bank()
        for m in range(2):
            for c in range(3):
                t = mm(b[:, m * 6 + 2 * c:m * 6 + 2 * c + 2], [(KD[0][:, c, m * 128:(m + 1) * 128], cn("ind2"))], t_bp, rd)
        bon = tiny(12).rearrange("p (m h) -> p m h", m=2)
        t_bon = copy(DV, bon, b[:, 0:12].rearrange("p (m h) -> p m h", m=2), t)
        free(i, t_bon)
        t_g = []
        for m in range(2):
            i, b, rd = bank()
            t = mm(b[:, 0:384], [(PF[:, 11, m * 128:(m + 1) * 128], pk("gup"))], t_sg, rd)
            e = copy(AC, G[:, m, :], b[:, 0:384], t, t_kr, t_bg)
            free(i, e)
            t_g.append(e)
        together(batch(0, 1, True), batch(1, 0, True))

        gst = tiny(24).rearrange("p (m a h) -> p m a h", m=2, a=2)
        t_mix = []
        for m in range(2):
            y = Y[:, m, :]
            tmp = region(39 + 1.5 * m, 384)
            yv = y.rearrange("p (h d) -> p h d", h=6)
            tv = tmp.rearrange("p (h d) -> p h d", h=6)
            mu, rs = gst[:, m, 0, :], gst[:, m, 1, :]

            def wide(v):
                return v.unsqueeze(2).to_broadcast([128, 6, 64])

            a = DV.run(lambda e, mu=mu, yv=yv: e.tensor_reduce(mu, yv, AX.X, ADD), y_done[m])
            a = ts(DV, mu, mu, 1.0 / 64, None, MUL, None, a)
            a = tt(DV, yv, yv, wide(mu), SUB, a)
            s = act(tmp, y, ACT.Square, a, t_bp)
            s = DV.run(lambda e, rs=rs, tv=tv: e.tensor_reduce(rs, tv, AX.X, ADD), s)
            _, r = rsq(rs, rs, 1.0 / 64, 64e-5, s)
            vb = tt(PL, tv, VN[:, m, :].rearrange("p (h d) -> p h d", h=6), wide(bon[:, m, :]), MUL, t_bon, r, t_vn)
            vb = tt(PL, tmp, tmp, pk("lnxb"), ADD, vb)
            a = tt(DV, yv, yv, wide(rs), MUL, r)
            a = tt(DV, y, y, pk("lnxg"), MUL, a)
            a = tt(DV, y, y, tmp, ADD, a, vb)
            a = tt(DV, y, y, G[:, m, :], MUL, a, t_g)
            i, b, rd = bank()
            for c in range(3):
                t = turn(b[:, c * 128:(c + 1) * 128], y[:, c * 128:(c + 1) * 128], a, rd)
            e = copy(AC, MIX[:, 5:8, m * 128:(m + 1) * 128], b[:, 0:384].rearrange("p (c t) -> p c t", c=3), t)
            free(i, e)
            t_mix.append(e)
        for k in range(6):
            add_slot(arena[:, (85 + 8 * k) * 256:(93 + 8 * k) * 256], *t_mix)
        refill()

        t_x3 = [None] * 8
        for s in range(4):
            wv, t = slab("wo2", s, 8)
            i, b, rd = bank()
            for j in range(2):
                last = mm(b[:, j * 256:(j + 1) * 256],
                          [(wv[:, k, j * 128:(j + 1) * 128], MIX[:, k, :]) for k in range(8)],
                          t, t_conv, t_mem2, t_mix, rd)
            done("wo2", s, last)
            xs = X[:, 2 * s:2 * s + 2, :]
            e = tt(DV, xs, b[:, :].rearrange("p (j t) -> p j t", j=2), xs, ADD, last)
            free(i, e)
            t_x3[2 * s] = t_x3[2 * s + 1] = e

        H3 = region(16, 8, 256)
        H3N = region(24, 2, 1024)
        XE = region(32, 8, 512)
        OH = region(48, 2, 512)
        GG = region(52, 2, 512)
        GT = region(56, 4, 256)
        W0, W1, W2 = region(60, 256), region(61, 256), region(62, 256)
        RS4 = region(84, 256)
        W3 = region(63, 256)
        t_w3 = PL.run(lambda e: e.memset(W3, 1.0), t_mix)
        t_r = norm(X, t_x3, SQ2, RS4, last)
        t_h3 = [stt(H3[:, k, :], X[:, k, :], pk("nffn")[:, k:k + 1], RS4, MUL, MUL, t_r) for k in range(8)]
        wr = pk("wr").rearrange("p (k e) -> p k e", k=8)
        i, b, rd = bank()
        for m in range(2):
            t = mm(b[:, m * 16:(m + 1) * 16], [(H3[:, k, m * 128:(m + 1) * 128], wr[:, k, :]) for k in range(8)], t_h3, rd)
        aff = tiny(32).rearrange("p (m e) -> p m e", m=2)
        rst = tiny(6).rearrange("p (a m) -> p a m", a=3)
        lg = b[:, 0:32].rearrange("p (m e) -> p m e", m=2)
        a = DV.run(lambda e: e.tensor_reduce(rst[:, 0, :], lg, AX.X, ALU.max, negate=True), t)
        x = [act(aff[:, m, :], lg[:, m, :], ACT.Exp, a, bias=rst[:, 0, m:m + 1], accum=rst[:, 1, m:m + 1])
             for m in range(2)]
        free(i, *x)
        a = DV.run(lambda e: e.reciprocal(rst[:, 2, :], rst[:, 1, :]), x)
        t_aff = tt(DV, aff, aff, rst[:, 2, :].unsqueeze(2).to_broadcast([128, 2, 16]), MUL, a)
        t_h3n = []
        for m in range(2):
            for g2 in range(2):
                i, b, rd = bank()
                for j in range(4):
                    t = turn(b[:, j * 128:(j + 1) * 128], H3[:, 4 * g2 + j, m * 128:(m + 1) * 128], t_h3, rd)
                e = copy(AC, H3N[:, m, g2 * 512:(g2 + 1) * 512], b[:, :], t)
                free(i, e)
                t_h3n.append(e)
        i, b, rd = bank()
        for m in range(2):
            t = mm(b[0:16, m * 128:(m + 1) * 128], [(aff[:, m, :], ident)], t_aff, rd)
        a = copy(DV, W0[0:16, :], b[0:16, 0:256], t)
        free(i, a)
        m8 = tiny(32).rearrange("p (r v) -> p r v", r=4)
        src = W0
        for r in range(4):
            dst = (W1, W2)[r % 2]
            a = DV.run(lambda e, r=r, src=src: e.max(m8[0:16, r, :], src[0:16, :]), a)
            a = DV.run(lambda e, r=r, src=src, dst=dst: e.match_replace(dst[0:16, :], m8[0:16, r, :], src[0:16, :], -1.0), a)
            src = dst
        a = ts(DV, W1[0:16, :], W2[0:16, :], 0.0, None, ALU.is_lt, None, a)
        a = DV.run(lambda e: e.tensor_tensor_scan(W0[0:16, :], W3[0:16, :], W1[0:16, :], 0.0, MUL, ADD), a, t_w3)
        a = tt(DV, W0[0:16, :], W0[0:16, :], W1[0:16, :], MUL, a)
        i, b, rd = bank()
        for m in range(2):
            t = mm(b[:, m * 16:(m + 1) * 16], [(W0[0:16, m * 128:(m + 1) * 128], ident[0:16, 0:16])], a, rd)
        pos = tiny(32).rearrange("p (m e) -> p m e", m=2)
        a = copy(DV, pos, b[:, 0:32].rearrange("p (m e) -> p m e", m=2), t)
        free(i, a)
        t_oh, t_gg = [], []
        for m in range(2):
            ov = OH[:, m, :].rearrange("p (e s) -> p e s", e=16)
            t_oh.append(tt(DV, ov, pos[:, m, :].unsqueeze(2).to_broadcast([128, 16, 32]),
                           cn("iota").unsqueeze(1).to_broadcast([128, 16, 32]), ALU.is_equal, a, t_const))
        for m in range(2):
            t_gg.append(tt(PL, GG[:, m, :].rearrange("p (e s) -> p e s", e=16),
                           OH[:, m, :].rearrange("p (e s) -> p e s", e=16),
                           aff[:, m, :].unsqueeze(2).to_broadcast([128, 16, 32]), MUL, t_oh[m], t_aff))
        t_xe = []
        for k in range(8):
            i, b, rd = bank()
            t = mm(b[:, :], [(H3N[:, m, k * 128:(k + 1) * 128], OH[:, m, :]) for m in range(2)], t_oh, t_h3n, rd)
            e = copy(AC if k % 2 else DV, XE[:, k, :], b[:, :], t)
            free(i, e)
            t_xe.append(e)

        HID = region(64, 2, 256)
        TMP = region(66, 2, 256)
        YT = region(68, 2, 8, 128)
        YE = region(76, 2, 1024)
        t_gt = []
        hid, t_yt = {}, {}
        yt_free, ye_free = [None, None], [None, None]

        def gate_up(e):
            i, b, rd = bank()
            for half, name in enumerate(("eg", "eu")):
                for s in range(4):
                    wv, t = slab(name, 4 * e + s, 8)
                    for j in range(2):
                        o = half * 256 + (2 * s + j) * 32
                        last = mm(b[:, o:o + 32], [(wv[:, k, j * 128:(j + 1) * 128], XE[:, k, e * 32:(e + 1) * 32])
                                                   for k in range(8)], t, t_xe, rd)
                    done(name, 4 * e + s, last)
            tm = TMP[:, e % 2, :]
            a = act(tm, b[:, 0:256], ACT.Tanh, last, hid.get(e - 2), scale=0.5)
            a = ts(DV, tm, tm, 0.5, 0.5, MUL, ADD, a)
            a = tt(DV, tm, b[:, 0:256], tm, MUL, a)
            hid[e] = tt(DV, HID[:, e % 2, :], b[:, 256:512], tm, MUL, a, t_yt.get(e - 2))
            free(i, hid[e])

        def down(e):
            g = e // 4
            i, b, rd = bank()
            for s in range(4):
                wv, t = slab("ed", 4 * e + s, 8)
                for j in range(2):
                    o = (2 * s + j) * 32
                    last = mm(b[:, o:o + 32], [(wv[:, k, j * 128:(j + 1) * 128], HID[:, e % 2, k * 32:(k + 1) * 32])
                                               for k in range(8)], t, hid[e], rd)
                done("ed", 4 * e + s, last)
            t_yt[e] = copy(AC, YT[:, g % 2, :, (e % 4) * 32:(e % 4 + 1) * 32],
                           b[:, 0:256].rearrange("p (j s) -> p j s", j=8), last, yt_free[g % 2])
            free(i, t_yt[e])

        t_x4 = t_x3

        def combine(g):
            o = []
            for h in range(2):
                i, b, rd = bank()
                for j in range(4):
                    t = turn(b[:, j * 128:(j + 1) * 128], YT[:, g % 2, 4 * h + j, :], t_yt[4 * g + 3], rd)
                e = copy(AC, YE[:, g % 2, h * 512:(h + 1) * 512], b[:, :], t, ye_free[g % 2])
                free(i, e)
                o.append(e)
            yt_free[g % 2] = t
            for c2_ in range(4):
                i, b, rd = bank()
                for j in range(2):
                    c = 2 * c2_ + j
                    t = mm(b[:, j * 256:(j + 1) * 256], [(YE[:, g % 2, c * 128:(c + 1) * 128], GT[:, g, :])], o, t_gt, rd)
                xs = X[:, 2 * c2_:2 * c2_ + 2, :]
                e = tt(DV, xs, b[:, :].rearrange("p (j t) -> p j t", j=2), xs, ADD, t, t_h3)
                free(i, e)
                t_x4[2 * c2_] = t_x4[2 * c2_ + 1] = e
            ye_free[g % 2] = t

        for e in range(18):
            if e < 16:
                gate_up(e)
            if e == 0:
                for g2 in range(2):
                    i, b, rd = bank()
                    for j in range(2):
                        for m in range(2):
                            g = 2 * g2 + j
                            t = turn(b[:, (2 * j + m) * 128:(2 * j + m + 1) * 128], GG[:, m, g * 128:(g + 1) * 128],
                                     t_gg, rd)
                    x = copy(AC, GT[:, 2 * g2:2 * g2 + 2, :], b[:, :].rearrange("p (j t) -> p j t", j=2), t)
                    free(i, x)
                    t_gt.append(x)
            if 1 <= e <= 16:
                down(e - 1)
            if e >= 5 and (e - 5) % 4 == 0:
                combine((e - 5) // 4)

        t_r = norm(X, t_x4, SQ2, RS4)
        OUT = H3
        s_out = sem("s_out")
        for h in range(2):
            o = [stt(OUT[:, k, :], X[:, k, :], pk("fing")[:, k:k + 1], RS4, MUL, MUL, t_r) for k in range(4 * h, 4 * h + 4)]
            SP.load(out[:, 4 * h:4 * h + 4, :], OUT[:, 4 * h:4 * h + 4, :], s_out, 16, o)
        SP.wait([(s_out, 32)])
        assert not pending and not landed

        block = ctx.enter_context(nc.Block())

        @block.tensor
        def _(e):
            for f in PE.queue:
                f(e)

        @block.scalar
        def _(e):
            for f in AC.queue:
                f(e)

        @block.vector
        def _(e):
            for f in DV.queue:
                f(e)

        @block.gpsimd
        def _(e):
            for f in PL.queue:
                f(e)

        @block.sync
        def _(e):
            for f in SP.queue:
                f(e)


def shape_constants():
    t, p = np.arange(256), np.arange(128)
    o = {"ident": np.eye(128), "ones": np.ones((128, 128)), "blk": (p[:, None] // 64 == p[None] // 64)}
    th = 2 * np.pi * ((p[:, None] * p[None]) % 128) / 128
    o["dftc"] = np.concatenate([np.cos(th), np.sin(th)], 1)
    ph = 2 * np.pi * ((t[:, None] * t[None]) % 256) / 256
    n = np.stack([np.cos(ph), -np.sin(ph)]) / np.sqrt(256.0 * 128.0)
    o["dftn"] = n.reshape(2, 2, 128, 256).transpose(2, 0, 1, 3)
    d = np.arange(64)
    inv = 10000.0 ** (-(2.0 * (d % 16)) / 32.0)
    at = np.where(d[None] < 32, (t // 64)[:, None], (t % 64)[:, None])
    ang = at.astype(np.float32) * inv.astype(np.float32)[None]
    sg = np.where(d % 32 < 16, -1.0, 1.0)
    o["cos"] = np.cos(ang).reshape(2, 128, 64).transpose(1, 0, 2)
    o["sin"] = (np.sin(ang) * sg).reshape(2, 128, 64).transpose(1, 0, 2)
    c = p % 64
    start = np.clip(c - 8, 0, 48)
    kc = np.arange(64)
    o["amask"] = np.where((kc[None] >= start[:, None]) & (kc[None] < start[:, None] + 16), 0.0, -1e30)
    o["iota"] = np.tile(np.arange(1, 33), (128, 1))
    o["ind2"] = p[:, None] // 64 == np.arange(2)[None]
    const = np.concatenate([np.asarray(o[name], np.float32).reshape(128, n) for name, n in CONST], 1)
    m = []
    for lv in range(LEVELS):
        b = 1 << lv
        low = (p[:, None] // (2 * b) == p[None] // (2 * b)) & (p[:, None] % (2 * b) >= b) & (p[None] % (2 * b) < b)
        m += [low, low.T, low]
    up = [p[:, None] < p[None], p[:, None] <= p[None]]
    masks = np.concatenate(m + up + [p[:, None] > p[None], p[:, None] >= p[None]], 1).astype(np.float32)
    return np.ascontiguousarray(const), np.ascontiguousarray(masks)


def kernel(**inputs):
    import concourse.bacc as _bacc
    from concourse.bass_utils import run_bass_kernel_spmd as _run

    a = {n: np.asarray(v) for n, v in inputs.items()}

    def cols(v):
        v = np.asarray(v).reshape(-1)
        return v.reshape(-1, 128).T

    def rowsof(v):
        return np.broadcast_to(np.asarray(v).reshape(1, -1), (128, v.size))

    def tokens(v):
        return np.ascontiguousarray(v.reshape(256, 8, 128).transpose(2, 1, 0))

    def slabs(v, n):
        k = v.shape[0] // 128
        return v.reshape(k, 128, v.shape[1] // n, n).transpose(2, 1, 0, 3).reshape(-1, 128, SLAB)

    pk = {
        "c2": np.stack([cols(a["c"]), cols(a["c_ctx"])], 2).reshape(128, 16),
        "bada": cols(a["b_ada"]), "n1": cols(a["norm1_g"]), "n2": cols(a["norm2_g"]),
        "qg": rowsof(a["q_norm_g"]), "kg": rowsof(a["k_norm_g"]),
        "nmix": cols(a["norm_mix_g_2"]), "nmem": cols(a["norm_mem_g_2"]),
        "convw": a["conv_w_2"][0].reshape(31, 3, 128).transpose(2, 1, 0).reshape(128, 93),
        "convb": cols(a["conv_b_2"]), "lng": cols(a["conv_ln_g_2"]), "lnb": cols(a["conv_ln_b_2"]),
        "smu": cols(a["shift_mu_2"]), "dw0": cols(a["decay_w0_2"]), "ia0": cols(a["iclr_a0_2"]),
        "kk": cols(a["k_k_2"]), "ka": cols(a["k_a_2"]), "rk": cols(a["r_k_2"]),
        "nffn": cols(a["norm_ffn_g_2"]), "fing": cols(a["final_norm_g_2"]),
        "lnxg": rowsof(a["lnx_g_2"]), "lnxb": rowsof(a["lnx_b_2"]),
        "wr": a["w_router_2"][0].reshape(8, 128, 16).transpose(1, 0, 2).reshape(128, 128),
        "dup": a["decay_up_2"].reshape(128, 384), "iup": a["iclr_up_2"].reshape(128, 384),
        "gup": a["gate_up_2"].reshape(128, 384),
    }
    pack = np.ascontiguousarray(np.concatenate([pk[n].reshape(128, c) for n, c in PACK], 1))
    r, c = np.arange(4), np.arange(64)
    dr = r[None, :] - r[:, None] + 7
    dc = np.clip(c[None, :] - c[:, None] + 15, 0, 30)
    bias = a["rpb"][0][:, dr[:, None, :, None], dc[None, :, None, :]].reshape(8, 2, 128, 256)
    bias = np.ascontiguousarray(bias.transpose(2, 0, 1, 3).reshape(128, 4096))
    const, masks = shape_constants()
    m2 = a["w_mlp2"][0].reshape(2, 16, 128, 8, 128).transpose(3, 0, 2, 1, 4).reshape(16, 128, SLAB)
    ws = {
        "ada": slabs(a["w_ada"][0], 256), "win": slabs(a["w_in"][0], 256), "gate": slabs(a["w_branch_gate"][0], 256),
        "fo": slabs(a["w_fourier_out"][0], 512), "ao": slabs(a["w_attn_out"][0], 512), "wo": slabs(a["w_out"][0], 256),
        "m1": slabs(a["w_mlp1"][0], 256), "m2": m2, "win2": slabs(a["w_in_2"][0], 256),
        "mk": slabs(a["w_mk_2"][0], 256), "mv": slabs(a["w_mv_2"][0], 256), "wo2": slabs(a["w_out_2"][0], 256),
    }
    for n, full in (("eg", "w_e_gate_2"), ("eu", "w_e_up_2"), ("ed", "w_e_down_2")):
        v = a[full][0]
        ws[n] = v.reshape(16, 8, 128, 4, 256).transpose(0, 3, 2, 1, 4).reshape(64, 128, SLAB)

    arrays = {
        "xT": tokens(a["x"]), "cT": tokens(a["ctx"]), "memT": tokens(a["mem_2"]), "pack": pack, "bias": bias,
        "const": const, "masks": masks,
    }
    for n, v in ws.items():
        arrays["w_" + n] = np.ascontiguousarray(v)
    nc = _bacc.Bacc("TRN2", target_bir_lowering=False, num_devices=1)
    t = {n: nc.dram_tensor(n, v.shape, mybir.dt.from_np(v.dtype), kind="ExternalInput").ap() for n, v in arrays.items()}
    out = nc.dram_tensor("out", (128, 8, 256), F32, kind="ExternalOutput").ap()
    build(nc, t["xT"], t["cT"], t["memT"], t["pack"], t["bias"], t["const"], t["masks"],
          {n: t["w_" + n] for n in ws}, out)
    got = _run(nc, [arrays], core_ids=[0]).results[0]["out"]
    return np.ascontiguousarray(got.transpose(2, 1, 0)).reshape(1, 256, 1024)
```

```python
from collections import deque
from contextlib import ExitStack

import numpy as np

import concourse.bass as bass
from concourse import mybir

F32 = mybir.dt.float32
U8 = mybir.dt.uint8
ALU = mybir.AluOpType
ACT = mybir.ActivationFunctionType
AX = mybir.AxisListType

DECAY = 0.606531
SLAB = 2048

PACK = [
    ("c2", 16), ("bada", 48), ("n1", 8), ("n2", 8), ("qg", 64), ("kg", 64), ("nmix", 8), ("nmem", 8),
    ("convw", 93), ("convb", 3), ("lng", 3), ("lnb", 3), ("smu", 24), ("dw0", 6), ("ia0", 6), ("kk", 3),
    ("ka", 3), ("rk", 3), ("nffn", 8), ("fing", 8), ("lnxg", 384), ("lnxb", 384), ("wr", 128),
    ("dup", 384), ("iup", 384), ("gup", 384),
]
CONST = [
    ("ident", 128), ("ones", 128), ("blk", 128), ("dftc", 256), ("dftn", 1024), ("cos", 128), ("sin", 128),
    ("amask", 64), ("iota", 32), ("ind2", 2),
]
LEVELS = 7
WIN2 = (5, 6, 8, 9, 4, 7, 1, 2, 3, 0)


def offsets(table):
    at, out = 0, {}
    for name, n in table:
        out[name] = (at, n)
        at += n
    return out, at


SLABS = [("ada", 24), ("win", 8), ("gate", 8), ("fo", 2), ("ao", 2), ("wo", 4), ("m1", 16), ("m2", 16),
         ("win2", 10), ("mk", 1), ("mv", 1), ("wo2", 4), ("eg", 64), ("eu", 64), ("ed", 64)]


def slab_order():
    order = [("ada", s) for s in range(8)]
    order += [("win", s) for s in (4, 5, 2, 3, 6, 7, 0, 1)]
    for s in range(4):
        order += [("gate", 2 * s), ("gate", 2 * s + 1)] + [("ada", 8 + 4 * s + q) for q in range(4)]
    order += [("fo", 0), ("fo", 1), ("ao", 0), ("ao", 1)]
    order += [("wo", s) for s in range(4)]
    order += [("mk", 0), ("mv", 0)]
    order += [("m1", s) for s in range(16)] + [("m2", s) for s in range(16)]
    order += [("win2", s) for s in WIN2]
    order += [("wo2", s) for s in range(4)]
    for e in range(17):
        if e < 16:
            order += [(n, 4 * e + 2 * kh + fh) for kh in range(2) for n in ("eg", "eu") for fh in range(2)]
        if e and e % 4 == 0:
            order += [("ed", 4 * x + 2 * kh + fh) for fh in range(2) for kh in range(2) for x in range(e - 4, e)]
    return order


class Engine:

    def __init__(self, sem):
        self.queue, self.sem, self.tick, self.passed = [], sem, 0, {}

    def wait(self, producers):
        need, left = {}, [producers]
        while left:
            p = left.pop()
            if isinstance(p, tuple) and len(p) == 2 and isinstance(p[1], int):
                need[p[0]] = max(need.get(p[0], 0), p[1])
            elif p is not None:
                left.extend(p)
        for sem, value in need.items():
            if self.passed.get(sem, 0) < value:
                self.passed[sem] = value
                self.queue.append(lambda e, s=sem, v=value: e.wait_ge(s, v))

    def run(self, fn, *producers):
        self.wait(producers)
        self.tick += 1
        self.queue.append(lambda e, f=fn, s=self.sem: f(e).then_inc(s, 1))
        return (self.sem, self.tick)

    def quiet(self, fn, *producers):
        self.wait(producers)
        self.queue.append(fn)

    def load(self, out, src, sem, value, *producers):
        self.wait(producers)
        self.queue.append(lambda e: e.dma_start(out, src).then_inc(sem, 16))
        return (sem, value)


def build(nc, xT, cT, memT, pack, bias, const, masks, w, out):
    PO, PN = offsets(PACK)
    CO, CN = offsets(CONST)
    ctx = ExitStack()
    with ctx:
        def sb(name, shape, dt=F32):
            return ctx.enter_context(nc.sbuf_tensor(name, shape, dt))

        def sem(name):
            return ctx.enter_context(nc.semaphore(name))

        NRING = 5
        AR = 144 * 256
        packt = sb("packt", [128, PN])
        constt = sb("constt", [128, CN])
        maskt = sb("maskt", [128, LEVELS * 384 + 512], U8)
        small = sb("small", [128, 820])
        ring = sb("ring", [128, NRING * SLAB])
        arena = sb("arena", [128, AR])
        banks = [ctx.enter_context(nc.psum_tensor(f"bank{i}", [128, 512], F32)) for i in range(8)]

        PE, AC, DV, PL, SP = (Engine(sem(n)) for n in ("s_pe", "s_act", "s_dve", "s_pool", "s_sp"))

        def pk(name):
            a, n = PO[name]
            return packt[:, a:a + n]

        def cn(name):
            a, n = CO[name]
            return constt[:, a:a + n]

        small_at = [0]

        def tiny(n):
            a = small_at[0]
            small_at[0] += n
            assert small_at[0] <= 820
            return small[:, a:a + n]

        def region(kb, *dims):
            n = int(np.prod(dims))
            a = int(kb * 256)
            assert a + n <= AR, (kb, dims)
            v = arena[:, a:a + n]
            names = "abcd"[:len(dims)]
            if len(dims) > 1:
                v = v.rearrange(f"p ({' '.join(names)}) -> p {' '.join(names)}",
                                **{names[i]: dims[i] for i in range(len(dims))})
            return v

        ident = cn("ident")
        ones = cn("ones")

        pool = deque((i, []) for i in range(8))

        def bank():
            i, readers = pool.popleft()
            return i, banks[i], readers

        def free(i, *readers):
            pool.append((i, list(readers)))

        slots = deque()
        for i in range(NRING):
            slots.append((ring[:, i * SLAB:(i + 1) * SLAB], sem(f"s_w{i}"), 0, []))
        pending = deque(slab_order())
        landed, extra = {}, []

        def refill():
            while slots and pending:
                place, s, used, readers = slots.popleft()
                name, n = pending.popleft()
                t = SP.load(place, w[name][n], s, 16 * (used + 1), readers)
                landed[(name, n)] = (place, t, s, used + 1)

        def add_slot(view, *readers):
            s = sem(f"s_x{len(extra)}")
            extra.append(s)
            slots.append((view, s, 0, list(readers)))
            return s

        def slab(name, n, k):
            refill()
            place, t, s, used = landed[(name, n)]
            return place.rearrange("p (k n) -> p k n", k=k), t

        retired = []

        def done(name, n, reader):
            place, t, s, used = landed.pop((name, n))
            if retired and s is retired[0]:
                return
            slots.append((place, s, used, [reader]))
            refill()

        def mm(dst, pairs, *producers):
            PE.wait(producers)
            last = len(pairs) - 1
            for j, (l, r) in enumerate(pairs):
                f = lambda e, l=l, r=r, j=j: e.matmul(dst, l, r, start=(j == 0), stop=(j == last))
                if j < last:
                    PE.quiet(f)
                else:
                    t = PE.run(f)
            return t

        def turn(dst, src, *producers):
            return PE.run(lambda e: e.transpose(dst, src, ident), *producers)

        def act(dst, src, func, *producers, bias=0.0, scale=1.0, accum=None):
            if accum is None:
                return AC.run(lambda e: e.activation(dst, src, func, bias=bias, scale=scale), *producers)
            return AC.run(lambda e: e.activation(dst, src, func, bias=bias, scale=scale, accum_out=accum),
                          *producers)

        def copy(eng, dst, src, *producers):
            if eng is AC:
                return act(dst, src, ACT.Copy, *producers)
            return eng.run(lambda e: e.tensor_copy(dst, src), *producers)

        def tt(eng, dst, a, b, op, *producers):
            return eng.run(lambda e: e.tensor_tensor(dst, a, b, op), *producers)

        def ts(eng, dst, a, s1, s2, op0, op1, *producers):
            if op1 is None:
                return eng.run(lambda e: e.tensor_scalar(dst, a, s1, None, op0), *producers)
            return eng.run(lambda e: e.tensor_scalar(dst, a, s1, s2, op0, op1), *producers)

        def stt(dst, a, s, b, op0, op1, *producers):
            return DV.run(lambda e: e.scalar_tensor_tensor(dst, a, s, b, op0, op1), *producers)

        def rsq(dst, src, scale, eps, *producers):
            a = ts(DV, dst, src, scale, eps, ALU.mult, ALU.add, *producers)
            b = act(dst, dst, ACT.Sqrt, a)
            c = DV.run(lambda e: e.reciprocal(dst, dst), b)
            return a, c

        MUL, ADD, SUB = ALU.mult, ALU.add, ALU.subtract

        X = region(0, 8, 256)
        C = region(8, 8, 256)
        HX = region(16, 8, 512)
        TH = region(32, 16, 256)
        BI = region(48, 64, 64)
        V = region(64, 4, 512)
        QT = region(72, 4, 256)
        KT = region(76, 4, 512)
        QN = region(84, 4, 512)
        FT = region(92, 4, 256)
        O = region(92, 2, 512)
        YF = region(96, 4, 256)
        YA = region(100, 4, 256)
        P = region(104, 3, 512)
        PT = region(110, 3, 512)
        UC = region(104, 2, 4, 256)
        CQ = region(116, 2, 64)
        SQ = region(116.5, 2, 64)
        CK = region(117, 2, 64)
        SK = region(117.5, 2, 64)
        RS = region(118, 512)
        SQR = region(32, 8, 512)

        t_pack = AC.load(packt[:, :], pack, sem("s_pack"), 16)
        t_x = AC.load(X, xT, sem("s_x"), 16)
        t_c = AC.load(C, cT, sem("s_c"), 16)
        t_const = AC.load(constt[:, :], const, sem("s_const"), 16)
        MF = region(120, LEVELS * 384 + 512)
        t_mask = AC.load(MF, masks, sem("s_mask"), 16)
        refill()

        cwide = region(134.5, 256)
        c2v = cwide.rearrange("p (k m) -> p k m", k=8)
        t_c2 = PL.run(lambda e: e.memset(cwide, 0.0))
        c2 = tiny(16)
        a = act(c2, pk("c2"), ACT.Tanh, t_pack, scale=0.5)
        a = ts(DV, c2, c2, 0.5, 0.5, MUL, ADD, a)
        t_c2 = tt(DV, c2v[:, :, 0:2], c2.rearrange("p (k b) -> p k b", k=8),
                  pk("c2").rearrange("p (k b) -> p k b", k=8), MUL, a, t_c2)

        mod = tiny(96).rearrange("p (m b) -> p m b", m=48)
        bada = pk("bada")
        MR = region(132.5, 512)

        def ada(part, kh, b, readers):
            wv = [slab("ada", 8 * part + 4 * kh + q, 4) for q in range(4)]
            for k in range(4):
                for q in range(4):
                    f = lambda e, k=k, q=q: e.matmul(b[32 * q:32 * q + 32, :], c2v[:, 4 * kh + k, :], wv[q][0][:, k, :],
                                                     start=(kh == 0 and k == 0), stop=(kh == 1 and k == 3),
                                                     tile_position=(0, 32 * q))
                    last = PE.run(f, wv[q][1], t_c2, readers) if k == 3 or k == 0 else PE.quiet(f)
                    if k == 3:
                        done("ada", 8 * part + 4 * kh + q, last)
            return last

        def ada_end(part, i, b, last, mr_free):
            e = copy(AC, MR, b[:, :], last, mr_free)
            free(i, e)
            i, b, rd = bank()
            for j in range(4):
                t = turn(b[:, j * 128:(j + 1) * 128], MR[:, j * 128:(j + 1) * 128], e, rd, t_const)
            m = tt(DV, mod[:, 16 * part:16 * part + 16, :].rearrange("p (q j) b -> p q j b", q=4),
                   b[:, :].rearrange("p (j q m) -> p q j m", j=4, q=4)[:, :, :, 0:2],
                   bada[:, 16 * part:16 * part + 16].rearrange("p (q j) -> p q j", q=4).unsqueeze(3)
                   .to_broadcast([128, 4, 4, 2]), ADD, t)
            free(i, m)
            return t, m

        sa = act(SQR[:, :, 0:256], X, ACT.Square, t_x)
        sc = act(SQR[:, :, 256:512], C, ACT.Square, t_c)
        bi, b, rd = bank()
        t = mm(b[:, :], [(ones, SQR[:, k, :]) for k in range(8)], sa, sc, t_const, rd)
        fr, t_rs = rsq(RS, b[:, :], 1.0 / 1024, 1e-6, t)
        free(bi, fr)
        t_bias = AC.load(region(48, 4096), bias, sem("s_bias"), 16)
        xn0 = tt(DV, HX[:, :, 0:256], X, RS[:, 0:256].unsqueeze(1).to_broadcast([128, 8, 256]), MUL, t_rs, t_x)
        xn1 = tt(DV, HX[:, :, 256:512], C, RS[:, 256:512].unsqueeze(1).to_broadcast([128, 8, 256]), MUL, t_rs, t_c)

        ai, ab, ard = bank()
        ada(0, 0, ab, ard)
        t_mr, t = ada_end(0, ai, ab, ada(0, 1, ab, ard), None)
        gs1 = tiny(16).rearrange("p (m b) -> p m b", m=8)
        t = stt(gs1, mod[:, 8:16, :], 1.0, pk("n1").unsqueeze(2).to_broadcast([128, 8, 2]), ADD, MUL, t)
        t_h = [None] * 8
        for k in range(8):
            u = ts(DV, HX[:, k, 0:256], HX[:, k, 0:256], gs1[:, k, 0:1], mod[:, k, 0:1], MUL, ADD, t, xn0)
            v = act(HX[:, k, 256:512], HX[:, k, 256:512], ACT.Identity, t, xn1,
                    scale=gs1[:, k, 1:2], bias=mod[:, k, 1:2])
            t_h[k] = [u, v]

        qg, kg = pk("qg"), pk("kg")

        def tables(g, dc, ds, scale):
            gg = tiny(64)
            a = ts(PL, gg, g, scale, 0.0, MUL, ADD, t_pack)
            o = []
            for i in range(2):
                cs = cn("cos").rearrange("p (i d) -> p i d", i=2)[:, i, :]
                sn = cn("sin").rearrange("p (i d) -> p i d", i=2)[:, i, :]
                o.append(tt(PL, dc[:, i, :], cs, gg, MUL, a, t_const))
                for x in range(2):
                    for half in range(2):
                        d, f = 32 * x + 16 * half, 32 * x + 16 * (1 - half)
                        o.append(tt(PL, ds[:, i, d:d + 16], sn[:, d:d + 16], gg[:, f:f + 16], MUL, a, t_const))
            return o

        t_tq = tables(qg, CQ, SQ, 0.125)
        t_tk = tables(kg, CK, SK, 1.0)
        t_mask = PL.run(lambda e: e.tensor_copy(maskt[:, :], MF), t_mask)
        lent = add_slot(arena[:, 120 * 256:128 * 256], t_mask)
        t_bm = tt(PL, BI, BI, cn("amask").unsqueeze(1).to_broadcast([128, 64, 64]), ADD, t_bias, t_const)

        QNR = region(32, 6, 512)
        m_free = [None] * 4

        def rows(names, tiles):
            got = [bank() for _ in tiles]
            for h, n in enumerate(names):
                wv, t = slab("win", n, 8)
                for ti, tl in enumerate(tiles):
                    i, b, rd = got[ti]
                    last = mm(b[:, h * 256:(h + 1) * 256],
                              [(HX[:, k, tl * 128:(tl + 1) * 128], wv[:, k, :]) for k in range(8)],
                              t, t_h, rd)
                    got[ti] = (i, b, last)
                done("win", n, last)
            return got

        rstd = tiny(8 * 6).rearrange("p (i h) -> p i h", i=6)
        t_turned = {}
        normed = []

        def norm_rope(kind, tl, i, b, t):
            z = len(normed)
            n = QNR[:, z, :]
            m = QN[:, z % 4, :]
            bv = b[:, :].rearrange("p (h d) -> p h d", h=8)
            nv = n.rearrange("p (h d) -> p h d", h=8)
            mv = m.rearrange("p (h d) -> p h d", h=8)
            r = rstd[:, z, :]
            a = act(n, b[:, :], ACT.Square, t)
            a = DV.run(lambda e: e.tensor_reduce(r, nv, AX.X, ADD), a)
            _, a = rsq(r, r, 1.0 / 64, 1e-6, a)
            a = tt(DV, nv, bv, r.unsqueeze(2).to_broadcast([128, 8, 64]), MUL, a)
            free(i, a)
            if kind == "c":
                a = tt(PL, nv, nv, kg.unsqueeze(1).to_broadcast([128, 8, 64]), MUL, a)
            else:
                cs, sn, tabs = (CQ, SQ, t_tq) if kind == "q" else (CK, SK, t_tk)
                o = []
                for x in range(2):
                    for half in range(2):
                        d, f = 32 * x + 16 * half, 32 * x + 16 * (1 - half)
                        o.append(tt(DV, mv[:, :, d:d + 16], nv[:, :, f:f + 16],
                                    sn[:, tl, d:d + 16].unsqueeze(1).to_broadcast([128, 8, 16]), MUL, a, tabs,
                                    m_free[z % 4]))
                c = tt(PL, nv, nv, cs[:, tl, :].unsqueeze(1).to_broadcast([128, 8, 64]), MUL, o, a, tabs)
                a = tt(PL, n, n, m, ADD, c, o)
                m_free[z % 4] = a
            normed.append((kind, tl, n, a))

        def turn_rows(kind, tl, n, a):
            j, p, rd = bank()
            for c in range(4):
                t = turn(p[:, c * 128:(c + 1) * 128], n[:, c * 128:(c + 1) * 128], a, rd)
            at = tl + (2 if kind == "c" else 0)
            dst = (QT if kind == "q" else KT)[:, :, at * 128:(at + 1) * 128]
            e = copy(AC, dst, p[:, :].rearrange("p (c t) -> p c t", c=4), t)
            free(j, e)
            t_turned[(kind, tl)] = e

        got = rows((4, 5), (0, 1, 2, 3))
        gq = rows((2, 3), (0, 1))
        for tl in range(4):
            norm_rope("k" if tl < 2 else "c", tl % 2, *got[tl])
        for tl in range(2):
            norm_rope("q", tl, *gq[tl])
        got = rows((6, 7), (0, 1, 2, 3))
        t_v = []
        for tl in range(4):
            i, b, t = got[tl]
            e = copy(AC, V[:, tl, :], b[:, :], t)
            free(i, e)
            t_v.append(e)

        t_f = []
        for n in range(2):
            wv, t = slab("win", n, 8)
            i, b, rd = bank()
            for j in range(2):
                last = mm(b[:, j * 256:(j + 1) * 256],
                          [(wv[:, k, j * 128:(j + 1) * 128], HX[:, k, 0:256]) for k in range(8)], t, t_h, rd)
            done("win", n, last)
            e = copy(AC, FT[:, 2 * n:2 * n + 2, :], b[:, :].rearrange("p (j t) -> p j t", j=2), last)
            free(i, e)
            t_f.append(e)
        for z in normed:
            turn_rows(*z)

        dc = cn("dftc")
        dn = cn("dftn").rearrange("p (s m t) -> p s m t", s=2, m=2)
        t_u = []
        for m in range(2):
            for g2 in range(2):
                i, b, rd = bank()
                for j in range(2):
                    t = mm(b[:, j * 256:(j + 1) * 256], [(FT[:, 2 * g2 + j, m * 128:(m + 1) * 128], dc)],
                           t_f[g2], t_const, rd)
                e = copy(DV, UC[:, m, 2 * g2:2 * g2 + 2, :], b[:, :].rearrange("p (j t) -> p j t", j=2), t)
                free(i, e)
                t_u.append(e)
        t_yf = []
        for g2 in range(2):
            i, b, rd = bank()
            for j in range(2):
                g = 2 * g2 + j
                t = mm(b[:, j * 256:(j + 1) * 256],
                       [(UC[:, m, g, s * 128:(s + 1) * 128], dn[:, s, m, :]) for m in range(2) for s in range(2)],
                       t_u, rd)
            e = copy(DV, YF[:, 2 * g2:2 * g2 + 2, :], b[:, :].rearrange("p (j t) -> p j t", j=2), t)
            free(i, e)
            t_yf.append(e)
        t_uc_read = t

        t_th = [None] * 8

        def gate_step(s):
            wv, t = slab("gate", s, 8)
            i, b, rd = bank()
            for j in range(2):
                last = mm(b[:, j * 256:(j + 1) * 256],
                          [(wv[:, k, j * 128:(j + 1) * 128], HX[:, k, 0:256]) for k in range(8)], t, t_h, rd)
            done("gate", s, last)
            e = act(TH[:, 2 * s:2 * s + 2, :], b[:, :].rearrange("p (j t) -> p j t", j=2), ACT.Tanh, last, scale=0.5)
            free(i, e)
            t_th[s] = ts(PL, TH[:, 2 * s:2 * s + 2, :], TH[:, 2 * s:2 * s + 2, :], 0.5, 0.5, MUL, ADD, e)

        late = {"free": t_mr, "mod": []}

        def ada_step(part, kh):
            if kh == 0:
                late["bank"] = bank()
            i, b, rd = late["bank"]
            last = ada(part, kh, b, rd)
            if kh:
                late["free"], m = ada_end(part, i, b, last, late["free"])
                late["mod"].append(m)

        filler = deque()
        for s in range(4):
            filler.append(lambda s=s: gate_step(2 * s))
            filler.append(lambda s=s: gate_step(2 * s + 1))
            filler.append(lambda s=s: ada_step(1 + s // 2, s % 2))

        stat = tiny(3 * 16 * 2).rearrange("p (a u) -> p a u", a=3)
        units = [(h, qt) for h in range(8) for qt in range(2)]
        t_o = [[], []]
        o_last = {}
        BIv = region(48, 16, 256)
        p_free = [t_uc_read] * 3
        pt_free = [t_uc_read] * 3
        held = {}

        def att_scores(u):
            h, qt = units[u]
            c, r0 = h // 2, 64 * (h % 2)
            i, b, rd = bank()
            q = QT[r0:r0 + 64, c, qt * 128:(qt + 1) * 128]
            t = mm(b[:, :], [(q, KT[r0:r0 + 64, c, :])], list(t_turned.values()), rd)
            t = tt(DV, b[:, 0:256], b[:, 0:256], BIv[:, 2 * h + qt, :], ADD, t, t_bm)
            t = DV.run(lambda e: e.tensor_reduce(stat[:, 0, u:u + 1], b[:, :], AX.X, ALU.max, negate=True), t)
            t = act(P[:, u % 3, :], b[:, :], ACT.Exp, t, p_free[u % 3], bias=stat[:, 0, u:u + 1],
                    accum=stat[:, 1, u:u + 1])
            free(i, t)
            t2 = DV.run(lambda e: e.reciprocal(stat[:, 2, u:u + 1], stat[:, 1, u:u + 1]), t)
            held[u] = (t, t2)

        def att_turn(u):
            t, t2 = held[u]
            i, b, rd = bank()
            for j in range(4):
                x = turn(b[:, j * 128:(j + 1) * 128], P[:, u % 3, j * 128:(j + 1) * 128], t, rd)
            p_free[u % 3] = x
            e = copy(AC if u % 2 else DV, PT[:, u % 3, :], b[:, :], x, pt_free[u % 3])
            free(i, e)
            held[u] = (e, t2)

        def att_out(u):
            h, qt = units[u]
            e, t2 = held.pop(u)
            i, b, rd = bank()
            x = mm(b[:, 0:64],
                   [(PT[:, u % 3, j * 128:(j + 1) * 128], V[:, j, h * 64:(h + 1) * 64]) for j in range(4)],
                   e, t_v, rd)
            pt_free[u % 3] = x
            t_o[qt].append(ts(DV, O[:, qt, h * 64:(h + 1) * 64], b[:, 0:64],
                              stat[:, 2, u:u + 1], None, MUL, None, x, t2, t_u))
            free(i, t_o[qt][-1])

        for u in range(18):
            if u < 16:
                att_scores(u)
            if filler:
                filler.popleft()()
            if 0 <= u - 1 < 16:
                att_turn(u - 1)
            if 0 <= u - 2 < 16:
                att_out(u - 2)
        while filler:
            filler.popleft()()
        t_mod = late["mod"]
        gs2 = tiny(8)
        t_mod = t_mod + [stt(gs2, mod[:, 32:40, 0], 1.0, pk("n2"), ADD, MUL, t_mod)]
        t_ya = []
        for qt in range(2):
            i, b, rd = bank()
            for c in range(4):
                t = turn(b[:, c * 128:(c + 1) * 128], O[:, qt, c * 128:(c + 1) * 128], t_o[qt], rd)
            e = copy(AC, YA[:, :, qt * 128:(qt + 1) * 128], b[:, :].rearrange("p (c t) -> p c t", c=4), t)
            free(i, e)
            t_ya.append(e)

        MG = C
        M2 = region(84, 4, 512)
        t_mg = [None] * 4
        part = {}
        for name, Y, ty, g0 in (("fo", YF, t_yf, 0), ("ao", YA, t_ya, 8)):
            for s in range(2):
                wv, t = slab(name, s, 4)
                for c2_ in range(2):
                    n = 2 * s + c2_
                    i, b, rd = bank()
                    for j in range(2):
                        col = (2 * c2_ + j) * 128
                        last = mm(b[:, j * 256:(j + 1) * 256], [(wv[:, k, col:col + 128], Y[:, k, :]) for k in range(4)],
                                  t, ty, rd)
                    bv = b[:, :].rearrange("p (j t) -> p j t", j=2)
                    if name == "fo":
                        part[n] = tt(DV, MG[:, 2 * n:2 * n + 2, :], bv, TH[:, 2 * n:2 * n + 2, :], MUL,
                                     last, t_th[n], xn1)
                        free(i, part[n])
                    else:
                        m = M2[:, n, :].rearrange("p (j t) -> p j t", j=2)
                        e = tt(DV, m, bv, TH[:, 8 + 2 * n:10 + 2 * n, :], MUL, last, t_th[4 + n], m_free)
                        free(i, e)
                        t_mg[n] = tt(PL, MG[:, 2 * n:2 * n + 2, :], MG[:, 2 * n:2 * n + 2, :], m, ADD, e, part[n])
                done(name, s, last)

        MEM = region(24, 8, 256)
        t_mem = SP.load(MEM, memT, sem("s_mem"), 16, last)
        t_x1 = [None] * 8
        for s in range(4):
            wv, t = slab("wo", s, 8)
            i, b, rd = bank()
            for j in range(2):
                last = mm(b[:, j * 256:(j + 1) * 256],
                          [(wv[:, k, j * 128:(j + 1) * 128], MG[:, k, :]) for k in range(8)], t, t_mg, rd)
            done("wo", s, last)
            o = []
            for j in range(2):
                c = 2 * s + j
                t_x1[c] = stt(X[:, c, :], b[:, j * 256:(j + 1) * 256], mod[:, 16 + c, 0:1], X[:, c, :], MUL, ADD,
                              last, t_mod)
                o.append(t_x1[c])
            free(i, *o)

        def norm(src, producers, sq, rs, *sq_free):
            t = [act(sq[:, k, :], src[:, k, :], ACT.Square, producers[k], *sq_free) for k in range(8)]
            i, b, rd = bank()
            t = mm(b[:, 0:256], [(ones, sq[:, k, :]) for k in range(8)], t, rd)
            fr, t = rsq(rs, b[:, 0:256], 1.0 / 1024, 1e-6, t)
            free(i, fr)
            return t

        SQ2 = region(8, 8, 256)
        RS2 = region(118, 256)
        RS3 = region(119, 256)
        H = region(16, 8, 256)
        t_rm = norm(MEM, [t_mem] * 8, SQ2, RS3, last)
        t_m = []
        for k in range(8):
            t_m.append(stt(MEM[:, k, :], MEM[:, k, :], pk("nmem")[:, k:k + 1], RS3, MUL, MUL, t_rm))
        t_r2 = norm(X, t_x1, SQ2, RS2, t_rm)
        KH = region(64, 2, 256)
        VH = region(66, 2, 256)
        wv, t = slab("mk", 0, 8)
        i, b, rd = bank()
        for j in range(2):
            last = mm(b[:, j * 256:(j + 1) * 256], [(wv[:, k, j * 128:(j + 1) * 128], MEM[:, k, :]) for k in range(8)],
                      t, t_m, rd)
        done("mk", 0, last)
        t_kh = copy(AC, KH, b[:, :].rearrange("p (j t) -> p j t", j=2), last)
        free(i, t_kh)
        wv, t = slab("mv", 0, 8)
        i, b, rd = bank()
        for j in range(2):
            last = mm(b[:, j * 256:(j + 1) * 256], [(MEM[:, k, j * 128:(j + 1) * 128], wv[:, k, :]) for k in range(8)],
                      t, t_m, rd)
        done("mv", 0, last)
        t_vh = copy(AC, VH, b[:, :].rearrange("p (j t) -> p j t", j=2), last)
        free(i, t_vh)

        t_h2 = []
        for k in range(8):
            a = tt(DV, H[:, k, :], X[:, k, :], RS2, MUL, t_r2, t_x1[k])
            t_h2.append(ts(DV, H[:, k, :], H[:, k, :], gs2[:, k:k + 1], mod[:, 24 + k, 0:1], MUL, ADD, a, t_mod))

        A = region(32, 32, 256)
        t_a = [None] * 16
        for s in range(16):
            wv, t = slab("m1", s, 8)
            i, b, rd = bank()
            for j in range(2):
                last = mm(b[:, j * 256:(j + 1) * 256],
                          [(wv[:, k, j * 128:(j + 1) * 128], H[:, k, :]) for k in range(8)], t, t_h2, rd)
            done("m1", s, last)
            av = A[:, 2 * s:2 * s + 2, :]
            bv = b[:, :].rearrange("p (j t) -> p j t", j=2)
            e = act(av, bv, ACT.Relu, last)
            t_a[s] = tt(DV, av, av, bv, MUL, e)
            free(i, t_a[s])
        for s in range(16):
            wv, t = slab("m2", s, 16)
            if s % 2 == 0:
                i, b, rd = bank()
            c = s // 2
            PE.wait([t, rd] + t_a)
            for k in range(16):
                f = lambda e, k=k, b=b, wv=wv, s=s: e.matmul(b[:, 0:256], wv[:, k, :], A[:, 16 * (s % 2) + k, :],
                                                             start=(s % 2 == 0 and k == 0), stop=(s % 2 == 1 and k == 15))
                if k < 15:
                    PE.quiet(f)
                else:
                    last = PE.run(f)
            done("m2", s, last)
            if s % 2:
                t_x1[c] = stt(X[:, c, :], b[:, 0:256], mod[:, 40 + c, 0:1], X[:, c, :], MUL, ADD, last, t_mod)
                free(i, t_x1[c])
        t_x2 = t_x1
        t_mlp = last

        t_r = norm(X, t_x2, SQ2, RS2)
        t_h = [stt(H[:, k, :], X[:, k, :], pk("nmix")[:, k:k + 1], RS2, MUL, MUL, t_r) for k in range(8)]

        MIX = region(8, 8, 256)
        PF = region(24, 12, 256)
        VAL = region(68, 3, 256)
        GA = region(71, 3, 256)
        U = region(136, 3, 288)
        CA = region(139.5, 3, 256)
        CSQ = region(10, 3, 256)
        RAW = region(83.5, 4, 258)
        QH = region(88, 2, 256)
        P2 = region(90, 2, 512)
        PT2 = region(94, 2, 512)
        CM = region(142.5, 256)
        CR = region(33, 256)

        zz = [PL.run(lambda e: e.memset(U[:, :, 0:15], 0.0), t_mlp),
              PL.run(lambda e: e.memset(U[:, :, 271:288], 0.0), t_mlp),
              PL.run(lambda e: e.memset(RAW[:, :, 0:1], 0.0), t_mlp),
              PL.run(lambda e: e.memset(RAW[:, :, 257:258], 0.0), t_mlp)]
        smu = pk("smu").rearrange("p (a c) -> p a c", a=2)
        c0 = tiny(12)
        a = tt(PL, c0, smu[:, 0, :], smu[:, 1, :], ADD, t_pack)
        t_c0 = ts(PL, c0, c0, -1.0, 1.0, MUL, ADD, a)
        raw_free = [None] * 4
        t_pf = [None] * 12
        t_val = [None] * 3
        t_ga = [None] * 3
        t_q2 = [None] * 2

        def in_step(s):
            wv, t = slab("win2", s, 8)
            i, b, rd = bank()
            o = []
            for j in range(2):
                last = mm(b[:, j * 256:(j + 1) * 256],
                          [(wv[:, k, j * 128:(j + 1) * 128], H[:, k, :]) for k in range(8)], t, t_h, rd)
            done("win2", s, last)
            for j in range(2):
                c = 2 * s + j
                bv = b[:, j * 256:(j + 1) * 256]
                if c < 2:
                    t_q2[c] = copy(AC, QH[:, c, :], bv, last)
                    o.append(t_q2[c])
                elif c < 5:
                    t_val[c - 2] = copy(AC, VAL[:, c - 2, :], bv, last, t_mlp)
                    o.append(t_val[c - 2])
                elif c < 8:
                    t_ga[c - 5] = act(GA[:, c - 5, :], bv, ACT.Tanh, last, t_mlp, scale=0.5)
                    o.append(t_ga[c - 5])
                else:
                    c -= 8
                    r = RAW[:, c % 4, :]
                    e = copy(AC, r[:, 1:257], bv, last, raw_free[c % 4])
                    x = act(PF[:, c, :], bv, ACT.Copy, last, t_c0, t_mlp, scale=c0[:, c:c + 1])
                    o += [e, x]
                    x = stt(PF[:, c, :], r[:, 0:256], smu[:, 0, c:c + 1], PF[:, c, :], MUL, ADD, e, x, zz)
                    t_pf[c] = stt(PF[:, c, :], r[:, 2:258], smu[:, 1, c:c + 1], PF[:, c, :], MUL, ADD, x)
                    raw_free[c % 4] = t_pf[c]
            free(i, *o)

        retired.append(lent)
        for s in WIN2:
            in_step(s)
        cw = pk("convw").rearrange("p (c k) -> p c k", c=3)
        t_cv = [None] * 3
        t_u3 = []

        def conv_start():
            for c in range(3):
                a = ts(DV, GA[:, c, :], GA[:, c, :], 0.5, 0.5, MUL, ADD, t_ga[c])
                a = tt(DV, U[:, c, 15:271], VAL[:, c, :], GA[:, c, :], MUL, a, t_val[c])
                t_u3.append(a)
                t_cv[c] = ts(DV, CA[:, c, :], U[:, c, 0:256], cw[:, c, 0:1], pk("convb")[:, c:c + 1], MUL, ADD, a, zz)

        def conv_taps():
            for k in range(1, 31):
                for c in range(3):
                    t_cv[c] = stt(CA[:, c, :], U[:, c, k:k + 256], cw[:, c, k:k + 1], CA[:, c, :], MUL, ADD, t_cv[c])
                if k % 2 == 0:
                    yield

        O2S = region(106, 2, 256)
        s2 = tiny(32).rearrange("p (a h q) -> p a h q", a=4, h=4)
        t_o2 = []
        pf2, ptf2 = [None, None], [None, None]

        def mem_head(h):
            c, r0 = h // 2, 64 * (h % 2)
            i, b, rd = bank()
            bv = b[:, :].rearrange("p (q m) -> p q m", q=2)
            for q in range(2):
                t = mm(bv[:, q, :], [(QH[r0:r0 + 64, c, q * 128:(q + 1) * 128], KH[r0:r0 + 64, c, :])],
                       t_q2, t_kh, rd)
            m = s2[:, 0, h, :]
            a = DV.run(lambda e: e.tensor_reduce(m, bv, AX.X, ALU.max), t)
            a = ts(DV, s2[:, 1, h, :], m, -0.125, None, MUL, None, a)
            pv = P2[:, h % 2, :].rearrange("p (q m) -> p q m", q=2)
            x = [act(pv[:, q, :], bv[:, q, :], ACT.Exp, a, pf2[h % 2], scale=0.125, bias=s2[:, 1, h, q:q + 1],
                     accum=s2[:, 2, h, q:q + 1]) for q in range(2)]
            free(i, *x)
            r = DV.run(lambda e: e.reciprocal(s2[:, 3, h, :], s2[:, 2, h, :]), x)
            i, b, rd = bank()
            for j in range(4):
                t = turn(b[:, j * 128:(j + 1) * 128], P2[:, h % 2, j * 128:(j + 1) * 128], x, rd)
            pf2[h % 2] = t
            e = copy(AC, PT2[:, h % 2, :], b[:, :], t, ptf2[h % 2])
            free(i, e)
            i, b, rd = bank()
            for q in range(2):
                t = mm(b[:, q * 64:(q + 1) * 64],
                       [(PT2[:, h % 2, (2 * q + m) * 128:(2 * q + m + 1) * 128], VH[:, m, h * 64:(h + 1) * 64])
                        for m in range(2)], e, t_vh, rd)
            t_o2.append(tt(DV, O2S[:, :, h * 64:(h + 1) * 64], b[:, 0:128].rearrange("p (q d) -> p q d", q=2),
                           s2[:, 3, h, :].unsqueeze(2).to_broadcast([128, 2, 64]), MUL, t, r))
            free(i, t_o2[-1])
            ptf2[h % 2] = t

        def mem_end():
            i, b, rd = bank()
            for q in range(2):
                for c in range(2):
                    t = turn(b[:, (c * 2 + q) * 128:(c * 2 + q + 1) * 128], O2S[:, q, c * 128:(c + 1) * 128], t_o2, rd)
            e = copy(AC, MIX[:, 0:2, :], b[:, :].rearrange("p (c t) -> p c t", c=2), t)
            free(i, e)
            return e

        KK = region(36, 3, 256)
        RRK = region(39, 3, 256)
        AA = region(42, 3, 256)
        LW = region(45, 3, 256)
        X1 = region(48, 3, 256)
        RHS = [region(51 + 1.5 * d, 384) for d in range(2)]
        KD = [region(54 + 3 * d, 3, 256) for d in range(2)]
        SA = [region(60 + 1.5 * d, 384) for d in range(2)]
        VV = [region(100 + 3 * d, 6, 128) for d in range(2)]
        Y = region(106, 2, 384)
        KR = [region(109 + 12 * d, 6, 2, 128) for d in range(2)]
        BG = [region(115 + 12 * d, 6, 2, 128) for d in range(2)]
        VN = region(133, 2, 384)
        BGN = [region(16 + 3 * d, 2, 384) for d in range(2)]
        ST = [region((22, 42)[d], 3, 128) for d in range(2)]
        G = region(36, 2, 384)
        XX = [region(64 + 18 * d, 6, 2, 128) for d in range(2)]
        LN = [region(70 + 18 * d, 6, 2, 128) for d in range(2)]
        MQ = [region(76 + 18 * d, 6, 2, 128) for d in range(2)]

        def tiles(v):
            return v.rearrange("p c (i t) -> p (c i) t", i=2)

        hw = tiny(12)
        t_hw = [ts(PL, hw[:, 0:6], pk("dw0"), 0.5, 0.0, MUL, ADD, t_pack),
                ts(PL, hw[:, 6:12], pk("ia0"), 0.5, 0.0, MUL, ADD, t_pack)]
        omka = tiny(3)
        t_ka = ts(PL, omka, pk("ka"), -1.0, 1.0, MUL, ADD, t_pack)

        t_kk = []
        RSK = [X1[:, c, :] for c in range(3)]
        for c in range(3):
            a = ts(DV, KK[:, c, :], PF[:, 3 + c, :], pk("kk")[:, c:c + 1], None, MUL, None, t_pf[3 + c], t_mlp)
            s = act(LW[:, c, :], KK[:, c, :], ACT.Square, a)
            i, b, rd = bank()
            t = mm(b[:, 0:256], [(cn("blk"), LW[:, c, :])], s, rd)
            fr, r = rsq(RSK[c], b[:, 0:256], 1.0, 1e-12, t)
            free(i, fr)
            t_kk.append(tt(DV, KK[:, c, :], KK[:, c, :], RSK[c], MUL, r))
        t_rrk = [ts(DV, RRK[:, c, :], PF[:, c, :], pk("rk")[:, c:c + 1], None, MUL, None, t_pf[c]) for c in range(3)]
        t_wd = act(PF[:, 9, :], PF[:, 9, :], ACT.Tanh, t_pf[9])
        a = act(PF[:, 11, :], PF[:, 11, :], ACT.Tanh, t_pf[11], scale=0.5)
        t_sg = ts(PL, PF[:, 11, :], PF[:, 11, :], 0.5, 0.5, MUL, ADD, a)

        t_vn = []
        for m in range(2):
            i, b, rd = bank()
            for c in range(3):
                t = turn(b[:, c * 128:(c + 1) * 128], PF[:, 6 + c, m * 128:(m + 1) * 128], t_pf[6 + c], rd)
            e = copy(AC, VN[:, m, :], b[:, 0:384], t)
            free(i, e)
            t_vn.append(e)

        es = tiny(6).rearrange("p (d c) -> p d c", d=2)
        ht = tiny(12).rearrange("p (d c i) -> p d c i", d=2, c=3)
        t_es, t_kr, t_bg, t_kd, t_bgn = [None] * 2, [None] * 2, [None] * 2, [None] * 2, [None] * 2
        lw_free, aa_free, x1_free = [None], [None], [t_kk]

        def up(name, src, d, dst, bias, *producers):
            o = []
            for c in range(3):
                i, b, rd = bank()
                t = mm(b[:, 0:256], [(pk(name)[64 * d:64 * d + 64, c * 128:(c + 1) * 128], src[64 * d:64 * d + 64, :])],
                       rd, *producers[:1])
                e = act(dst[:, c, :], b[:, 0:256], ACT.Tanh, t, t_hw, *producers[1:], scale=0.5,
                        bias=bias[:, 3 * d + c:3 * d + c + 1])
                free(i, e)
                o.append(e)
            return o

        aa_free[0] = [t_mask]
        for d in range(2):
            t = up("dup", PF[:, 9, :], d, LW, hw[:, 0:6], t_wd, lw_free[0], t_kk)
            u = up("iup", PF[:, 10, :], d, AA, hw[:, 6:12], t_pf[10], aa_free[0])
            t = ts(DV, LW, LW, -0.5 * DECAY, -0.5 * DECAY, MUL, ADD, t)
            sc = [DV.run(lambda e, c=c, m=m: e.tensor_tensor_scan(
                X1[:, c, m * 128:(m + 1) * 128], ones, LW[:, c, m * 128:(m + 1) * 128], 0.0, MUL, ADD),
                t, x1_free[0], t_const) for c in range(3) for m in range(2)]
            hd = ht[:, d, :, :].rearrange("p c i -> p (c i)")
            h = ts(DV, hd, tiles(X1)[:, :, 127], 0.5, None, MUL, None, sc)
            x1 = tt(DV, tiles(X1), tiles(X1), hd.unsqueeze(2).to_broadcast([128, 6, 128]), SUB, h)
            x2 = tt(DV, LW, X1, LW, SUB, x1)
            a = tt(DV, es[:, d, :], ht[:, d, :, 0], ht[:, d, :, 1], ADD, h)
            x1v, x2v = tiles(X1), tiles(LW)
            if d == 0:
                e0 = act(KR[d][:, :, 0, :], x2v, ACT.Exp, x2, t_h)
                e1 = act(KR[d][:, :, 1, :], x1v, ACT.Exp, x1)
                e2 = act(BG[d][:, :, 1, :], x1v, ACT.Exp, x1, scale=-1.0)
            else:
                e0 = act(KR[d][:, :, 0, :], x1v, ACT.Exp, x1, scale=-1.0)
                e1 = act(KR[d][:, :, 1, :], x2v, ACT.Exp, x2, scale=-1.0)
                e2 = act(BG[d][:, :, 1, :], x2v, ACT.Exp, x2)
            lw_free[0], x1_free[0] = [e0, e1, e2], [e0, e1, e2]
            t_es[d] = act(es[:, d, :], es[:, d, :], ACT.Exp, a)
            u = ts(DV, AA, AA, 0.5, 0.5, MUL, ADD, u)
            k0 = [ts(DV, KD[d][:, c, :], AA[:, c, :], pk("ka")[:, c:c + 1], omka[:, c:c + 1], MUL, ADD, u, t_ka)
                  for c in range(3)]
            t_kd[d] = tt(PL, KD[d], KD[d], PF[:, 3:6, :], MUL, k0, t_pf[3:6])
            n = stt(AA, AA, -1.0, KK, MUL, MUL, k0, t_kk)
            a = tt(PL, KR[d][:, :, 0, :], KR[d][:, :, 0, :], tiles(KK), MUL, e0, t_kk)
            b_ = tt(PL, KR[d][:, :, 1, :], KR[d][:, :, 1, :], tiles(PF[:, 0:3, :]), MUL, e1, t_pf[0:3])
            t_kr[d] = [a, b_]
            a = tt(DV, BG[d][:, :, 0, :], tiles(AA), BG[d][:, :, 1, :], MUL, n, e2)
            aa_free[0] = a
            b_ = tt(DV, BG[d][:, :, 1, :], BG[d][:, :, 1, :], tiles(KD[d]), MUL, e2, t_kd[d], a)
            t_bg[d] = [a, b_]

        conv_start()
        for h in range(4):
            mem_head(h)
        t_mem2 = mem_end()

        for d in range(2):
            for y in range(2):
                i, b, rd = bank()
                for c in range(3):
                    t = turn(b[:, c * 128:(c + 1) * 128], BG[d][:, 2 * c + d, y, :], t_bg[d], rd)
                e = copy(AC, BGN[d][:, y, :], b[:, 0:384], t)
                free(i, e)
                t_bgn[d] = [e, t_bgn[d]] if y == 0 else [t_bgn[d][0], e]

        lm = maskt[:, 0:LEVELS * 384].rearrange("p (l m) -> p l m", l=LEVELS)
        si = maskt[:, LEVELS * 384:LEVELS * 384 + 512].rearrange("p (d m) -> p d m", d=2)
        t_zero = [None] * 2
        for d in range(2):
            t_zero[d] = [PL.run(lambda e, d=d: e.memset(LN[d], 0.0), t_u3, t_mem2, t_pf),
                         DV.run(lambda e, d=d: e.memset(MQ[d], 0.0), t_u3, t_mem2, t_pf)]
        set_free = [None, None]
        t_st = [None, None]
        y_done = [None, None]

        def flat(v):
            return v.rearrange("p a t -> p (a t)")

        def batch(d, m, second):
            x_, l_, q_ = XX[d], LN[d], MQ[d]
            init = DV.run(lambda e: e.tensor_copy(x_.rearrange("p u a t -> p (u a) t"),
                                                  ident.unsqueeze(1).to_broadcast([128, 12, 128])),
                          set_free[d], t_u3, t_mem2, t_pf, t_const)
            ready = [None] * 6
            for p in range(3):
                j, bq, rdq = bank()
                o = []
                tq = None
                for u in (2 * p, 2 * p + 1):
                    r0, idx = 64 * (u % 2), 2 * (u // 2) + m
                    kr = KR[d][r0:r0 + 64, idx, :, :]
                    be = BG[d][r0:r0 + 64, idx, 0, :]
                    ga = BG[d][r0:r0 + 64, idx, 1, :]
                    i, b, rd = bank()
                    mm(b[:, 0:128], [(kr[:, 0, :], be)], t_kr[d], t_bg[d], rd)
                    t = mm(b[:, 128:384], [(be, flat(kr))])
                    tq = mm(bq[:, (u % 2) * 256:(u % 2) * 256 + 256], [(ga, flat(kr))], rdq, tq)
                    a = DV.run(lambda e, u=u, b=b: e.copy_predicated(flat(x_[:, u, :, :]), lm[:, 0, 128 * d:128 * d + 256],
                                                                     b[:, 0:256]), t, init, t_mask)
                    c = DV.run(lambda e, u=u, b=b: e.copy_predicated(flat(l_[:, u, :, :]), si[:, d, :], b[:, 128:384]),
                               t, t_zero[d], set_free[d])
                    free(i, a, c)
                    o += [a, c]
                c = DV.run(lambda e, p=p, bq=bq: e.copy_predicated(
                    q_[:, 2 * p:2 * p + 2, :, :].rearrange("p u a t -> p u (a t)"),
                    si[:, d, :].unsqueeze(1).to_broadcast([128, 2, 256]),
                    bq[:, :].rearrange("p (u t) -> p u t", u=2)), tq, t_zero[d], set_free[d])
                free(j, c)
                ready[2 * p] = ready[2 * p + 1] = [*o, c]
            yield
            vfree = [None] * 3
            for lv in range(1, LEVELS):
                tv = []
                for p in range(3):
                    i, b, rd = bank()
                    for u in (2 * p, 2 * p + 1):
                        t = mm(b[:, (u % 2) * 128:(u % 2) * 128 + 128], [(l_[:, u, 0, :], x_[:, u, 0, :])], ready[u], rd)
                    e = copy(AC, VV[d][:, 2 * p:2 * p + 2, :], b[:, 0:256].rearrange("p (u t) -> p u t", u=2), t,
                             vfree[p], set_free[d])
                    free(i, e)
                    tv.append(e)
                yield
                tz = []
                for p in range(3):
                    i, b, rd = bank()
                    for u in (2 * p, 2 * p + 1):
                        t = mm(b[:, (u % 2) * 128:(u % 2) * 128 + 128], [(VV[d][:, u, :], x_[:, u, 1, :])], tv[p], rd)
                    vfree[p] = t
                    c = DV.run(lambda e, p=p, b=b, lv=lv: e.copy_predicated(
                        x_[:, 2 * p:2 * p + 2, 1, :],
                        lm[:, lv, 128 * (d + 1):128 * (d + 2)].unsqueeze(1).to_broadcast([128, 2, 128]),
                        b[:, 0:256].rearrange("p (u t) -> p u t", u=2)), t)
                    free(i, c)
                    ready[2 * p] = ready[2 * p + 1] = c
                yield
                if lv == LEVELS - 1:
                    break
                for p in range(3):
                    i, b, rd = bank()
                    for u in (2 * p, 2 * p + 1):
                        t = turn(b[:, (u % 2) * 128:(u % 2) * 128 + 128], x_[:, u, 1, :], ready[u], rd)
                    e = copy(AC, x_[:, 2 * p:2 * p + 2, 0, :], b[:, 0:256].rearrange("p (u t) -> p u t", u=2), t)
                    free(i, e)
                    ready[2 * p] = ready[2 * p + 1] = e
                yield

            def st(h):
                return ST[d][64 * (h % 2):64 * (h % 2) + 64, h // 2, :]

            def kr_(h, a):
                return KR[d][64 * (h % 2):64 * (h % 2) + 64, 2 * (h // 2) + m, a, :]

            def pair(v, h):
                return v[:, (h // 2) * 128:(h // 2) * 128 + 128]

            vn = VN[:, m, :]

            def heads(pairs, *producers):
                got = []
                for h0, h1 in ((0, 4), (4, 6)):
                    i, b, rd = bank()
                    t = None
                    for h in range(h0, h1):
                        t = mm(b[:, (h - h0) * 128:(h - h0 + 1) * 128], pairs(h), producers, rd,
                               t if second else None)
                    n = (h1 - h0) // 2
                    v = b[:, 0:n * 256].rearrange("p (c q j) -> p c q j", c=n, q=4)[:, :, 0:4:3, :]
                    got.append((i, v, t, h0 // 2, n))
                return got

            def parts(v, c0_, n):
                return v[:, c0_ * 128:(c0_ + n) * 128].rearrange("p (c q j) -> p c q j", c=n, q=2)

            def keep(dst, got, *producers):
                o = []
                for i, v, t, c0_, n in got:
                    e = copy(DV, parts(dst, c0_, n), v, t, producers)
                    free(i, e)
                    o.append(e)
                return o

            e = keep(RHS[d], heads(lambda h: [(q_[:, h, 0, :], pair(vn, h))] + ([(kr_(h, 0), st(h))] if second else []),
                                   t_vn, ready, t_st[d] if second else None))
            yield
            e = keep(SA[d], heads(lambda h: [(x_[:, h, 1, :], pair(RHS[d], h))], e))
            yield
            if not second:
                i, b, rd = bank()
                for h in range(6):
                    r0 = 64 * (h % 2)
                    t = mm(b[r0:r0 + 64, (h // 2) * 128:(h // 2) * 128 + 128],
                           [(BGN[d][:, 0, h * 64:(h + 1) * 64], pair(SA[d], h)),
                            (BGN[d][:, 1, h * 64:(h + 1) * 64], pair(vn, h))], e, t_bgn[d], rd)
                t_st[d] = tt(DV, ST[d], b[:, 0:384].rearrange("p (c j) -> p c j", c=3),
                             es[:, d, :].unsqueeze(2).to_broadcast([128, 3, 128]), MUL, t, t_es[d], aa_free[0])
                free(i, t_st[d])
            got = heads(lambda h: [(l_[:, h, 1, :], pair(SA[d], h)), (q_[:, h, 1, :], pair(vn, h))]
                        + ([(kr_(h, 1), st(h))] if second else []), e)
            set_free[d] = got[-1][2]
            if second:
                o = []
                for i, v, t, c0_, n in got:
                    o.append(tt(DV, parts(Y[:, m, :], c0_, n), v, parts(Y[:, m, :], c0_, n), ADD, t, y_done[m]))
                    free(i, o[-1])
                y_done[m] = o
            else:
                y_done[m] = keep(Y[:, m, :], got, t_mem2)
            yield

        def together(*gens):
            live = list(gens)
            while live:
                for g in list(live):
                    try:
                        next(g)
                    except StopIteration:
                        live.remove(g)

        together(batch(0, 0, False), batch(1, 1, False), conv_taps())
        i, b, rd = bank()
        t = mm(b[:, 0:256], [(ones, CA[:, c, :]) for c in range(3)], t_cv, rd)
        a = ts(DV, CM, b[:, 0:256], 1.0 / 384, None, MUL, None, t)
        free(i, a)
        a = tt(DV, CA, CA, CM.unsqueeze(1).to_broadcast([128, 3, 256]), SUB, a)
        s = act(CSQ, CA, ACT.Square, a)
        i, b, rd = bank()
        t = mm(b[:, 0:256], [(ones, CSQ[:, c, :]) for c in range(3)], s, rd)
        fr, r = rsq(CR, b[:, 0:256], 1.0 / 384, 1e-5, t)
        free(i, fr)
        a = tt(PL, CA, CA, CR.unsqueeze(1).to_broadcast([128, 3, 256]), MUL, r)
        z = [ts(PL, CA[:, c, :], CA[:, c, :], pk("lng")[:, c:c + 1], pk("lnb")[:, c:c + 1], MUL, ADD, a)
             for c in range(3)]
        a = act(CSQ, CA, ACT.Tanh, z, scale=0.5)
        a = ts(PL, CSQ, CSQ, 0.5, 0.5, MUL, ADD, a)
        t_conv = tt(PL, MIX[:, 2:5, :], CA, CSQ, MUL, a)
        a = tt(PL, KD[0], KD[0], KD[1], ADD, t_kd, t_bg[0], t_bg[1])
        t_bp = tt(PL, KD[0], KD[0], RRK, MUL, a, t_rrk)
        i, b, rd = bank()
        for m in range(2):
            for c in range(3):
                t = mm(b[:, m * 6 + 2 * c:m * 6 + 2 * c + 2], [(KD[0][:, c, m * 128:(m + 1) * 128], cn("ind2"))], t_bp, rd)
        bon = tiny(12).rearrange("p (m h) -> p m h", m=2)
        t_bon = copy(DV, bon, b[:, 0:12].rearrange("p (m h) -> p m h", m=2), t)
        free(i, t_bon)
        t_g = []
        for m in range(2):
            i, b, rd = bank()
            t = mm(b[:, 0:384], [(PF[:, 11, m * 128:(m + 1) * 128], pk("gup"))], t_sg, rd)
            e = copy(AC, G[:, m, :], b[:, 0:384], t, t_kr, t_bg)
            free(i, e)
            t_g.append(e)
        together(batch(0, 1, True), batch(1, 0, True))

        gst = tiny(24).rearrange("p (m a h) -> p m a h", m=2, a=2)
        t_mix = []
        for m in range(2):
            y = Y[:, m, :]
            tmp = region(39 + 1.5 * m, 384)
            yv = y.rearrange("p (h d) -> p h d", h=6)
            tv = tmp.rearrange("p (h d) -> p h d", h=6)
            mu, rs = gst[:, m, 0, :], gst[:, m, 1, :]

            def wide(v):
                return v.unsqueeze(2).to_broadcast([128, 6, 64])

            a = DV.run(lambda e, mu=mu, yv=yv: e.tensor_reduce(mu, yv, AX.X, ADD), y_done[m])
            a = ts(DV, mu, mu, 1.0 / 64, None, MUL, None, a)
            a = tt(DV, yv, yv, wide(mu), SUB, a)
            s = act(tmp, y, ACT.Square, a, t_bp)
            s = DV.run(lambda e, rs=rs, tv=tv: e.tensor_reduce(rs, tv, AX.X, ADD), s)
            _, r = rsq(rs, rs, 1.0 / 64, 64e-5, s)
            vb = tt(PL, tv, VN[:, m, :].rearrange("p (h d) -> p h d", h=6), wide(bon[:, m, :]), MUL, t_bon, r, t_vn)
            vb = tt(PL, tmp, tmp, pk("lnxb"), ADD, vb)
            a = tt(DV, yv, yv, wide(rs), MUL, r)
            a = tt(DV, y, y, pk("lnxg"), MUL, a)
            a = tt(DV, y, y, tmp, ADD, a, vb)
            a = tt(DV, y, y, G[:, m, :], MUL, a, t_g)
            i, b, rd = bank()
            for c in range(3):
                t = turn(b[:, c * 128:(c + 1) * 128], y[:, c * 128:(c + 1) * 128], a, rd)
            e = copy(AC, MIX[:, 5:8, m * 128:(m + 1) * 128], b[:, 0:384].rearrange("p (c t) -> p c t", c=3), t)
            free(i, e)
            t_mix.append(e)
        for k in range(6):
            add_slot(arena[:, (87 + 8 * k) * 256:(95 + 8 * k) * 256], *t_mix)
        add_slot(arena[:, 136 * 256:144 * 256], t_conv)
        refill()

        t_x3 = [None] * 8
        for s in range(4):
            wv, t = slab("wo2", s, 8)
            i, b, rd = bank()
            for j in range(2):
                last = mm(b[:, j * 256:(j + 1) * 256],
                          [(wv[:, k, j * 128:(j + 1) * 128], MIX[:, k, :]) for k in range(8)],
                          t, t_conv, t_mem2, t_mix, rd)
            done("wo2", s, last)
            xs = X[:, 2 * s:2 * s + 2, :]
            e = tt(DV, xs, b[:, :].rearrange("p (j t) -> p j t", j=2), xs, ADD, last)
            free(i, e)
            t_x3[2 * s] = t_x3[2 * s + 1] = e

        H3 = region(16, 8, 256)
        H3N = region(24, 2, 1024)
        XE = region(32, 8, 512)
        OH = region(48, 2, 512)
        GG = region(52, 2, 512)
        GT = region(56, 4, 256)
        W0, W1, W2 = region(60, 256), region(61, 256), region(62, 256)
        RS4 = region(135, 256)
        W3 = region(63, 256)
        t_w3 = PL.run(lambda e: e.memset(W3, 1.0), t_mix)
        t_r = norm(X, t_x3, SQ2, RS4, last)
        t_h3 = [stt(H3[:, k, :], X[:, k, :], pk("nffn")[:, k:k + 1], RS4, MUL, MUL, t_r) for k in range(8)]
        wr = pk("wr").rearrange("p (k e) -> p k e", k=8)
        i, b, rd = bank()
        for m in range(2):
            t = mm(b[:, m * 16:(m + 1) * 16], [(H3[:, k, m * 128:(m + 1) * 128], wr[:, k, :]) for k in range(8)], t_h3, rd)
        aff = tiny(32).rearrange("p (m e) -> p m e", m=2)
        rst = tiny(6).rearrange("p (a m) -> p a m", a=3)
        lg = b[:, 0:32].rearrange("p (m e) -> p m e", m=2)
        a = DV.run(lambda e: e.tensor_reduce(rst[:, 0, :], lg, AX.X, ALU.max, negate=True), t)
        x = [act(aff[:, m, :], lg[:, m, :], ACT.Exp, a, bias=rst[:, 0, m:m + 1], accum=rst[:, 1, m:m + 1])
             for m in range(2)]
        free(i, *x)
        a = DV.run(lambda e: e.reciprocal(rst[:, 2, :], rst[:, 1, :]), x)
        t_aff = tt(DV, aff, aff, rst[:, 2, :].unsqueeze(2).to_broadcast([128, 2, 16]), MUL, a)
        t_h3n = []
        for m in range(2):
            for g2 in range(2):
                i, b, rd = bank()
                for j in range(4):
                    t = turn(b[:, j * 128:(j + 1) * 128], H3[:, 4 * g2 + j, m * 128:(m + 1) * 128], t_h3, rd)
                e = copy(AC, H3N[:, m, g2 * 512:(g2 + 1) * 512], b[:, :], t)
                free(i, e)
                t_h3n.append(e)
        i, b, rd = bank()
        for m in range(2):
            t = mm(b[0:16, m * 128:(m + 1) * 128], [(aff[:, m, :], ident)], t_aff, rd)
        a = copy(DV, W0[0:16, :], b[0:16, 0:256], t)
        free(i, a)
        m8 = tiny(32).rearrange("p (r v) -> p r v", r=4)
        src = W0
        for r in range(4):
            dst = (W1, W2)[r % 2]
            a = DV.run(lambda e, r=r, src=src: e.max(m8[0:16, r, :], src[0:16, :]), a)
            a = DV.run(lambda e, r=r, src=src, dst=dst: e.match_replace(dst[0:16, :], m8[0:16, r, :], src[0:16, :], -1.0), a)
            src = dst
        a = ts(DV, W1[0:16, :], W2[0:16, :], 0.0, None, ALU.is_lt, None, a)
        a = DV.run(lambda e: e.tensor_tensor_scan(W0[0:16, :], W3[0:16, :], W1[0:16, :], 0.0, MUL, ADD), a, t_w3)
        a = tt(DV, W0[0:16, :], W0[0:16, :], W1[0:16, :], MUL, a)
        i, b, rd = bank()
        for m in range(2):
            t = mm(b[:, m * 16:(m + 1) * 16], [(W0[0:16, m * 128:(m + 1) * 128], ident[0:16, 0:16])], a, rd)
        pos = tiny(32).rearrange("p (m e) -> p m e", m=2)
        a = copy(DV, pos, b[:, 0:32].rearrange("p (m e) -> p m e", m=2), t)
        free(i, a)
        t_oh, t_gg = [], []
        for m in range(2):
            ov = OH[:, m, :].rearrange("p (e s) -> p e s", e=16)
            t_oh.append(tt(DV, ov, pos[:, m, :].unsqueeze(2).to_broadcast([128, 16, 32]),
                           cn("iota").unsqueeze(1).to_broadcast([128, 16, 32]), ALU.is_equal, a, t_const))
        for m in range(2):
            t_gg.append(tt(PL, GG[:, m, :].rearrange("p (e s) -> p e s", e=16),
                           OH[:, m, :].rearrange("p (e s) -> p e s", e=16),
                           aff[:, m, :].unsqueeze(2).to_broadcast([128, 16, 32]), MUL, t_oh[m], t_aff))
        t_xe = []
        for k in range(8):
            i, b, rd = bank()
            t = mm(b[:, :], [(H3N[:, m, k * 128:(k + 1) * 128], OH[:, m, :]) for m in range(2)], t_oh, t_h3n, rd)
            e = copy(AC if k % 2 else DV, XE[:, k, :], b[:, :], t)
            free(i, e)
            t_xe.append(e)

        HID = region(64, 8, 4, 64)
        TMP = region(72, 2, 4, 64)
        GU = region(74, 2, 512)
        YE = region(78, 2, 1024)
        t_gt = []
        hid, hid_free, gu_free = {}, {}, {}
        ye_free = [None, None]

        def gate_up(e):
            i, b, rd = bank()
            for kh in range(2):
                wv = [slab(n, 4 * e + 2 * kh + fh, 4) for n in ("eg", "eu") for fh in range(2)]
                for k in range(4):
                    for q in range(4):
                        f = lambda en, k=k, q=q, kh=kh, wv=wv: en.matmul(
                            b[32 * q:32 * q + 32, :], XE[:, 4 * kh + k, e * 32:(e + 1) * 32], wv[q][0][:, k, :],
                            start=(kh == 0 and k == 0), stop=(kh == 1 and k == 3), tile_position=(0, 32 * q))
                        if k in (0, 3):
                            last = PE.run(f, wv[q][1], t_xe, rd)
                        else:
                            PE.quiet(f)
                        if k == 3:
                            done(("eg", "eu")[q // 2], 4 * e + 2 * kh + q % 2, last)
            return i, b, last

        def hidden(e, i, b, last):
            gu, tm = GU[:, e % 2, :], TMP[:, e % 2, :, :]
            x = copy(AC, gu, b[:, :], last, gu_free.get(e - 2))
            free(i, x)
            i, b, rd = bank()
            for c in range(4):
                t = turn(b[:, c * 128:(c + 1) * 128], gu[:, c * 128:(c + 1) * 128], x, rd)
            gu_free[e] = t
            bv = b[:, :].rearrange("p (c n) -> p c n", c=4)
            a = act(tm, bv[:, :, 0:64], ACT.Tanh, t, hid.get(e - 2), scale=0.5)
            a = ts(DV, tm, tm, 0.5, 0.5, MUL, ADD, a)
            a = tt(DV, tm, bv[:, :, 0:64], tm, MUL, a)
            hid[e] = tt(DV, HID[:, e % 8, :, :], bv[:, :, 64:128], tm, MUL, a, hid_free.get(e - 8))
            free(i, hid[e])

        t_x4 = t_x3

        def down(g):
            ev = []
            es_ = range(4 * g, 4 * g + 4)
            for fh in range(2):
                i, b, rd = bank()
                for kh in range(2):
                    wv = [slab("ed", 4 * e + 2 * kh + fh, 4) for e in es_]
                    for k in range(4):
                        for q, e in enumerate(es_):
                            f = lambda en, k=k, q=q, e=e, kh=kh, wv=wv, b=b: en.matmul(
                                b[32 * q:32 * q + 32, :], HID[:, e % 8, k, 32 * kh:32 * kh + 32], wv[q][0][:, k, :],
                                start=(kh == 0 and k == 0), stop=(kh == 1 and k == 3), tile_position=(0, 32 * q))
                            if k in (0, 3):
                                last = PE.run(f, wv[q][1], hid[e], rd)
                            else:
                                PE.quiet(f)
                            if k == 3:
                                done("ed", 4 * e + 2 * kh + fh, last)
                x = copy(AC, YE[:, g % 2, fh * 512:(fh + 1) * 512], b[:, :], last, ye_free[g % 2])
                free(i, x)
                ev.append(x)
            for e in es_:
                hid_free[e] = last
            return ev

        def combine(g, ev):
            for c2_ in range(4):
                i, b, rd = bank()
                for j in range(2):
                    c = 2 * c2_ + j
                    t = mm(b[:, j * 256:(j + 1) * 256], [(YE[:, g % 2, c * 128:(c + 1) * 128], GT[:, g, :])],
                           ev[c2_ // 2], t_gt, rd)
                xs = X[:, 2 * c2_:2 * c2_ + 2, :]
                e = tt(DV, xs, b[:, :].rearrange("p (j t) -> p j t", j=2), xs, ADD, t, t_h3)
                free(i, e)
                t_x4[2 * c2_] = t_x4[2 * c2_ + 1] = e
            ye_free[g % 2] = t

        prev = None
        for e in range(17):
            if e < 16:
                now = gate_up(e)
            if prev:
                hidden(e - 1, *prev)
            prev = now
            if e == 0:
                for g2 in range(2):
                    i, b, rd = bank()
                    for j in range(2):
                        for m in range(2):
                            g = 2 * g2 + j
                            t = turn(b[:, (2 * j + m) * 128:(2 * j + m + 1) * 128], GG[:, m, g * 128:(g + 1) * 128],
                                     t_gg, rd)
                    x = copy(AC, GT[:, 2 * g2:2 * g2 + 2, :], b[:, :].rearrange("p (j t) -> p j t", j=2), t)
                    free(i, x)
                    t_gt.append(x)
            if e and e % 4 == 0:
                combine(e // 4 - 1, down(e // 4 - 1))

        t_r = norm(X, t_x4, SQ2, RS4)
        OUT = H3
        s_out = sem("s_out")
        for h in range(2):
            o = [stt(OUT[:, k, :], X[:, k, :], pk("fing")[:, k:k + 1], RS4, MUL, MUL, t_r) for k in range(4 * h, 4 * h + 4)]
            SP.load(out[:, 4 * h:4 * h + 4, :], OUT[:, 4 * h:4 * h + 4, :], s_out, 16, o)
        SP.wait([(s_out, 32)])
        assert not pending and not landed

        block = ctx.enter_context(nc.Block())

        @block.tensor
        def _(e):
            for f in PE.queue:
                f(e)

        @block.scalar
        def _(e):
            for f in AC.queue:
                f(e)

        @block.vector
        def _(e):
            for f in DV.queue:
                f(e)

        @block.gpsimd
        def _(e):
            for f in PL.queue:
                f(e)

        @block.sync
        def _(e):
            for f in SP.queue:
                f(e)


def shape_constants():
    t, p = np.arange(256), np.arange(128)
    o = {"ident": np.eye(128), "ones": np.ones((128, 128)), "blk": (p[:, None] // 64 == p[None] // 64)}
    th = 2 * np.pi * ((p[:, None] * p[None]) % 128) / 128
    o["dftc"] = np.concatenate([np.cos(th), np.sin(th)], 1)
    ph = 2 * np.pi * ((t[:, None] * t[None]) % 256) / 256
    n = np.stack([np.cos(ph), -np.sin(ph)]) / np.sqrt(256.0 * 128.0)
    o["dftn"] = n.reshape(2, 2, 128, 256).transpose(2, 0, 1, 3)
    d = np.arange(64)
    inv = 10000.0 ** (-(2.0 * (d % 16)) / 32.0)
    at = np.where(d[None] < 32, (t // 64)[:, None], (t % 64)[:, None])
    ang = at.astype(np.float32) * inv.astype(np.float32)[None]
    sg = np.where(d % 32 < 16, -1.0, 1.0)
    o["cos"] = np.cos(ang).reshape(2, 128, 64).transpose(1, 0, 2)
    o["sin"] = (np.sin(ang) * sg).reshape(2, 128, 64).transpose(1, 0, 2)
    c = p % 64
    start = np.clip(c - 8, 0, 48)
    kc = np.arange(64)
    o["amask"] = np.where((kc[None] >= start[:, None]) & (kc[None] < start[:, None] + 16), 0.0, -1e30)
    o["iota"] = np.tile(np.arange(1, 33), (128, 1))
    o["ind2"] = p[:, None] // 64 == np.arange(2)[None]
    const = np.concatenate([np.asarray(o[name], np.float32).reshape(128, n) for name, n in CONST], 1)
    m = []
    for lv in range(LEVELS):
        b = 1 << lv
        low = (p[:, None] // (2 * b) == p[None] // (2 * b)) & (p[:, None] % (2 * b) >= b) & (p[None] % (2 * b) < b)
        m += [low, low.T, low]
    up = [p[:, None] < p[None], p[:, None] <= p[None]]
    masks = np.concatenate(m + up + [p[:, None] > p[None], p[:, None] >= p[None]], 1).astype(np.float32)
    return np.ascontiguousarray(const), np.ascontiguousarray(masks)


def kernel(**inputs):
    import concourse.bacc as _bacc
    from concourse.bass_utils import run_bass_kernel_spmd as _run

    a = {n: np.asarray(v) for n, v in inputs.items()}

    def cols(v):
        v = np.asarray(v).reshape(-1)
        return v.reshape(-1, 128).T

    def rowsof(v):
        return np.broadcast_to(np.asarray(v).reshape(1, -1), (128, v.size))

    def tokens(v):
        return np.ascontiguousarray(v.reshape(256, 8, 128).transpose(2, 1, 0))

    def slabs(v, n):
        k = v.shape[0] // 128
        return v.reshape(k, 128, v.shape[1] // n, n).transpose(2, 1, 0, 3).reshape(-1, 128, SLAB)

    pk = {
        "c2": np.stack([cols(a["c"]), cols(a["c_ctx"])], 2).reshape(128, 16),
        "bada": cols(a["b_ada"]), "n1": cols(a["norm1_g"]), "n2": cols(a["norm2_g"]),
        "qg": rowsof(a["q_norm_g"]), "kg": rowsof(a["k_norm_g"]),
        "nmix": cols(a["norm_mix_g_2"]), "nmem": cols(a["norm_mem_g_2"]),
        "convw": a["conv_w_2"][0].reshape(31, 3, 128).transpose(2, 1, 0).reshape(128, 93),
        "convb": cols(a["conv_b_2"]), "lng": cols(a["conv_ln_g_2"]), "lnb": cols(a["conv_ln_b_2"]),
        "smu": cols(a["shift_mu_2"]), "dw0": cols(a["decay_w0_2"]), "ia0": cols(a["iclr_a0_2"]),
        "kk": cols(a["k_k_2"]), "ka": cols(a["k_a_2"]), "rk": cols(a["r_k_2"]),
        "nffn": cols(a["norm_ffn_g_2"]), "fing": cols(a["final_norm_g_2"]),
        "lnxg": rowsof(a["lnx_g_2"]), "lnxb": rowsof(a["lnx_b_2"]),
        "wr": a["w_router_2"][0].reshape(8, 128, 16).transpose(1, 0, 2).reshape(128, 128),
        "dup": a["decay_up_2"].reshape(128, 384), "iup": a["iclr_up_2"].reshape(128, 384),
        "gup": a["gate_up_2"].reshape(128, 384),
    }
    pack = np.ascontiguousarray(np.concatenate([pk[n].reshape(128, c) for n, c in PACK], 1))
    r, c = np.arange(4), np.arange(64)
    dr = r[None, :] - r[:, None] + 7
    dc = np.clip(c[None, :] - c[:, None] + 15, 0, 30)
    bias = a["rpb"][0][:, dr[:, None, :, None], dc[None, :, None, :]].reshape(8, 2, 128, 256)
    bias = np.ascontiguousarray(bias.transpose(2, 0, 1, 3).reshape(128, 4096))
    const, masks = shape_constants()
    m2 = a["w_mlp2"][0].reshape(2, 16, 128, 8, 128).transpose(3, 0, 2, 1, 4).reshape(16, 128, SLAB)
    ws = {
        "win": slabs(a["w_in"][0], 256), "gate": slabs(a["w_branch_gate"][0], 256),
        "fo": slabs(a["w_fourier_out"][0], 512), "ao": slabs(a["w_attn_out"][0], 512), "wo": slabs(a["w_out"][0], 256),
        "m1": slabs(a["w_mlp1"][0], 256), "m2": m2, "win2": slabs(a["w_in_2"][0], 256),
        "mk": slabs(a["w_mk_2"][0], 256), "mv": slabs(a["w_mv_2"][0], 256), "wo2": slabs(a["w_out_2"][0], 256),
    }
    ws["ada"] = a["w_ada"][0].reshape(2, 4, 128, 3, 4, 512).transpose(3, 0, 4, 2, 1, 5).reshape(24, 128, SLAB)
    for n, full in (("eg", "w_e_gate_2"), ("eu", "w_e_up_2"), ("ed", "w_e_down_2")):
        v = a[full][0]
        ws[n] = v.reshape(16, 2, 4, 128, 2, 512).transpose(0, 1, 4, 3, 2, 5).reshape(64, 128, SLAB)

    arrays = {
        "xT": tokens(a["x"]), "cT": tokens(a["ctx"]), "memT": tokens(a["mem_2"]), "pack": pack, "bias": bias,
        "const": const, "masks": masks,
    }
    for n, v in ws.items():
        arrays["w_" + n] = np.ascontiguousarray(v)
    nc = _bacc.Bacc("TRN2", target_bir_lowering=False, num_devices=1)
    t = {n: nc.dram_tensor(n, v.shape, mybir.dt.from_np(v.dtype), kind="ExternalInput").ap() for n, v in arrays.items()}
    out = nc.dram_tensor("out", (128, 8, 256), F32, kind="ExternalOutput").ap()
    build(nc, t["xT"], t["cT"], t["memT"], t["pack"], t["bias"], t["const"], t["masks"],
          {n: t["w_" + n] for n in ws}, out)
    got = _run(nc, [arrays], core_ids=[0]).results[0]["out"]
    return np.ascontiguousarray(got.transpose(2, 1, 0)).reshape(1, 256, 1024)
```

```python
from collections import deque
from contextlib import ExitStack

import numpy as np

import concourse.bass as bass
from concourse import mybir

F32 = mybir.dt.float32
F32R = mybir.dt.float32r
U8 = mybir.dt.uint8
ALU = mybir.AluOpType
ACT = mybir.ActivationFunctionType
AX = mybir.AxisListType

DECAY = 0.606531
SLAB = 2048

PACK = [
    ("c2", 16), ("bada", 48), ("n1", 8), ("n2", 8), ("qg", 64), ("kg", 64), ("nmix", 8), ("nmem", 8),
    ("convw", 93), ("convb", 3), ("lng", 3), ("lnb", 3), ("smu", 24), ("dw0", 6), ("ia0", 6), ("kk", 3),
    ("ka", 3), ("rk", 3), ("nffn", 8), ("fing", 8), ("lnxg", 384), ("lnxb", 384), ("wr", 128),
    ("dup", 384), ("iup", 384), ("gup", 384),
]
CONST = [
    ("ident", 128), ("ones", 128), ("iota", 32), ("ind2", 2), ("blk", 128), ("dftc", 256), ("dftn", 1024),
    ("cos", 128), ("sin", 128), ("amask", 64),
]
LEVELS = 7
WIN2 = (5, 6, 8, 9, 0, 4, 7, 1, 2, 3)


def offsets(table):
    at, out = 0, {}
    for name, n in table:
        out[name] = (at, n)
        at += n
    return out, at


SLABS = [("ada", 24), ("win", 8), ("gate", 8), ("fo", 2), ("ao", 2), ("wo", 4), ("m1", 16), ("m2", 16),
         ("win2", 10), ("mk", 1), ("mv", 1), ("wo2", 4), ("gu", 128), ("ed", 64)]


HALVED = ("win", "gate", "fo", "ao", "wo", "m1", "m2", "win2")


def slab_order():
    order = [("mk", 0), ("ada", 0), ("ada", 1), ("mv", 0)] + [("ada", s) for s in range(2, 8)]
    order += [("win", s) for s in (4, 5, 2, 3, 6, 7, 0, 1)]
    for s in range(8):
        order += [("gate", s), ("ada", 8 + 2 * s), ("ada", 9 + 2 * s)]
    order += [("fo", 0), ("fo", 1), ("ao", 0), ("ao", 1)]
    order += [("wo", s) for s in range(4)]
    order += [("m1", s) for s in range(16)] + [("m2", s) for s in range(16)]
    order += [("win2", s) for s in WIN2]
    order += [("wo2", s) for s in range(4)]
    for e in range(17):
        if e < 16:
            order += [("gu", 8 * e + k) for k in range(8)]
        if e and e % 4 == 0:
            order += [("ed", 4 * e - 16 + k) for k in range(16)]
    return order


class Engine:

    def __init__(self, sem):
        self.queue, self.sem, self.tick, self.passed = [], sem, 0, {}

    def wait(self, producers):
        need, left = {}, [producers]
        while left:
            p = left.pop()
            if isinstance(p, tuple) and len(p) == 2 and isinstance(p[1], int):
                need[p[0]] = max(need.get(p[0], 0), p[1])
            elif p is not None:
                left.extend(p)
        for sem, value in need.items():
            if self.passed.get(sem, 0) < value:
                self.passed[sem] = value
                self.queue.append(lambda e, s=sem, v=value: e.wait_ge(s, v))

    def run(self, fn, *producers):
        self.wait(producers)
        self.tick += 1
        self.queue.append(lambda e, f=fn, s=self.sem: f(e).then_inc(s, 1))
        return (self.sem, self.tick)

    def quiet(self, fn, *producers):
        self.wait(producers)
        self.queue.append(fn)

    def load(self, out, src, sem, value, *producers):
        self.wait(producers)
        self.queue.append(lambda e: e.dma_start(out, src).then_inc(sem, 16))
        return (sem, value)


def build(nc, xT, cT, memT, pack, bias, const, masks, w, out):
    PO, PN = offsets(PACK)
    CO, CN = offsets(CONST)
    ctx = ExitStack()
    with ctx:
        def sb(name, shape, dt=F32):
            return ctx.enter_context(nc.sbuf_tensor(name, shape, dt))

        def sem(name):
            return ctx.enter_context(nc.semaphore(name))

        NRING = 5
        AR = 144 * 256
        packt = sb("packt", [128, PN])
        NM = LEVELS * 384 + 512
        constt = sb("constt", [128, CN + NM // 4])
        maskt = constt[:, CN:CN + NM // 4].bitcast(U8)
        small = sb("small", [128, 820])
        with ExitStack() as names:
            halved = [names.enter_context(nc.sbuf_tensor(f"half{i}", [128, SLAB], F32R))
                      for i in range(NRING + AR // SLAB)]
        ring = sb("ring", [128, NRING * SLAB])
        arena = sb("arena", [128, AR])
        banks = [ctx.enter_context(nc.psum_tensor(f"bank{i}", [128, 512], F32)) for i in range(8)]

        PE, AC, DV, PL, SP = (Engine(sem(n)) for n in ("s_pe", "s_act", "s_dve", "s_pool", "s_sp"))

        def pk(name):
            a, n = PO[name]
            return packt[:, a:a + n]

        def cn(name):
            a, n = CO[name]
            return constt[:, a:a + n]

        small_at = [0]

        def tiny(n):
            a = small_at[0]
            small_at[0] += n
            assert small_at[0] <= 820
            return small[:, a:a + n]

        def region(kb, *dims):
            n = int(np.prod(dims))
            a = int(kb * 256)
            assert a + n <= AR, (kb, dims)
            v = arena[:, a:a + n]
            names = "abcd"[:len(dims)]
            if len(dims) > 1:
                v = v.rearrange(f"p ({' '.join(names)}) -> p {' '.join(names)}",
                                **{names[i]: dims[i] for i in range(len(dims))})
            return v

        MUL, ADD, SUB = ALU.mult, ALU.add, ALU.subtract
        ALL = slice(None)
        ident = cn("ident")
        ones = cn("ones")

        pool = deque((i, []) for i in range(8))

        def bank():
            i, readers = pool.popleft()
            return i, banks[i], readers

        def free(i, *readers):
            pool.append((i, list(readers)))

        slots = deque()
        for i in range(NRING):
            slots.append((ring[:, i * SLAB:(i + 1) * SLAB], sem(f"s_w{i}"), 0, []))
        pending = deque(slab_order())
        landed, extra = {}, []

        def refill(n=1000):
            while slots and pending and n:
                n -= 1
                place, s, used, readers = slots.popleft()
                name, n = pending.popleft()
                t = SP.load(place, w[name][n], s, 16 * (used + 1), readers)
                landed[(name, n)] = (place, t, s, used + 1)

        def add_slot(view, *readers):
            s = sem(f"s_x{len(extra)}")
            extra.append(s)
            slots.append((view, s, 0, list(readers)))
            return s

        def slab(name, n, k):
            refill()
            place, t, s, used = landed[(name, n)]
            return place.rearrange("p (k n) -> p k n", k=k), t

        def done(name, n, reader):
            place, t, s, used = landed.pop((name, n))
            if (name, n) in halves and halves[(name, n)][0].offset not in stale:
                hi_free.append((halves[(name, n)][0], [reader]))
            for v, x in once:
                if s is x:
                    hi_free.append((v, [reader]))
                    return
            slots.append((place, s, used, [reader]))
            refill()

        hi_free, halves, stale = deque([(region(136, SLAB), [])]), {}, []
        once = [(v, add_slot(v)) for v in (region(120, SLAB), region(128, SLAB))]
        slots.rotate(2)
        to_cut = deque(x for x in slab_order() if x[0] in HALVED)

        def half(v):
            width = NRING * SLAB if v.name == "ring" else AR
            row, at = divmod(v.offset, width)
            assert v.ap[0][0] == width
            return bass.AP(halved[at // SLAB + (0 if v.name == "ring" else NRING)], row * SLAB + at % SLAB,
                           [(SLAB, v.ap[0][1])] + list(v.ap[1:]))

        def halve(hi, v, *producers, eng=None):
            a = act(half(hi), v, ACT.Copy, *producers)
            return [a, tt(eng or DV, half(v), v, half(hi).bitcast(F32), SUB, a)]

        def on_pool(x):
            return x == ("win", 4) or x[0] in ("gate", "fo", "wo", "win2")

        def cut():
            x = to_cut.popleft()
            v, readers = hi_free.popleft()
            place, t, _, _ = landed[x]
            halves[x] = (v, halve(v, place, t, readers, eng=PL if on_pool(x) else DV))

        def ahead():
            while hi_free and to_cut and to_cut[0] in landed:
                cut()

        def slab2(name, n, k):
            refill()
            if (name, n) not in halves:
                cut()
            ahead()
            hi, t = halves[(name, n)]
            return [half(v.rearrange("p (k n) -> p k n", k=k)) for v in (hi, landed[(name, n)][0])], t

        def three(pairs):
            return [x for (ah, al), (bh, bl) in pairs for x in ((ah, bh), (ah, bl), (al, bh))]

        def both(hi_lo, *at):
            return [v[at] for v in hi_lo]

        def mm(dst, pairs, *producers, each=()):
            PE.wait(producers)
            last = len(pairs) - 1
            for j, (l, r) in enumerate(pairs):
                if each and j % (len(pairs) // len(each)) == 0:
                    PE.wait(each[j // (len(pairs) // len(each))])
                f = lambda e, l=l, r=r, j=j: e.matmul(dst, l, r, start=(j == 0), stop=(j == last))
                if j < last:
                    PE.quiet(f)
                else:
                    t = PE.run(f)
            return t

        def quarters(b, left, wv, k, *producers):
            PE.wait(producers)
            for q in range(4):
                f = lambda e, q=q: e.matmul(b[32 * q:32 * q + 32, :], left[q], wv[:, q, :], start=(k == 0),
                                            stop=(k == 7), tile_position=(0, 32 * q))
                if q < 3:
                    PE.quiet(f)
                else:
                    t = PE.run(f)
            return t

        def keep_warm(n):
            i, b, rd = bank()
            free(i, mm(b[:, 0:256], [(ident, constt[:, 0:256])] * n, rd, t_id))

        def turn(dst, src, *producers):
            return PE.run(lambda e: e.transpose(dst, src, ident), *producers)

        def act(dst, src, func, *producers, bias=0.0, scale=1.0, accum=None):
            if accum is None:
                return AC.run(lambda e: e.activation(dst, src, func, bias=bias, scale=scale), *producers)
            return AC.run(lambda e: e.activation(dst, src, func, bias=bias, scale=scale, accum_out=accum),
                          *producers)

        def copy(eng, dst, src, *producers):
            if eng is AC:
                return act(dst, src, ACT.Copy, *producers)
            return eng.run(lambda e: e.tensor_copy(dst, src), *producers)

        def tt(eng, dst, a, b, op, *producers):
            return eng.run(lambda e: e.tensor_tensor(dst, a, b, op), *producers)

        def ts(eng, dst, a, s1, s2, op0, op1, *producers):
            if op1 is None:
                return eng.run(lambda e: e.tensor_scalar(dst, a, s1, None, op0), *producers)
            return eng.run(lambda e: e.tensor_scalar(dst, a, s1, s2, op0, op1), *producers)

        def stt(dst, a, s, b, op0, op1, *producers):
            return DV.run(lambda e: e.scalar_tensor_tensor(dst, a, s, b, op0, op1), *producers)

        def rsq(dst, src, scale, eps, *producers):
            a = ts(DV, dst, src, scale, eps, ALU.mult, ALU.add, *producers)
            b = act(dst, dst, ACT.Sqrt, a)
            c = DV.run(lambda e: e.reciprocal(dst, dst), b)
            return a, c


        X = region(0, 8, 256)
        C = region(8, 8, 256)
        HX = region(16, 8, 512)
        TH = region(32, 16, 256)
        BI = region(48, 64, 64)
        V = region(64, 4, 512)
        QT = region(72, 4, 256)
        KT = region(76, 4, 512)
        QN = region(84, 4, 512)
        FT = region(92, 4, 256)
        O = region(92, 2, 512)
        YF = region(96, 4, 256)
        YA = region(100, 4, 256)
        P = region(104, 3, 512)
        PT = region(110, 3, 512)
        UC = region(104, 2, 4, 256)
        CQ = region(116, 2, 64)
        SQ = region(116.5, 2, 64)
        CK = region(117, 2, 64)
        SK = region(117.5, 2, 64)
        RS = region(118, 512)
        SQR = region(32, 8, 512)

        n0 = PO["lnxg"][0]
        MEM = region(84, 8, 256)
        SQM = region(64, 8, 256)
        RS3 = region(102, 256)
        KH = packt[:, n0:n0 + 512].rearrange("p (j t) -> p j t", j=2)
        VH = packt[:, n0 + 512:n0 + 1024].rearrange("p (j t) -> p j t", j=2)
        t_pack = SP.load(packt[:, 0:n0], pack[:, 0:n0], sem("s_pack"), 16)
        t_id = SP.load(constt[:, 0:256], const[:, 0:256], sem("s_id"), 16)
        t_mem = SP.load(MEM, memT, sem("s_mem"), 16)
        refill(1)
        t_x = SP.load(X, xT, sem("s_x"), 16)
        refill(1)
        t_c = SP.load(C, cT, sem("s_c"), 16)
        refill()
        t_const = [t_id, (sem("s_const"), 16)]
        t_pack2 = (sem("s_pack2"), 16)

        class Norm:

            def __init__(self, src, sq):
                self.src, self.sq, self.k = src, sq, 0
                self.i, self.b, self.rd = bank()

            def square(self, k, *producers):
                return act(self.sq[:, k, :], self.src[:, k, :], ACT.Square, *producers)

            def add(self, t):
                k = self.k
                f = lambda e: e.matmul(self.b[:, 0:256], ones, self.sq[:, k, :], start=(k == 0), stop=(k == 7))
                self.t = PE.run(f, t, self.rd)
                self.k += 1

            def end(self, rs, *producers):
                fr, t = rsq(rs, self.b[:, 0:256], 1.0 / 1024, 1e-6, self.t, *producers)
                free(self.i, fr)
                return t

        def norm(src, producers, sq, rs, *sq_free):
            n = Norm(src, sq)
            for t in [n.square(k, producers[k], *sq_free) for k in range(8)]:
                n.add(t)
            return n.end(rs)

        def mem_k():
            wv, t = slab("mk", 0, 8)
            i, b, rd = bank()
            for j in range(2):
                last = mm(b[:, j * 256:(j + 1) * 256],
                          [(wv[:, k, j * 128:(j + 1) * 128], MEM[:, k, :]) for k in range(8)], t, rd, each=t_m)
            done("mk", 0, last)
            t_kh = copy(AC, KH, b[:, :].rearrange("p (j t) -> p j t", j=2), last)
            free(i, t_kh)
            return t_kh

        def mem_v():
            wv, t = slab("mv", 0, 8)
            i, b, rd = bank()
            for j in range(2):
                last = mm(b[:, j * 256:(j + 1) * 256],
                          [(MEM[:, k, j * 128:(j + 1) * 128], wv[:, k, :]) for k in range(8)], t, t_m, rd)
            done("mv", 0, last)
            t_vh = copy(AC, VH, b[:, :].rearrange("p (j t) -> p j t", j=2), last)
            free(i, t_vh)
            return t_vh

        cwide = region(100, 256)
        c2v = cwide.rearrange("p (k m) -> p k m", k=8)
        t_c2 = PL.run(lambda e: e.memset(cwide, 0.0))
        c2 = tiny(16)
        a = act(c2, pk("c2"), ACT.Tanh, t_pack, scale=0.5)
        a = ts(DV, c2, c2, 0.5, 0.5, MUL, ADD, a)
        t_c2 = tt(DV, c2v[:, :, 0:2], c2.rearrange("p (k b) -> p k b", k=8),
                  pk("c2").rearrange("p (k b) -> p k b", k=8), MUL, a, t_c2)

        mod = tiny(96).rearrange("p (m b) -> p m b", m=48)
        bada = pk("bada")
        MR0, MR = region(112, 512), region(118, 512)

        def ada(part, k0, n, b, readers):
            for k in range(k0, k0 + n):
                wv, t = slab("ada", 8 * part + k, 4)
                last = quarters(b, [c2v[:, k, :]] * 4, wv, k, t, t_c2, readers)
                done("ada", 8 * part + k, last)
            return last

        def ada_end(part, i, b, last, mr_free, MR=MR):
            e = copy(AC, MR, b[:, :], last, mr_free)
            free(i, e)
            i, b, rd = bank()
            for j in range(4):
                t = turn(b[:, j * 128:(j + 1) * 128], MR[:, j * 128:(j + 1) * 128], e, rd, t_id)
            m = tt(DV, mod[:, 16 * part:16 * part + 16, :].rearrange("p (q j) b -> p q j b", q=4),
                   b[:, :].rearrange("p (j q m) -> p q j m", j=4, q=4)[:, :, :, 0:2],
                   bada[:, 16 * part:16 * part + 16].rearrange("p (q j) -> p q j", q=4).unsqueeze(3)
                   .to_broadcast([128, 4, 4, 2]), ADD, t)
            free(i, m)
            return t, m

        ai, ab, ard = bank()

        def unit(v, at, eng, *producers):
            q = act(SQR[:, :, at], v, ACT.Square, *producers)
            bi, b, rd = bank()
            t = mm(b[:, 0:256], [(ones, SQR[:, k, at]) for k in range(8)], q, t_id, rd)
            fr, t = rsq(RS[:, at], b[:, 0:256], 1.0 / 1024, 1e-6, t)
            free(bi, fr)
            return tt(eng, HX[:, :, at], v, RS[:, at].unsqueeze(1).to_broadcast([128, 8, 256]), MUL, t)

        t_rm = norm(MEM, [t_mem] * 8, SQM, RS3)
        t_m = [stt(MEM[:, k, :], MEM[:, k, :], pk("nmem")[:, k:k + 1], RS3, MUL, MUL, t_rm, t_pack) for k in range(8)]
        xn0 = unit(X, slice(0, 256), DV, t_x)
        t_kh = mem_k()
        ada(0, 0, 2, ab, ard)
        xn1 = unit(C, slice(256, 512), PL, t_c)
        ada(0, 2, 2, ab, ard)
        t_vh = mem_v()
        last = ada(0, 4, 4, ab, ard)
        SP.load(constt[:, 256:CN], const[:, 256:CN], *t_const[1])
        t_mr, t = ada_end(0, ai, ab, last, None, MR0)
        cut()
        t_mr = [xn0, xn1]
        gs1 = tiny(16).rearrange("p (m b) -> p m b", m=8)
        t = stt(gs1, mod[:, 8:16, :], 1.0, pk("n1").unsqueeze(2).to_broadcast([128, 8, 2]), ADD, MUL, t)
        HXH = [C, region(48, 8, 256)]

        def hx(k, t0, t1):
            h = t0 // 256
            return half(HXH[h][:, k, t0 - 256 * h:t1 - 256 * h]), half(HX[:, k, t0:t1])

        t_hx, t_hc = [], []
        for k in range(8):
            x = HX[:, k, 0:256]
            a = act(half(HXH[0][:, k, :]), x, ACT.Identity, t, xn0, xn1, scale=gs1[:, k, 0:1], bias=mod[:, k, 0:1])
            b_ = ts(DV, x, x, gs1[:, k, 0:1], mod[:, k, 0:1], MUL, ADD, a)
            t_hx.append([a, tt(DV, half(x), x, half(HXH[0][:, k, :]).bitcast(F32), SUB, b_)])
        ahead()
        for k in range(8):
            x = HX[:, k, 256:512]
            a = act(half(HXH[1][:, k, :]), x, ACT.Identity, t, xn1, scale=gs1[:, k, 1:2], bias=mod[:, k, 1:2])
            b_ = ts(PL, x, x, gs1[:, k, 1:2], mod[:, k, 1:2], MUL, ADD, a)
            t_hc.append([a, tt(DV, half(x), x, half(HXH[1][:, k, :]).bitcast(F32), SUB, b_)])
        t_h = t_hx

        qg, kg = pk("qg"), pk("kg")

        def tables(g, dc, ds, scale):
            gg = tiny(64)
            a = ts(PL, gg, g, scale, 0.0, MUL, ADD, t_pack)
            o = []
            for i in range(2):
                cs = cn("cos").rearrange("p (i d) -> p i d", i=2)[:, i, :]
                sn = cn("sin").rearrange("p (i d) -> p i d", i=2)[:, i, :]
                o.append(tt(PL, dc[:, i, :], cs, gg, MUL, a, t_const))
                for x in range(2):
                    for half in range(2):
                        d, f = 32 * x + 16 * half, 32 * x + 16 * (1 - half)
                        o.append(tt(PL, ds[:, i, d:d + 16], sn[:, d:d + 16], gg[:, f:f + 16], MUL, a, t_const))
            return o

        t_tq = tables(qg, CQ, SQ, 0.125)
        t_tk = tables(kg, CK, SK, 1.0)

        QNR = region(32, 6, 512)
        m_free = [None] * 4

        def first_slab(got, wv, t):
            w1, w2 = t[0], t[1]

            def run(tl, w, part, wait, start, stop):
                i, b, rd = got[tl]
                PE.wait([rd, wait])
                for k in range(8):
                    PE.wait((t_hx if tl < 2 else t_hc)[k])
                    for j, v in enumerate(hx(k, tl * 128, (tl + 1) * 128)[:part]):
                        f = lambda e, k=k, j=j, v=v: e.matmul(b[:, 0:256], v, w[:, k], start=(start and k + j == 0),
                                                              stop=(stop and k == 7))
                        x = PE.run(f)
                return x

            for group in ((0, 1), (2, 3)):
                for tl in group:
                    run(tl, wv[0], 2, w1, True, False)
                for tl in group:
                    x = run(tl, wv[1], 1, w2, False, True)
                    got[tl] = (*got[tl][:2], x)
            return x

        def rows(names, tiles):
            got = [bank() for _ in tiles]
            for h, n in enumerate(names):
                wv, t = slab2("win", n, 8)
                if n == 4:
                    last = first_slab(got, wv, t)
                    done("win", n, last)
                    continue
                for ti, tl in enumerate(tiles):
                    i, b, rd = got[ti]
                    last = mm(b[:, h * 256:(h + 1) * 256],
                              three((hx(k, tl * 128, (tl + 1) * 128), both(wv, ALL, k)) for k in range(8)),
                              t, rd, each=t_hx if tl < 2 else t_hc)
                    got[ti] = (i, b, last)
                done("win", n, last)
            return got

        rstd = tiny(8 * 6).rearrange("p (i h) -> p i h", i=6)
        t_turned = {}
        normed = []

        def norm_rope(kind, tl, i, b, t):
            z = len(normed)
            n = QNR[:, z, :]
            m = QN[:, z % 4, :]
            bv = b[:, :].rearrange("p (h d) -> p h d", h=8)
            nv = n.rearrange("p (h d) -> p h d", h=8)
            mv = m.rearrange("p (h d) -> p h d", h=8)
            r = rstd[:, z, :]
            a = act(n, b[:, :], ACT.Square, t)
            a = DV.run(lambda e: e.tensor_reduce(r, nv, AX.X, ADD), a)
            _, a = rsq(r, r, 1.0 / 64, 1e-6, a)
            a = tt(DV, nv, bv, r.unsqueeze(2).to_broadcast([128, 8, 64]), MUL, a)
            free(i, a)
            if kind == "c":
                a = tt(PL, nv, nv, kg.unsqueeze(1).to_broadcast([128, 8, 64]), MUL, a)
            else:
                cs, sn, tabs = (CQ, SQ, t_tq) if kind == "q" else (CK, SK, t_tk)
                o = []
                for x in range(2):
                    for half in range(2):
                        d, f = 32 * x + 16 * half, 32 * x + 16 * (1 - half)
                        o.append(tt(DV, mv[:, :, d:d + 16], nv[:, :, f:f + 16],
                                    sn[:, tl, d:d + 16].unsqueeze(1).to_broadcast([128, 8, 16]), MUL, a, tabs,
                                    m_free[z % 4]))
                c = tt(PL, nv, nv, cs[:, tl, :].unsqueeze(1).to_broadcast([128, 8, 64]), MUL, o, a, tabs)
                a = tt(PL, n, n, m, ADD, c, o)
                m_free[z % 4] = a
            normed.append((kind, tl, n, a))

        def turn_rows(kind, tl, n, a):
            j, p, rd = bank()
            for c in range(4):
                t = turn(p[:, c * 128:(c + 1) * 128], n[:, c * 128:(c + 1) * 128], a, rd)
            at = tl + (2 if kind == "c" else 0)
            dst = (QT if kind == "q" else KT)[:, :, at * 128:(at + 1) * 128]
            e = copy(AC, dst, p[:, :].rearrange("p (c t) -> p c t", c=4), t)
            free(j, e)
            t_turned[(kind, tl)] = e

        got = rows((4, 5), (0, 1, 2, 3))
        for tl in range(4):
            norm_rope("k" if tl < 2 else "c", tl % 2, *got[tl])
        gq = rows((2, 3), (0, 1))
        ahead()
        for tl in range(2):
            norm_rope("q", tl, *gq[tl])
        got = rows((6, 7), (0, 1, 2, 3))
        t_v = []
        for tl in range(4):
            i, b, t = got[tl]
            e = copy(AC, V[:, tl, :], b[:, :], t)
            free(i, e)
            t_v.append(e)
        t_hc_read = t

        t_f = []
        for n in range(2):
            wv, t = slab2("win", n, 8)
            i, b, rd = bank()
            for j in range(2):
                last = mm(b[:, j * 256:(j + 1) * 256],
                          three((both(wv, ALL, k, slice(j * 128, (j + 1) * 128)), hx(k, 0, 256)) for k in range(8)),
                          t, t_h, rd)
            done("win", n, last)
            e = copy(AC, FT[:, 2 * n:2 * n + 2, :], b[:, :].rearrange("p (j t) -> p j t", j=2), last)
            free(i, e)
            t_f.append(e)
        t_bias = SP.load(region(48, 4096), bias, sem("s_bias"), 16, t_hc_read)
        t_bm = tt(PL, BI, BI, cn("amask").unsqueeze(1).to_broadcast([128, 64, 64]), ADD, t_bias, t_const)
        for z in normed:
            turn_rows(*z)

        dc = cn("dftc")
        dn = cn("dftn").rearrange("p (s m t) -> p s m t", s=2, m=2)
        t_u = []
        for m in range(2):
            for g2 in range(2):
                i, b, rd = bank()
                for j in range(2):
                    t = mm(b[:, j * 256:(j + 1) * 256], [(FT[:, 2 * g2 + j, m * 128:(m + 1) * 128], dc)],
                           t_f[g2], t_const, rd)
                e = copy(DV, UC[:, m, 2 * g2:2 * g2 + 2, :], b[:, :].rearrange("p (j t) -> p j t", j=2), t)
                free(i, e)
                t_u.append(e)
        YFH = region(84, 4, 256)
        t_yf = []
        for g2 in range(2):
            i, b, rd = bank()
            for j in range(2):
                g = 2 * g2 + j
                t = mm(b[:, j * 256:(j + 1) * 256],
                       [(UC[:, m, g, s * 128:(s + 1) * 128], dn[:, s, m, :]) for m in range(2) for s in range(2)],
                       t_u, rd)
            x, g = b[:, :].rearrange("p (j t) -> p j t", j=2), slice(2 * g2, 2 * g2 + 2)
            h = act(half(YFH[:, g, :]), x, ACT.Copy, t, m_free)
            e = tt(DV, half(YF[:, g, :]), x, half(YFH[:, g, :]).bitcast(F32), SUB, h)
            free(i, e)
            t_yf.append(e)
        t_uc_read = t

        t_th = [None] * 8

        def gate_step(s):
            wv, t = slab2("gate", s, 8)
            i, b, rd = bank()
            for j in range(2):
                last = mm(b[:, j * 256:(j + 1) * 256],
                          three((both(wv, ALL, k, slice(j * 128, (j + 1) * 128)), hx(k, 0, 256)) for k in range(8)),
                          t, t_h, rd)
            done("gate", s, last)
            e = act(TH[:, 2 * s:2 * s + 2, :], b[:, :].rearrange("p (j t) -> p j t", j=2), ACT.Tanh, last, scale=0.5)
            free(i, e)
            t_th[s] = ts(PL, TH[:, 2 * s:2 * s + 2, :], TH[:, 2 * s:2 * s + 2, :], 0.5, 0.5, MUL, ADD, e)

        late = {"free": t_mr, "mod": []}

        def ada_step(n):
            part = 1 + n // 4
            if n % 4 == 0:
                late["bank"] = bank()
            i, b, rd = late["bank"]
            last = ada(part, 2 * (n % 4), 2, b, rd)
            if n % 4 == 3:
                late["free"], m = ada_end(part, i, b, last, late["free"])
                late["mod"].append(m)

        filler = deque()
        for s in range(8):
            filler.append(lambda s=s: gate_step(s))
            filler.append(lambda s=s: ada_step(s))

        stat = tiny(3 * 16 * 2).rearrange("p (a u) -> p a u", a=3)
        units = [(h, qt) for h in range(8) for qt in range(2)]
        t_o = [[], []]
        o_last = {}
        BIv = region(48, 16, 256)
        p_free = [t_uc_read] * 3
        pt_free = [t_uc_read] * 3
        held = {}

        def att_scores(u):
            h, qt = units[u]
            c, r0 = h // 2, 64 * (h % 2)
            i, b, rd = bank()
            q = QT[r0:r0 + 64, c, qt * 128:(qt + 1) * 128]
            t = mm(b[:, :], [(q, KT[r0:r0 + 64, c, :])], list(t_turned.values()), rd)
            t = tt(DV, b[:, 0:256], b[:, 0:256], BIv[:, 2 * h + qt, :], ADD, t, t_bm)
            t = DV.run(lambda e: e.tensor_reduce(stat[:, 0, u:u + 1], b[:, :], AX.X, ALU.max, negate=True), t)
            t = act(P[:, u % 3, :], b[:, :], ACT.Exp, t, p_free[u % 3], bias=stat[:, 0, u:u + 1],
                    accum=stat[:, 1, u:u + 1])
            free(i, t)
            t2 = DV.run(lambda e: e.reciprocal(stat[:, 2, u:u + 1], stat[:, 1, u:u + 1]), t)
            held[u] = (t, t2)

        def att_turn(u):
            t, t2 = held[u]
            i, b, rd = bank()
            for j in range(4):
                x = turn(b[:, j * 128:(j + 1) * 128], P[:, u % 3, j * 128:(j + 1) * 128], t, rd)
            p_free[u % 3] = x
            e = copy(AC if u % 2 else DV, PT[:, u % 3, :], b[:, :], x, pt_free[u % 3])
            free(i, e)
            held[u] = (e, t2)

        def att_out(u):
            h, qt = units[u]
            e, t2 = held.pop(u)
            i, b, rd = bank()
            x = mm(b[:, 0:64],
                   [(PT[:, u % 3, j * 128:(j + 1) * 128], V[:, j, h * 64:(h + 1) * 64]) for j in range(4)],
                   e, t_v, rd)
            pt_free[u % 3] = x
            t_o[qt].append(ts(DV, O[:, qt, h * 64:(h + 1) * 64], b[:, 0:64],
                              stat[:, 2, u:u + 1], None, MUL, None, x, t2, t_u))
            free(i, t_o[qt][-1])

        for u in range(18):
            if u < 16:
                att_scores(u)
            if filler:
                filler.popleft()()
            if u not in (14, 15):
                ahead()
            if 0 <= u - 1 < 16:
                att_turn(u - 1)
            if 0 <= u - 2 < 16:
                att_out(u - 2)
        while filler:
            filler.popleft()()
        t_mod, t_mr = late["mod"], late["free"]
        gs2 = tiny(8)
        t_mod = t_mod + [stt(gs2, mod[:, 32:40, 0], 1.0, pk("n2"), ADD, MUL, t_mod)]
        YAH = region(88, 4, 256)
        t_ya = []
        for qt in range(2):
            i, b, rd = bank()
            for c in range(4):
                t = turn(b[:, c * 128:(c + 1) * 128], O[:, qt, c * 128:(c + 1) * 128], t_o[qt], rd)
            x = b[:, :].rearrange("p (c t) -> p c t", c=4)
            at = slice(qt * 128, (qt + 1) * 128)
            h = act(half(YAH[:, :, at]), x, ACT.Copy, t, m_free)
            e = tt(DV, half(YA[:, :, at]), x, half(YAH[:, :, at]).bitcast(F32), SUB, h, t_mod)
            free(i, e)
            t_ya.append(e)

        MG = C
        M2 = region(48, 4, 512)
        MGH = region(104, 8, 256)
        t_mg = [None] * 4
        part = {}
        for name, Y, ty, g0 in (("fo", (YFH, YF), t_yf, 0), ("ao", (YAH, YA), t_ya, 8)):
            for s in range(2):
                wv, t = slab2(name, s, 4)
                for c2_ in range(2):
                    n = 2 * s + c2_
                    i, b, rd = bank()
                    for j in range(2):
                        col = (2 * c2_ + j) * 128
                        last = mm(b[:, j * 256:(j + 1) * 256], three((both(wv, ALL, k, slice(col, col + 128)), [half(v[:, k, :]) for v in Y])
                                        for k in range(4)), t, ty, rd)
                    bv = b[:, :].rearrange("p (j t) -> p j t", j=2)
                    if name == "fo":
                        part[n] = tt(DV, MG[:, 2 * n:2 * n + 2, :], bv, TH[:, 2 * n:2 * n + 2, :], MUL,
                                     last, t_th[n], xn1)
                        free(i, part[n])
                    else:
                        m = M2[:, n, :].rearrange("p (j t) -> p j t", j=2)
                        e = tt(DV, m, bv, TH[:, 8 + 2 * n:10 + 2 * n, :], MUL, last, t_th[4 + n], m_free)
                        free(i, e)
                        at = slice(2 * n, 2 * n + 2)
                        h = tt(DV, half(MGH[:, at, :]), MG[:, at, :], m, ADD, e, part[n], p_free, pt_free)
                        e = tt(DV, MG[:, at, :], MG[:, at, :], half(MGH[:, at, :]).bitcast(F32), SUB, h)
                        t_mg[n] = tt(DV if n > 1 else PL, half(MG[:, at, :]), MG[:, at, :], m, ADD, e)
                done(name, s, last)

        RS2 = region(118, 256)
        t_x1, xg = [None] * 8, []
        H = region(16, 8, 256)
        SQ1 = region(32, 8, 256)
        nx, sq = Norm(X, SQ1), []
        for s in range(4):
            wv, t = slab2("wo", s, 8)
            i, b, rd = bank()
            for j in range(2):
                last = mm(b[:, j * 256:(j + 1) * 256],
                          three((both(wv, ALL, k, slice(j * 128, (j + 1) * 128)), (half(MGH[:, k, :]), half(MG[:, k, :])))
                                for k in range(8)), t, rd, each=t_mg)
            done("wo", s, last)
            o = []
            for j in range(2):
                c = 2 * s + j
                t_x1[c] = stt(X[:, c, :], b[:, j * 256:(j + 1) * 256], mod[:, 16 + c, 0:1], X[:, c, :], MUL, ADD,
                              last, t_mod)
                o.append(t_x1[c])
            free(i, *o)
            if s:
                nx.add(sq[2 * s - 2])
                nx.add(sq[2 * s - 1])
            for c in (2 * s, 2 * s + 1):
                sq.append(nx.square(c, t_x1[c], t_mg))
                xg.append(act(H[:, c, :], X[:, c, :], ACT.Copy, t_x1[c], t_th, t_mod, scale=gs2[:, c:c + 1]))

        MF = region(104, LEVELS * 384 + 512)
        t_mask = SP.load(MF, masks, sem("s_mask"), 16, last)
        t_mask = PL.run(lambda e: e.tensor_copy(maskt, MF), t_mask)

        HH = region(8, 8, 256)
        nx.add(sq[6])
        nx.add(sq[7])
        t_r2 = nx.end(RS2, t_mr)
        keep_warm(7)

        def scaled(rs, shift, *producers):
            v, o = [], []
            for k in range(9):
                if k < 8:
                    v.append(tt(DV, H[:, k, :], H[:, k, :], rs, MUL, producers))
                    h = act(half(HH[:, k, :]), H[:, k, :], ACT.Identity, v[k],
                            bias=shift[:, k:k + 1] if shift is not None else 0.0)
                    o.append([h])
                if k >= 1:
                    x, h = H[:, k - 1, :], half(HH[:, k - 1, :])
                    if shift is not None:
                        t = stt(half(x), x, shift[:, k - 1:k], h.bitcast(F32), ADD, SUB, o[k - 1])
                    else:
                        t = tt(DV, half(x), x, h.bitcast(F32), SUB, o[k - 1])
                    o[k - 1].append(t)
            return o

        t_h2 = scaled(RS2, mod[:, 24:32, 0], t_r2, xg, last)

        A = region(32, 32, 256)
        AH = region(68, 32, 256)
        t_a = [None] * 16
        for s in range(16):
            wv, t = slab2("m1", s, 8)
            i, b, rd = bank()
            for j in range(2):
                last = mm(b[:, j * 256:(j + 1) * 256],
                          three((both(wv, ALL, k, slice(j * 128, (j + 1) * 128)), (half(HH[:, k, :]), half(H[:, k, :])))
                                for k in range(8)), t, rd, each=t_h2)
            done("m1", s, last)
            av = A[:, 2 * s:2 * s + 2, :]
            bv = b[:, :].rearrange("p (j t) -> p j t", j=2)
            e = act(av, bv, ACT.Relu, last)
            e = tt(DV, av, av, bv, MUL, e)
            free(i, e)
            t_a[s] = halve(AH[:, 2 * s:2 * s + 2, :], av, e)
        SQ3 = region(104, 8, 256)
        nx, sq, xg, t_m1 = Norm(X, SQ3), [], [], last
        for s in range(16):
            wv, t = slab2("m2", s, 16)
            if s % 2 == 0:
                i, b, rd = bank()
            c = s // 2
            PE.wait([t, rd] + t_a[8 * (s % 2):8 * (s % 2) + 8])
            pairs = three((both(wv, ALL, k), [half(v[:, 16 * (s % 2) + k, :]) for v in (AH, A)]) for k in range(16))
            for k, (x, y) in enumerate(pairs):
                f = lambda e, k=k, b=b, x=x, y=y, s=s: e.matmul(b[:, 0:256], x, y, start=(s % 2 == 0 and k == 0),
                                                                stop=(s % 2 == 1 and k == 47))
                if k < 47:
                    PE.quiet(f)
                else:
                    last = PE.run(f)
            done("m2", s, last)
            if s % 2:
                t_x1[c] = stt(X[:, c, :], b[:, 0:256], mod[:, 40 + c, 0:1], X[:, c, :], MUL, ADD, last, t_mod)
                free(i, t_x1[c])
                if c:
                    nx.add(sq[c - 1])
                sq.append(nx.square(c, t_x1[c], t_mask))
                xg.append(act(H[:, c, :], X[:, c, :], ACT.Copy, t_x1[c], t_m1, scale=pk("nmix")[:, c:c + 1]))
        t_x2 = t_x1
        t_mlp = last

        nx.add(sq[7])
        t_r = nx.end(RS2)
        keep_warm(7)
        t_h = scaled(RS2, None, t_r, xg)
        KH2, VH2 = region(64, 2, 256), region(66, 2, 256)
        t_kh, t_vh = copy(PL, KH2, KH, t_kh, t_mlp), copy(PL, VH2, VH, t_vh, t_mlp)
        KH, VH = KH2, VH2
        stale += [region(120, SLAB).offset, region(128, SLAB).offset]
        fresh = [x for x in hi_free if x[0].offset not in stale]
        hi_free.clear()
        hi_free.extend(fresh + [(region(72, SLAB), [t_mlp]), (region(88, SLAB), [t_mlp])])

        MIX = region(8, 8, 256)
        PF = region(24, 12, 256)
        VAL = region(68, 3, 256)
        GA = region(80, 3, 256)
        RAW = region(83.5, 4, 258)
        P2 = region(96, 2, 512)
        PT2 = region(100, 2, 512)
        QH = region(104, 2, 256)
        O2S = region(133, 2, 256)
        CR = region(135, 256)
        U = region(136, 3, 288)
        CA = region(139.5, 3, 256)
        CM = region(142.5, 256)
        CSQ = region(10, 3, 256)

        KK = region(36, 3, 256)
        RRK = region(39, 3, 256)
        AA = region(42, 3, 256)
        LW = region(45, 3, 256)
        X1 = region(48, 3, 256)
        RHS = [region(51 + 1.5 * d, 384) for d in range(2)]
        KD = [region(54 + 3 * d, 3, 256) for d in range(2)]
        SA = [region(60 + 1.5 * d, 384) for d in range(2)]
        VV = [region(100 + 3 * d, 6, 128) for d in range(2)]
        KR = [region(106 + 12 * d, 6, 2, 128) for d in range(2)]
        BG = [region(112 + 12 * d, 6, 2, 128) for d in range(2)]
        VN = region(130, 2, 384)
        BGN = [region(16 + 3 * d, 2, 384) for d in range(2)]
        ST = [region((22, 42)[d], 3, 128) for d in range(2)]
        G = region(36, 2, 384)
        Y = region(45, 2, 384)
        XX = [region(64 + 18 * d, 6, 2, 128) for d in range(2)]
        LN = [region(70 + 18 * d, 6, 2, 128) for d in range(2)]
        MQ = [region(76 + 18 * d, 6, 2, 128) for d in range(2)]

        zz = [PL.run(lambda e: e.memset(RAW[:, :, 0:1], 0.0), t_mlp),
              PL.run(lambda e: e.memset(RAW[:, :, 257:258], 0.0), t_mlp)]
        smu = pk("smu").rearrange("p (a c) -> p a c", a=2)
        c0 = tiny(12)
        a = tt(PL, c0, smu[:, 0, :], smu[:, 1, :], ADD, t_pack)
        t_c0 = ts(PL, c0, c0, -1.0, 1.0, MUL, ADD, a)
        hw = tiny(12)
        t_hw = [ts(PL, hw[:, 0:6], pk("dw0"), 0.5, 0.0, MUL, ADD, t_pack),
                ts(PL, hw[:, 6:12], pk("ia0"), 0.5, 0.0, MUL, ADD, t_pack)]
        omka = tiny(3)
        t_ka = ts(PL, omka, pk("ka"), -1.0, 1.0, MUL, ADD, t_pack)
        raw_free = [None] * 4
        t_pf = [None] * 12
        t_val = [None] * 3
        t_ga = [None] * 3
        t_q2 = [None] * 2
        win2_last = [None]

        def in_step(s):
            wv, t = slab2("win2", s, 8)
            i, b, rd = bank()
            o = []
            for j in range(2):
                last = mm(b[:, j * 256:(j + 1) * 256],
                          three((both(wv, ALL, k, slice(j * 128, (j + 1) * 128)), (half(HH[:, k, :]), half(H[:, k, :])))
                                for k in range(8)), t, rd, each=t_h)
            done("win2", s, last)
            win2_last[0] = last
            for j in range(2):
                c = 2 * s + j
                bv = b[:, j * 256:(j + 1) * 256]
                if c < 2:
                    t_q2[c] = copy(AC, QH[:, c, :], bv, last)
                    o.append(t_q2[c])
                elif c < 5:
                    t_val[c - 2] = copy(AC, VAL[:, c - 2, :], bv, last, t_mlp)
                    o.append(t_val[c - 2])
                elif c < 8:
                    t_ga[c - 5] = act(GA[:, c - 5, :], bv, ACT.Tanh, last, t_mlp, scale=0.5)
                    o.append(t_ga[c - 5])
                else:
                    c -= 8
                    r = RAW[:, c % 4, :]
                    e = copy(AC, r[:, 1:257], bv, last, raw_free[c % 4])
                    x = act(PF[:, c, :], bv, ACT.Copy, last, t_c0, t_mlp, scale=c0[:, c:c + 1])
                    o += [e, x]
                    x = stt(PF[:, c, :], r[:, 0:256], smu[:, 0, c:c + 1], PF[:, c, :], MUL, ADD, e, x, zz)
                    t_pf[c] = stt(PF[:, c, :], r[:, 2:258], smu[:, 1, c:c + 1], PF[:, c, :], MUL, ADD, x)
                    raw_free[c % 4] = t_pf[c]
            free(i, *o)

        s2 = tiny(32).rearrange("p (a h q) -> p a h q", a=4, h=4)
        t_o2 = []
        pf2, ptf2 = [None, None], [None, None]
        t_mem2 = []

        def mem_head(h):
            c, r0 = h // 2, 64 * (h % 2)
            i, b, rd = bank()
            bv = b[:, :].rearrange("p (q m) -> p q m", q=2)
            for q in range(2):
                t = mm(bv[:, q, :], [(QH[r0:r0 + 64, c, q * 128:(q + 1) * 128], KH[r0:r0 + 64, c, :])],
                       t_q2, t_kh, rd)
            m = s2[:, 0, h, :]
            a = DV.run(lambda e: e.tensor_reduce(m, bv, AX.X, ALU.max), t)
            a = ts(DV, s2[:, 1, h, :], m, -0.125, None, MUL, None, a)
            pv = P2[:, h % 2, :].rearrange("p (q m) -> p q m", q=2)
            x = [act(pv[:, q, :], bv[:, q, :], ACT.Exp, a, pf2[h % 2], scale=0.125, bias=s2[:, 1, h, q:q + 1],
                     accum=s2[:, 2, h, q:q + 1]) for q in range(2)]
            free(i, *x)
            r = DV.run(lambda e: e.reciprocal(s2[:, 3, h, :], s2[:, 2, h, :]), x)
            yield
            i, b, rd = bank()
            for j in range(4):
                t = turn(b[:, j * 128:(j + 1) * 128], P2[:, h % 2, j * 128:(j + 1) * 128], x, rd)
            pf2[h % 2] = t
            e = copy(AC, PT2[:, h % 2, :], b[:, :], t, ptf2[h % 2])
            free(i, e)
            yield
            i, b, rd = bank()
            for q in range(2):
                t = mm(b[:, q * 64:(q + 1) * 64],
                       [(PT2[:, h % 2, (2 * q + m) * 128:(2 * q + m + 1) * 128], VH[:, m, h * 64:(h + 1) * 64])
                        for m in range(2)], e, t_vh, rd)
            t_o2.append(tt(DV, O2S[:, :, h * 64:(h + 1) * 64], b[:, 0:128].rearrange("p (q d) -> p q d", q=2),
                           s2[:, 3, h, :].unsqueeze(2).to_broadcast([128, 2, 64]), MUL, t, r))
            free(i, t_o2[-1])
            ptf2[h % 2] = t
            yield

        def mem_attention():
            for h in (0, 2):
                pair = [mem_head(h), mem_head(h + 1)]
                for stage in range(3):
                    for g in pair:
                        next(g)
                    yield
            keep_warm(2)
            i, b, rd = bank()
            for q in range(2):
                for c in range(2):
                    t = turn(b[:, (c * 2 + q) * 128:(c * 2 + q + 1) * 128], O2S[:, q, c * 128:(c + 1) * 128], t_o2, rd)
            e = copy(AC, MIX[:, 0:2, :], b[:, :].rearrange("p (c t) -> p c t", c=2), t, win2_last[0])
            free(i, e)
            t_mem2.append(e)
            yield

        def tiles(v):
            return v.rearrange("p c (i t) -> p (c i) t", i=2)

        def flat(v):
            return v.rearrange("p a t -> p (a t)")

        t_kk, t_rrk, t_sg, t_wd = [], [], [], []

        def keys():
            a = [ts(DV, KK[:, c, :], PF[:, 3 + c, :], pk("kk")[:, c:c + 1], None, MUL, None, t_pf[3 + c], t_mlp)
                 for c in range(3)]
            s = [act(LW[:, c, :], KK[:, c, :], ACT.Square, a[c]) for c in range(3)]
            yield
            rs = []
            for x, n in ((0, 512), (512, 256)):
                i, b, rd = bank()
                for c in range(0, n, 256):
                    t = mm(b[:, c:c + 256], [(cn("blk"), flat(LW)[:, x + c:x + c + 256])], s, rd)
                v = flat(X1)[:, x:x + n]
                fr = ts(DV, v, b[:, 0:n], 1.0, 1e-12, MUL, ADD, t)
                free(i, fr)
                rs.append(fr)
            r = act(flat(X1), flat(X1), ACT.Sqrt, rs)
            rs = [DV.run(lambda e: e.reciprocal(flat(X1), flat(X1)), r)]
            yield
            t_kk.append(tt(DV, KK, KK, X1, MUL, rs))
            t_wd.append(act(PF[:, 9, :], PF[:, 9, :], ACT.Tanh, t_pf[9]))
            e = act(PF[:, 11, :], PF[:, 11, :], ACT.Tanh, t_pf[11], scale=0.5)
            t_sg.append(ts(PL, PF[:, 11, :], PF[:, 11, :], 0.5, 0.5, MUL, ADD, e))
            yield

        t_vn = []

        def values():
            for m in range(2):
                i, b, rd = bank()
                for c in range(3):
                    t = turn(b[:, c * 128:(c + 1) * 128], PF[:, 6 + c, m * 128:(m + 1) * 128], t_pf[6 + c], rd)
                e = copy(AC, VN[:, m, :], b[:, 0:384], t)
                free(i, e)
                t_vn.append(e)

        es = tiny(6).rearrange("p (d c) -> p d c", d=2)
        ht = tiny(12).rearrange("p (d c i) -> p d c i", d=2, c=3)
        t_es, t_kr, t_bg, t_kd, t_bgn = [None] * 2, [None] * 2, [None] * 2, [None] * 2, [None] * 2
        lw_free, aa_free, x1_free = [None], [t_mask], [None]

        def up(name, src, d, dst, bias, *producers):
            o = []
            for c in range(3):
                i, b, rd = bank()
                t = mm(b[:, 0:256], [(pk(name)[64 * d:64 * d + 64, c * 128:(c + 1) * 128], src[64 * d:64 * d + 64, :])],
                       rd, t_pack2, *producers[:1])
                e = act(dst[:, c, :], b[:, 0:256], ACT.Tanh, t, t_hw, *producers[1:], scale=0.5,
                        bias=bias[:, 3 * d + c:3 * d + c + 1])
                free(i, e)
                o.append(e)
            return o

        def decays(d):
            t = up("dup", PF[:, 9, :], d, LW, hw[:, 0:6], t_wd, lw_free[0], t_kk)
            u = up("iup", PF[:, 10, :], d, AA, hw[:, 6:12], t_pf[10], aa_free[0])
            yield
            t = ts(DV, LW, LW, -0.5 * DECAY, -0.5 * DECAY, MUL, ADD, t)
            u = ts(DV, AA, AA, 0.5, 0.5, MUL, ADD, u)
            sc = [DV.run(lambda e, c=c, m=m: e.tensor_tensor_scan(
                X1[:, c, m * 128:(m + 1) * 128], ones, LW[:, c, m * 128:(m + 1) * 128], 0.0, MUL, ADD),
                t, x1_free[0], t_kk, t_const) for c in range(3) for m in range(2)]
            k0 = [ts(DV, KD[d][:, c, :], AA[:, c, :], pk("ka")[:, c:c + 1], omka[:, c:c + 1], MUL, ADD, u, t_ka)
                  for c in range(3)]
            hd = ht[:, d, :, :].rearrange("p c i -> p (c i)")
            h = ts(DV, hd, tiles(X1)[:, :, 127], 0.5, None, MUL, None, sc)
            t_kd[d] = tt(PL, KD[d], KD[d], PF[:, 3:6, :], MUL, k0, t_pf[3:6])
            yield
            x1 = tt(DV, tiles(X1), tiles(X1), hd.unsqueeze(2).to_broadcast([128, 6, 128]), SUB, h)
            n = stt(AA, AA, -1.0, KK, MUL, MUL, k0, t_kk)
            x2 = tt(DV, LW, X1, LW, SUB, x1)
            a = tt(DV, es[:, d, :], ht[:, d, :, 0], ht[:, d, :, 1], ADD, h)
            x1v, x2v = tiles(X1), tiles(LW)
            if d == 0:
                e2 = act(BG[d][:, :, 1, :], x1v, ACT.Exp, x1, scale=-1.0)
                e1 = act(KR[d][:, :, 1, :], x1v, ACT.Exp, x1)
                e0 = act(KR[d][:, :, 0, :], x2v, ACT.Exp, x2)
            else:
                e0 = act(KR[d][:, :, 0, :], x1v, ACT.Exp, x1, scale=-1.0)
                e1 = act(KR[d][:, :, 1, :], x2v, ACT.Exp, x2, scale=-1.0)
                e2 = act(BG[d][:, :, 1, :], x2v, ACT.Exp, x2)
            lw_free[0], x1_free[0] = [e0, e1, e2], [e0, e1, e2]
            t_es[d] = act(es[:, d, :], es[:, d, :], ACT.Exp, a)
            yield
            a = tt(PL, KR[d][:, :, 0, :], KR[d][:, :, 0, :], tiles(KK), MUL, e0, t_kk)
            b_ = tt(DV, KR[d][:, :, 1, :], KR[d][:, :, 1, :], tiles(PF[:, 0:3, :]), MUL, e1, t_pf[0:3])
            t_kr[d] = [a, b_]
            a = tt(DV, BG[d][:, :, 0, :], tiles(AA), BG[d][:, :, 1, :], MUL, n, e2)
            aa_free[0] = a
            b_ = tt(DV, BG[d][:, :, 1, :], BG[d][:, :, 1, :], tiles(KD[d]), MUL, e2, t_kd[d], a)
            t_bg[d] = [a, b_]
            yield

        def bg_rows(d):
            o = []
            for y in range(2):
                i, b, rd = bank()
                for c in range(3):
                    t = turn(b[:, c * 128:(c + 1) * 128], BG[d][:, 2 * c + d, y, :], t_bg[d], rd)
                e = copy(AC, BGN[d][:, y, :], b[:, 0:384], t, win2_last[0])
                free(i, e)
                o.append(e)
            t_bgn[d] = o

        cw = pk("convw").rearrange("p (c k) -> p c k", c=3)
        t_cv = [None] * 3
        t_u3, t_conv = [], []

        def conv_start():
            z = [PL.run(lambda e: e.memset(U[:, :, 0:15], 0.0), win2_last[0]),
                 PL.run(lambda e: e.memset(U[:, :, 271:288], 0.0), win2_last[0])]
            a = ts(DV, GA, GA, 0.5, 0.5, MUL, ADD, t_ga)
            a = tt(DV, U[:, :, 15:271], VAL, GA, MUL, a, t_val, z)
            t_u3.append(a)
            yield
            for c in range(3):
                t_cv[c] = ts(DV, CA[:, c, :], U[:, c, 0:256], cw[:, c, 0:1], pk("convb")[:, c:c + 1], MUL, ADD, a)
            yield

        def conv_rest():
            for k in range(1, 31):
                for c in range(3):
                    t_cv[c] = stt(CA[:, c, :], U[:, c, k:k + 256], cw[:, c, k:k + 1], CA[:, c, :], MUL, ADD, t_cv[c])
                yield
            i, b, rd = bank()
            t = mm(b[:, 0:256], [(ones, CA[:, c, :]) for c in range(3)], t_cv, rd)
            yield
            a = ts(DV, CM, b[:, 0:256], 1.0 / 384, None, MUL, None, t)
            free(i, a)
            a = tt(DV, CA, CA, CM.unsqueeze(1).to_broadcast([128, 3, 256]), SUB, a)
            s = act(CSQ, CA, ACT.Square, a)
            yield
            i, b, rd = bank()
            t = mm(b[:, 0:256], [(ones, CSQ[:, c, :]) for c in range(3)], s, rd)
            fr, r = rsq(CR, b[:, 0:256], 1.0 / 384, 1e-5, t)
            free(i, fr)
            yield
            a = tt(DV, CA, CA, CR.unsqueeze(1).to_broadcast([128, 3, 256]), MUL, r)
            z = [ts(DV, CA[:, c, :], CA[:, c, :], pk("lng")[:, c:c + 1], pk("lnb")[:, c:c + 1], MUL, ADD, a)
                 for c in range(3)]
            a = act(CSQ, CA, ACT.Tanh, z, scale=0.5)
            a = ts(PL, CSQ, CSQ, 0.5, 0.5, MUL, ADD, a)
            t_conv.append(tt(PL, MIX[:, 2:5, :], CA, CSQ, MUL, a))
            yield

        bon = tiny(12).rearrange("p (m h) -> p m h", m=2)
        t_bon, t_g, t_bp = [], [], []

        def bonus():
            a = tt(PL, KD[0], KD[0], KD[1], ADD, t_kd, t_bg)
            t_rrk.extend(ts(PL, RRK[:, c, :], PF[:, c, :], pk("rk")[:, c:c + 1], 0.0, MUL, ADD, t_pf[c])
                         for c in range(3))
            t_bp.append(tt(PL, KD[0], KD[0], RRK, MUL, a, t_rrk))
            yield
            for m in range(2):
                i, b, rd = bank()
                t = mm(b[:, 0:384], [(PF[:, 11, m * 128:(m + 1) * 128], pk("gup"))], t_sg, rd)
                e = copy(AC, G[:, m, :], b[:, 0:384], t, t_kr, t_bg)
                free(i, e)
                t_g.append(e)
                yield
            i, b, rd = bank()
            for m in range(2):
                for c in range(3):
                    t = mm(b[:, m * 6 + 2 * c:m * 6 + 2 * c + 2], [(KD[0][:, c, m * 128:(m + 1) * 128], cn("ind2"))],
                           t_bp, rd)
            t_bon.append(copy(DV, bon, b[:, 0:12].rearrange("p (m h) -> p m h", m=2), t))
            free(i, t_bon[0])
            yield

        lm = maskt[:, 0:LEVELS * 384].rearrange("p (l m) -> p l m", l=LEVELS)
        si = maskt[:, LEVELS * 384:LEVELS * 384 + 512].rearrange("p (d m) -> p d m", d=2)
        t_zero = [None] * 2
        set_free = [None, None]
        t_st = [None, None]
        y_done = [None, None]

        def zero(d):
            t_zero[d] = [PL.run(lambda e: e.memset(LN[d], 0.0), t_u3, t_mem2, t_pf, win2_last[0]),
                         PL.run(lambda e: e.memset(MQ[d], 0.0))]

        def batch(d, m, second):
            x_, l_, q_ = XX[d], LN[d], MQ[d]
            init = DV.run(lambda e: e.tensor_copy(x_.rearrange("p u a t -> p (u a) t"),
                                                  ident.unsqueeze(1).to_broadcast([128, 12, 128])),
                          set_free[d], t_u3, t_mem2, t_pf, t_const)
            ready = [None] * 6
            for p in range(3):
                j, bq, rdq = bank()
                o = []
                two, us, t2, tq = [bank(), bank()], (2 * p, 2 * p + 1), [None] * 2, None

                def operands(u):
                    r, idx = slice(64 * (u % 2), 64 * (u % 2) + 64), 2 * (u // 2) + m
                    return KR[d][r, idx, :, :], BG[d][r, idx, 0, :], BG[d][r, idx, 1, :]

                for u in us:
                    kr, be, ga = operands(u)
                    mm(two[u % 2][1][:, 0:128], [(kr[:, 0, :], be)], t_kr[d], t_bg[d], two[u % 2][2])
                for u in us:
                    kr, be, ga = operands(u)
                    t2[u % 2] = mm(two[u % 2][1][:, 128:384], [(be, flat(kr))])
                    tq = mm(bq[:, (u % 2) * 256:(u % 2) * 256 + 256], [(ga, flat(kr))], rdq, tq)
                for u in us:
                    (i, b, _), t = two[u % 2], t2[u % 2]
                    a = DV.run(lambda e, u=u, b=b: e.copy_predicated(flat(x_[:, u, :, :]), lm[:, 0, 128 * d:128 * d + 256],
                                                                     b[:, 0:256]), t, init, t_mask)
                    c = DV.run(lambda e, u=u, b=b: e.copy_predicated(flat(l_[:, u, :, :]), si[:, d, :], b[:, 128:384]),
                               t, t_zero[d], set_free[d])
                    free(i, a, c)
                    o += [a, c]
                c = DV.run(lambda e, p=p, bq=bq: e.copy_predicated(
                    q_[:, 2 * p:2 * p + 2, :, :].rearrange("p u a t -> p u (a t)"),
                    si[:, d, :].unsqueeze(1).to_broadcast([128, 2, 256]),
                    bq[:, :].rearrange("p (u t) -> p u t", u=2)), tq, t_zero[d], set_free[d])
                free(j, c)
                ready[2 * p] = ready[2 * p + 1] = [*o, c]
            yield
            vfree = [None] * 3
            for lv in range(1, LEVELS):
                tv = []
                for p in range(3):
                    i, b, rd = bank()
                    for u in (2 * p, 2 * p + 1):
                        t = mm(b[:, (u % 2) * 128:(u % 2) * 128 + 128], [(l_[:, u, 0, :], x_[:, u, 0, :])], ready[u], rd)
                    e = copy(AC, VV[d][:, 2 * p:2 * p + 2, :], b[:, 0:256].rearrange("p (u t) -> p u t", u=2), t,
                             vfree[p], set_free[d])
                    free(i, e)
                    tv.append(e)
                yield
                tz = []
                for p in range(3):
                    i, b, rd = bank()
                    for u in (2 * p, 2 * p + 1):
                        t = mm(b[:, (u % 2) * 128:(u % 2) * 128 + 128], [(VV[d][:, u, :], x_[:, u, 1, :])], tv[p], rd)
                    vfree[p] = t
                    c = DV.run(lambda e, p=p, b=b, lv=lv: e.copy_predicated(
                        x_[:, 2 * p:2 * p + 2, 1, :],
                        lm[:, lv, 128 * (d + 1):128 * (d + 2)].unsqueeze(1).to_broadcast([128, 2, 128]),
                        b[:, 0:256].rearrange("p (u t) -> p u t", u=2)), t)
                    free(i, c)
                    ready[2 * p] = ready[2 * p + 1] = c
                yield
                if lv == LEVELS - 1:
                    break
                for p in range(3):
                    i, b, rd = bank()
                    for u in (2 * p, 2 * p + 1):
                        t = turn(b[:, (u % 2) * 128:(u % 2) * 128 + 128], x_[:, u, 1, :], ready[u], rd)
                    e = copy(AC, x_[:, 2 * p:2 * p + 2, 0, :], b[:, 0:256].rearrange("p (u t) -> p u t", u=2), t)
                    free(i, e)
                    ready[2 * p] = ready[2 * p + 1] = e
                yield

            def st(h):
                return ST[d][64 * (h % 2):64 * (h % 2) + 64, h // 2, :]

            def kr_(h, a):
                return KR[d][64 * (h % 2):64 * (h % 2) + 64, 2 * (h // 2) + m, a, :]

            def pair(v, h):
                return v[:, (h // 2) * 128:(h // 2) * 128 + 128]

            vn = VN[:, m, :]

            def heads(pairs, *producers):
                two, t = [bank(), bank()], [None] * 6
                for h in (0, 2, 4, 1, 3, 5):
                    _, b, rd = two[h // 4]
                    t[h] = mm(b[:, (h % 4) * 128:(h % 4 + 1) * 128], pairs(h), producers, rd,
                              (t[0:4:2], t[4])[h // 4] if second and h % 2 else None)
                got = []
                for (i, b, _), c0_, n in zip(two, (0, 2), (2, 1)):
                    v = b[:, 0:n * 256].rearrange("p (c q j) -> p c q j", c=n, q=4)[:, :, 0:4:3, :]
                    got.append((i, v, t[5] if c0_ else t[3], c0_, n))
                return got

            def parts(v, c0_, n):
                return v[:, c0_ * 128:(c0_ + n) * 128].rearrange("p (c q j) -> p c q j", c=n, q=2)

            def keep(dst, got, *producers):
                o = []
                for i, v, t, c0_, n in got:
                    e = copy(DV, parts(dst, c0_, n), v, t, producers)
                    free(i, e)
                    o.append(e)
                return o

            e = keep(RHS[d], heads(lambda h: [(q_[:, h, 0, :], pair(vn, h))] + ([(kr_(h, 0), st(h))] if second else []),
                                   t_vn, ready, t_st[d] if second else None))
            yield
            e = keep(SA[d], heads(lambda h: [(x_[:, h, 1, :], pair(RHS[d], h))], e))
            yield
            if not second:
                i, b, rd = bank()
                for h in range(6):
                    r0 = 64 * (h % 2)
                    t = mm(b[r0:r0 + 64, (h // 2) * 128:(h // 2) * 128 + 128],
                           [(BGN[d][:, 0, h * 64:(h + 1) * 64], pair(SA[d], h)),
                            (BGN[d][:, 1, h * 64:(h + 1) * 64], pair(vn, h))], e, t_bgn[d], rd)
                t_st[d] = tt(DV, ST[d], b[:, 0:384].rearrange("p (c j) -> p c j", c=3),
                             es[:, d, :].unsqueeze(2).to_broadcast([128, 3, 128]), MUL, t, t_es[d], aa_free[0])
                free(i, t_st[d])
            got = heads(lambda h: [(l_[:, h, 1, :], pair(SA[d], h)), (q_[:, h, 1, :], pair(vn, h))]
                        + ([(kr_(h, 1), st(h))] if second else []), e)
            set_free[d] = got[-1][2]
            if second:
                o = []
                for i, v, t, c0_, n in got:
                    o.append(tt(DV, parts(Y[:, m, :], c0_, n), v, parts(Y[:, m, :], c0_, n), ADD, t, y_done[m]))
                    free(i, o[-1])
                y_done[m] = o
            else:
                y_done[m] = keep(Y[:, m, :], got, t_mem2)
            yield

        gst = tiny(24).rearrange("p (m a h) -> p m a h", m=2, a=2)
        t_mix = [None, None]

        def group_norm(m):
            y = Y[:, m, :]
            tmp = region(39 + 1.5 * m, 384)
            yv = y.rearrange("p (h d) -> p h d", h=6)
            tv = tmp.rearrange("p (h d) -> p h d", h=6)
            mu, rs = gst[:, m, 0, :], gst[:, m, 1, :]

            def wide(v):
                return v.unsqueeze(2).to_broadcast([128, 6, 64])

            a = DV.run(lambda e: e.tensor_reduce(mu, yv, AX.X, ADD), y_done[m])
            a = ts(DV, mu, mu, 1.0 / 64, None, MUL, None, a)
            a = tt(DV, yv, yv, wide(mu), SUB, a)
            s = act(tmp, y, ACT.Square, a, t_bp)
            yield
            s = DV.run(lambda e: e.tensor_reduce(rs, tv, AX.X, ADD), s)
            _, r = rsq(rs, rs, 1.0 / 64, 64e-5, s)
            vn = VN[:, m, :]
            vb = tt(PL, vn.rearrange("p (h d) -> p h d", h=6), vn.rearrange("p (h d) -> p h d", h=6), wide(bon[:, m, :]),
                    MUL, t_bon, t_vn, set_free)
            vb = tt(PL, vn, vn, pk("lnxb"), ADD, vb)
            vb = tt(PL, vn, vn, G[:, m, :], MUL, vb, t_g)
            gg = tt(PL, G[:, m, :], G[:, m, :], pk("lnxg"), MUL, vb)
            yield
            a = tt(DV, yv, yv, wide(rs), MUL, r)
            a = tt(DV, y, y, G[:, m, :], MUL, a, gg)
            a = tt(DV, y, y, vn, ADD, a, vb)
            yield
            i, b, rd = bank()
            for c in range(3):
                t = turn(b[:, c * 128:(c + 1) * 128], y[:, c * 128:(c + 1) * 128], a, rd)
            e = copy(AC, MIX[:, 5:8, m * 128:(m + 1) * 128], b[:, 0:384].rearrange("p (c t) -> p c t", c=3), t)
            free(i, e)
            t_mix[m] = e
            yield

        t_xa = [None] * 8
        t_x3 = [[None] * 8, [None] * 8]

        def wo2(k, c):
            place, t = slab("wo2", k // 2, 2)
            return place[:, k % 2, c * 128:(c + 1) * 128]

        def out_first():
            for c in range(8):
                i, b, rd = bank()
                t = mm(b[:, 0:256], [(wo2(k, c), MIX[:, k, :]) for k in range(5)],
                       [slab("wo2", n, 2)[1] for n in range(3)], rd, t_mem2, t_conv)
                t_xa[c] = tt(DV, X[:, c, :], b[:, 0:256], X[:, c, :], ADD, t)
                free(i, t_xa[c])
                yield
            done("wo2", 0, t)
            done("wo2", 1, t)

        def out_rest(m):
            at = slice(m * 128, (m + 1) * 128)
            for s in range(4):
                i, b, rd = bank()
                for j in range(2):
                    t = mm(b[:, j * 128:(j + 1) * 128], [(wo2(k, 2 * s + j), MIX[:, k, at]) for k in range(5, 8)],
                           t_mix[m], slab("wo2", 3, 2)[1], rd)
                xs = X[:, 2 * s:2 * s + 2, at]
                e = tt(DV, xs, b[:, 0:256].rearrange("p (j t) -> p j t", j=2), xs, ADD, t, t_xa[2 * s:2 * s + 2])
                free(i, e)
                t_x3[m][2 * s] = t_x3[m][2 * s + 1] = e
                yield
            if m == 0:
                done("wo2", 2, t)
                done("wo2", 3, t)
                add_slot(region(8, SLAB), t)
                refill()

        XNH = region(64, 2, 1024)
        XNL = region(72, 2, 1024)
        SCR = region(133, 512)
        wr = pk("wr").rearrange("p (k e) -> p k e", k=8)
        aff = tiny(32).rearrange("p (m e) -> p m e", m=2)
        rst = tiny(12).rearrange("p (a m) -> p a m", a=6)
        raw_read = [None] * 2
        t_aff, t_xn, scr_last = [None] * 2, [], [None]

        def route(m):
            at = slice(m * 128, (m + 1) * 128)
            got = [bank() for _ in range(2)]
            i2, raw, rd2 = bank()
            for k in range(8):
                _, b, rd = got[k // 4]
                t = turn(b[:, (k % 4) * 128:(k % 4 + 1) * 128], X[:, k, at], t_x3[m][k], rd)
            t2 = mm(raw[:, 0:16], [(X[:, k, at], wr[:, k, :]) for k in range(8)], t_wr, rd2)
            raw_read[m] = t2
            v = lambda n: rst[:, n, m:m + 1]
            s = []
            for h in range(2):
                s.append(act(SCR, got[h][1][:, :], ACT.Square, t, t_mem2, scr_last, accum=v(h)))
                scr_last[0] = s[-1]
            a = tt(DV, v(0), v(0), v(1), ADD, s)
            _, r = rsq(v(0), v(0), 1.0 / 1024, 1e-6, a)
            x = DV.run(lambda e: e.tensor_reduce(v(2), raw[:, 0:16], AX.X, ALU.max, negate=True), t2)
            x = tt(DV, v(2), v(2), v(0), MUL, x, r)
            yield
            x = act(aff[:, m, :], raw[:, 0:16], ACT.Exp, x, scale=v(0), bias=v(2), accum=v(3))
            free(i2, x)
            x = DV.run(lambda e: e.reciprocal(v(4), v(3)), x)
            t_aff[m] = ts(DV, aff[:, m, :], aff[:, m, :], v(4), None, MUL, None, x)
            yield
            for h in range(2):
                i, b, _ = got[h]
                f = slice(h * 512, (h + 1) * 512)
                e = act(half(XNH[:, m, f]), b[:, :], ACT.Copy, r, set_free[0], scale=v(0))
                l = stt(half(XNL[:, m, f]), b[:, :], v(0), half(XNH[:, m, f]).bitcast(F32), MUL, SUB, e)
                free(i, l)
                t_xn.append(l)
            if m:
                act(rst[:, 5, m:m + 1], v(0), ACT.Sqrt, r)
            yield

        def release(d, *kb):
            for x in kb:
                add_slot(region(x, SLAB), set_free[d], set_free[0] if x == 98 else None)
            if d:
                blk = CO["blk"][0]
                add_slot(constt[:, blk:blk + SLAB], set_free)
                assert t_bon
                add_slot(region(56, SLAB), set_free, t_bon, t_kr, t_bg)
            refill()
            return
            yield

        def spare():
            add_slot(region(24, SLAB), t_bp, t_rrk, t_g, t_kd, t_kr, t_vn)
            refill()
            return
            yield

        def conv_slot():
            add_slot(region(136, SLAB), t_conv)
            refill()
            return
            yield

        def pack_slot():
            add_slot(packt[:, n0:PN], raw_read)
            refill()
            return
            yield

        def after(*gens):
            for g in gens:
                yield from g

        def steps(g, n):
            for _ in range(n):
                next(g)

        def rest(n):
            for _ in range(n):
                yield

        def together(*gens):
            live = list(gens)
            while live:
                for g in list(live):
                    try:
                        next(g)
                    except StopIteration:
                        live.remove(g)

        kk_, d0, d1, mem, cv = keys(), decays(0), decays(1), mem_attention(), conv_start()
        in_step(5)
        in_step(6)
        steps(kk_, 1)
        AC.load(packt[:, n0:PN], pack[:, n0:PN], *t_pack2, t_kh, t_vh)
        in_step(8)
        steps(kk_, 1)
        in_step(9)
        steps(kk_, 1)
        in_step(0)
        steps(d0, 1)
        steps(mem, 1)
        in_step(4)
        steps(d0, 1)
        steps(mem, 1)
        in_step(7)
        steps(mem, 1)
        steps(d0, 2)
        steps(d1, 1)
        in_step(1)
        steps(d1, 1)
        values()
        steps(mem, 1)
        in_step(2)
        steps(d1, 1)
        steps(mem, 1)
        in_step(3)
        steps(cv, 1)
        steps(mem, 2)
        zero(0)
        steps(d1, 1)

        def prepare():
            zero(1)
            steps(cv, 1)
            bg_rows(0)
            yield
            bg_rows(1)
            yield

        t_wr = tt(PL, wr, wr, pk("nffn").unsqueeze(2).to_broadcast([128, 8, 16]), MUL, t_pack2)
        together(after(batch(0, 0, False), batch(0, 1, True), release(0, 16, 106), group_norm(1), out_rest(1), route(1)),
                 after(rest(1), prepare(), batch(1, 1, False), batch(1, 0, True), release(1, 114, 122, 82, 90, 98), group_norm(0), out_rest(0), route(0), pack_slot()),
                 after(rest(4), conv_rest(), conv_slot(), rest(3), out_first()), after(rest(8), bonus(), spare()))

        XE = region(32, 8, 512)
        OH = region(48, 2, 512)
        GG = region(52, 2, 512)
        GT = region(48, 4, 256)
        W0, W1, W2 = region(52, 256), region(53, 256), region(54, 256)
        RS4 = region(135, 256)
        W3 = region(55, 256)
        t_w3 = PL.run(lambda e: e.memset(W3, 1.0), t_mix)
        i, b, rd = bank()
        for m in range(2):
            t = mm(b[0:16, m * 128:(m + 1) * 128], [(aff[:, m, :], ident)], t_aff, rd)
        keep_warm(10)
        a = copy(DV, W0[0:16, :], b[0:16, 0:256], t)
        free(i, a)
        m8 = tiny(32).rearrange("p (r v) -> p r v", r=4)
        src = W0
        for r in range(4):
            dst = (W1, W2)[r % 2]
            a = DV.run(lambda e, r=r, src=src: e.max(m8[0:16, r, :], src[0:16, :]), a)
            a = DV.run(lambda e, r=r, src=src, dst=dst: e.match_replace(dst[0:16, :], m8[0:16, r, :], src[0:16, :], -1.0), a)
            src = dst
        a = ts(DV, W1[0:16, :], W2[0:16, :], 0.0, None, ALU.is_lt, None, a)
        a = DV.run(lambda e: e.tensor_tensor_scan(W0[0:16, :], W3[0:16, :], W1[0:16, :], 0.0, MUL, ADD), a, t_w3)
        a = tt(DV, W0[0:16, :], W0[0:16, :], W1[0:16, :], MUL, a)
        i, b, rd = bank()
        for m in range(2):
            t = mm(b[:, m * 16:(m + 1) * 16], [(W0[0:16, m * 128:(m + 1) * 128], ident[0:16, 0:16])], a, rd)
        pos = tiny(32).rearrange("p (m e) -> p m e", m=2)
        a = copy(DV, pos, b[:, 0:32].rearrange("p (m e) -> p m e", m=2), t)
        free(i, a)
        t_oh, t_gg = [], []
        for m in range(2):
            t_oh.append(tt(DV, half(OH[:, m, :]).rearrange("p (e s) -> p e s", e=16),
                           pos[:, m, :].unsqueeze(2).to_broadcast([128, 16, 32]),
                           cn("iota").unsqueeze(1).to_broadcast([128, 16, 32]), ALU.is_equal, a, t_const))
        for m in range(2):
            t_gg.append(tt(PL, GG[:, m, :].rearrange("p (e s) -> p e s", e=16),
                           half(OH[:, m, :]).bitcast(F32).rearrange("p (e s) -> p e s", e=16),
                           aff[:, m, :].unsqueeze(2).to_broadcast([128, 16, 32]), MUL, t_oh[m], t_aff))
        t_xe = [None] * 2

        def gather(g):
            o = []
            at = slice(g * 256, (g + 1) * 256)
            for h in range(4):
                i, b, rd = bank()
                for j in range(2):
                    f = slice((2 * h + j) * 128, (2 * h + j + 1) * 128)
                    t = mm(b[:, j * 256:(j + 1) * 256],
                           [(half(v[:, m, f]), half(OH[:, m, at])) for m in range(2) for v in (XNH, XNL)],
                           t_oh, t_xn, rd)
                o.append(tt(DV, XE[:, 2 * h:2 * h + 2, at], b[:, :].rearrange("p (j s) -> p j s", j=2),
                            pk("nffn")[:, 2 * h:2 * h + 2].unsqueeze(2).to_broadcast([128, 2, 256]), MUL, t))
                free(i, o[-1])
            t_xe[g] = o

        HID = region(64, 8, 4, 64)
        TMP = region(80, 2, 4, 64)
        GU = region(130, 2, 512)
        YE = region(72, 2, 1024)
        t_gt = []
        hid, hid_free, gu_free = {}, {}, {}
        ye_free = [None, None]

        def gate_up(e):
            i, b, rd = bank()
            for k in range(8):
                wv, t = slab("gu", 8 * e + k, 4)
                last = quarters(b, [XE[:, k, e * 32:(e + 1) * 32]] * 4, wv, k, t, t_xe[e // 8][k // 2], rd)
                done("gu", 8 * e + k, last)
            return i, b, last

        def hidden(e, i, b, last):
            gu, tm = GU[:, e % 2, :], TMP[:, e % 2, :, :]
            x = copy(AC, gu, b[:, :], last, gu_free.get(e - 2))
            free(i, x)
            i, b, rd = bank()
            for c in range(4):
                t = turn(b[:, c * 128:(c + 1) * 128], gu[:, c * 128:(c + 1) * 128], x, rd)
            gu_free[e] = t
            bv = b[:, :].rearrange("p (c n) -> p c n", c=4)
            a = act(tm, bv[:, :, 0:64], ACT.Tanh, t, hid.get(e - 2), scale=0.5)
            a = ts(DV, tm, tm, 0.5, 0.5, MUL, ADD, a)
            a = tt(DV, tm, bv[:, :, 0:64], tm, MUL, a)
            hid[e] = tt(DV, HID[:, e % 8, :, :], bv[:, :, 64:128], tm, MUL, a, hid_free.get(e - 8))
            free(i, hid[e])

        t_x4 = t_x3[0]

        def down(g, fh, between=()):
            es_ = range(4 * g, 4 * g + 4)
            i, b, rd = bank()
            for k in range(8):
                if k == 4:
                    for f in between:
                        f()
                wv, t = slab("ed", 16 * g + 8 * fh + k, 4)
                last = quarters(b, [HID[:, e % 8, k % 4, 32 * (k // 4):32 * (k // 4) + 32] for e in es_], wv, k,
                                t, [hid[e] for e in es_], rd)
                done("ed", 16 * g + 8 * fh + k, last)
            x = copy(AC, YE[:, g % 2, fh * 512:(fh + 1) * 512], b[:, :], last, ye_free[g % 2])
            free(i, x)
            if fh:
                for e in es_:
                    hid_free[e] = last
            return x

        def combine(g, fh, ev):
            for c2_ in (2 * fh, 2 * fh + 1):
                i, b, rd = bank()
                for j in range(2):
                    c = 2 * c2_ + j
                    t = mm(b[:, j * 256:(j + 1) * 256], [(YE[:, g % 2, c * 128:(c + 1) * 128], GT[:, g, :])],
                           ev, t_gt, rd)
                xs = X[:, 2 * c2_:2 * c2_ + 2, :]
                e = tt(DV, xs, b[:, :].rearrange("p (j t) -> p j t", j=2), xs, ADD, t, t_x3)
                free(i, e)
                t_x4[2 * c2_] = t_x4[2 * c2_ + 1] = e
            if fh:
                ye_free[g % 2] = t

        prev = None
        gather(0)
        for e in range(17):
            if e < 16:
                now = gate_up(e)
            if e == 0:
                gather(1)
            if prev:
                hidden(e - 1, *prev)
            prev = now
            if e == 0:
                for g2 in range(2):
                    i, b, rd = bank()
                    for j in range(2):
                        for m in range(2):
                            g = 2 * g2 + j
                            t = turn(b[:, (2 * j + m) * 128:(2 * j + m + 1) * 128], GG[:, m, g * 128:(g + 1) * 128],
                                     t_gg, rd)
                    x = copy(AC, GT[:, 2 * g2:2 * g2 + 2, :], b[:, :].rearrange("p (j t) -> p j t", j=2), t)
                    free(i, x)
                    t_gt.append(x)
            if e and e % 4 == 0:
                if e == 16:
                    nx, sq, xg = Norm(X, region(32, 8, 256)), [], []
                    OUT = region(40, 8, 256)
                for fh in range(2):
                    ev = down(e // 4 - 1, fh, [lambda t=t: nx.add(t) for t in sq] if e == 16 else ())
                    combine(e // 4 - 1, fh, ev)
                    if e == 16:
                        c = 4 * fh
                        sq = [nx.square(k, t_x4[k]) for k in range(c, c + 4)]
                        xg += [ts(DV, OUT[:, k, :], X[:, k, :], pk("fing")[:, k:k + 1], None, MUL, None, t_x4[k])
                               for k in range(c, c + 4)]
                        if not fh:
                            act(rst[:, 5, :], rst[:, 0, :], ACT.Sqrt)

        for t in sq:
            nx.add(t)
        t_r = nx.end(RS4)
        s_out = sem("s_out")
        for q, eng, k0, k1 in ((SP, DV, 0, 3), (AC, PL, 6, 8), (SP, DV, 3, 6)):
            v = OUT[:, k0:k1, :]
            o = tt(eng, v, v, RS4.unsqueeze(1).to_broadcast([128, k1 - k0, 256]), MUL, t_r, xg)
            q.load(out[:, k0:k1, :], v, s_out, 16, o)
        SP.wait([(s_out, 48)])
        assert not pending and not landed

        block = ctx.enter_context(nc.Block())

        @block.tensor
        def _(e):
            for f in PE.queue:
                f(e)

        @block.scalar
        def _(e):
            for f in AC.queue:
                f(e)

        @block.vector
        def _(e):
            for f in DV.queue:
                f(e)

        @block.gpsimd
        def _(e):
            for f in PL.queue:
                f(e)

        @block.sync
        def _(e):
            for f in SP.queue:
                f(e)


def shape_constants():
    t, p = np.arange(256), np.arange(128)
    o = {"ident": np.eye(128), "ones": np.ones((128, 128)), "blk": (p[:, None] // 64 == p[None] // 64)}
    th = 2 * np.pi * ((p[:, None] * p[None]) % 128) / 128
    o["dftc"] = np.concatenate([np.cos(th), np.sin(th)], 1)
    ph = 2 * np.pi * ((t[:, None] * t[None]) % 256) / 256
    n = np.stack([np.cos(ph), -np.sin(ph)]) / np.sqrt(256.0 * 128.0)
    o["dftn"] = n.reshape(2, 2, 128, 256).transpose(2, 0, 1, 3)
    d = np.arange(64)
    inv = 10000.0 ** (-(2.0 * (d % 16)) / 32.0)
    at = np.where(d[None] < 32, (t // 64)[:, None], (t % 64)[:, None])
    ang = at.astype(np.float32) * inv.astype(np.float32)[None]
    sg = np.where(d % 32 < 16, -1.0, 1.0)
    o["cos"] = np.cos(ang).reshape(2, 128, 64).transpose(1, 0, 2)
    o["sin"] = (np.sin(ang) * sg).reshape(2, 128, 64).transpose(1, 0, 2)
    c = p % 64
    start = np.clip(c - 8, 0, 48)
    kc = np.arange(64)
    o["amask"] = np.where((kc[None] >= start[:, None]) & (kc[None] < start[:, None] + 16), 0.0, -1e30)
    o["iota"] = np.tile(np.arange(1, 33), (128, 1))
    o["ind2"] = p[:, None] // 64 == np.arange(2)[None]
    const = np.concatenate([np.asarray(o[name], np.float32).reshape(128, n) for name, n in CONST], 1)
    m = []
    for lv in range(LEVELS):
        b = 1 << lv
        low = (p[:, None] // (2 * b) == p[None] // (2 * b)) & (p[:, None] % (2 * b) >= b) & (p[None] % (2 * b) < b)
        m += [low, low.T, low]
    up = [p[:, None] < p[None], p[:, None] <= p[None]]
    masks = np.concatenate(m + up + [p[:, None] > p[None], p[:, None] >= p[None]], 1).astype(np.float32)
    return np.ascontiguousarray(const), np.ascontiguousarray(masks)


def kernel(**inputs):
    import concourse.bacc as _bacc
    from concourse.bass_utils import run_bass_kernel_spmd as _run

    a = {n: np.asarray(v) for n, v in inputs.items()}

    def cols(v):
        v = np.asarray(v).reshape(-1)
        return v.reshape(-1, 128).T

    def rowsof(v):
        return np.broadcast_to(np.asarray(v).reshape(1, -1), (128, v.size))

    def tokens(v):
        return np.ascontiguousarray(v.reshape(256, 8, 128).transpose(2, 1, 0))

    def slabs(v, n):
        k = v.shape[0] // 128
        return v.reshape(k, 128, v.shape[1] // n, n).transpose(2, 1, 0, 3).reshape(-1, 128, SLAB)

    pk = {
        "c2": np.stack([cols(a["c"]), cols(a["c_ctx"])], 2).reshape(128, 16),
        "bada": cols(a["b_ada"]), "n1": cols(a["norm1_g"]), "n2": cols(a["norm2_g"]),
        "qg": rowsof(a["q_norm_g"]), "kg": rowsof(a["k_norm_g"]),
        "nmix": cols(a["norm_mix_g_2"]), "nmem": cols(a["norm_mem_g_2"]),
        "convw": a["conv_w_2"][0].reshape(31, 3, 128).transpose(2, 1, 0).reshape(128, 93),
        "convb": cols(a["conv_b_2"]), "lng": cols(a["conv_ln_g_2"]), "lnb": cols(a["conv_ln_b_2"]),
        "smu": cols(a["shift_mu_2"]), "dw0": cols(a["decay_w0_2"]), "ia0": cols(a["iclr_a0_2"]),
        "kk": cols(a["k_k_2"]), "ka": cols(a["k_a_2"]), "rk": cols(a["r_k_2"]),
        "nffn": cols(a["norm_ffn_g_2"]), "fing": cols(a["final_norm_g_2"]),
        "lnxg": rowsof(a["lnx_g_2"]), "lnxb": rowsof(a["lnx_b_2"]),
        "wr": a["w_router_2"][0].reshape(8, 128, 16).transpose(1, 0, 2).reshape(128, 128),
        "dup": a["decay_up_2"].reshape(128, 384), "iup": a["iclr_up_2"].reshape(128, 384),
        "gup": a["gate_up_2"].reshape(128, 384),
    }
    pack = np.ascontiguousarray(np.concatenate([pk[n].reshape(128, c) for n, c in PACK], 1))
    r, c = np.arange(4), np.arange(64)
    dr = r[None, :] - r[:, None] + 7
    dc = np.clip(c[None, :] - c[:, None] + 15, 0, 30)
    bias = a["rpb"][0][:, dr[:, None, :, None], dc[None, :, None, :]].reshape(8, 2, 128, 256)
    bias = np.ascontiguousarray(bias.transpose(2, 0, 1, 3).reshape(128, 4096))
    const, masks = shape_constants()
    m2 = a["w_mlp2"][0].reshape(2, 16, 128, 8, 128).transpose(3, 0, 2, 1, 4).reshape(16, 128, SLAB)
    ws = {
        "win": slabs(a["w_in"][0], 256), "gate": slabs(a["w_branch_gate"][0], 256),
        "fo": slabs(a["w_fourier_out"][0], 512), "ao": slabs(a["w_attn_out"][0], 512), "wo": slabs(a["w_out"][0], 256),
        "m1": slabs(a["w_mlp1"][0], 256), "m2": m2, "win2": slabs(a["w_in_2"][0], 256),
        "mk": slabs(a["w_mk_2"][0], 256), "mv": slabs(a["w_mv_2"][0], 256), "wo2": a["w_out_2"][0].reshape(4, 2, 128, 1024).transpose(0, 2, 1, 3).reshape(4, 128, SLAB),
    }
    ws["ada"] = a["w_ada"][0].reshape(8, 128, 3, SLAB).transpose(2, 0, 1, 3).reshape(24, 128, SLAB)
    ws["gu"] = np.concatenate([a["w_e_gate_2"][0], a["w_e_up_2"][0]], 2).reshape(128, 128, SLAB)
    ws["ed"] = a["w_e_down_2"][0].reshape(4, 4, 8, 128, 2, 512).transpose(0, 4, 2, 3, 1, 5).reshape(64, 128, SLAB)

    arrays = {
        "xT": tokens(a["x"]), "cT": tokens(a["ctx"]), "memT": tokens(a["mem_2"]), "pack": pack, "bias": bias,
        "const": const, "masks": masks,
    }
    for n, v in ws.items():
        arrays["w_" + n] = np.ascontiguousarray(v)
    nc = _bacc.Bacc("TRN2", target_bir_lowering=False, num_devices=1)
    t = {n: nc.dram_tensor(n, v.shape, mybir.dt.from_np(v.dtype), kind="ExternalInput").ap() for n, v in arrays.items()}
    out = nc.dram_tensor("out", (128, 8, 256), F32, kind="ExternalOutput").ap()
    build(nc, t["xT"], t["cT"], t["memT"], t["pack"], t["bias"], t["const"], t["masks"],
          {n: t["w_" + n] for n in ws}, out)
    got = _run(nc, [arrays], core_ids=[0]).results[0]["out"]
    return np.ascontiguousarray(got.transpose(2, 1, 0)).reshape(1, 256, 1024)
```
